# Optimizing a Trainium2 kernel written in Bass

```python
import math
import jax, jax.numpy as jnp
from jax import lax
import numpy as np

D_MODEL = 1024
BATCH = 1
SEQ = 256
DEPTH = 2

N_EVEN = (DEPTH + 1) // 2
N_ODD = DEPTH // 2
DN_ALPHA = (2.0 * DEPTH) ** 0.25
DN_BETA = (8.0 * DEPTH) ** -0.25
LN_EPS = 1e-5
NEG = -1e30
Q_BLOCK = 128

GM_WIDTH = D_MODEL // 2
GM_GROUPS = 4
GM_GROUP_DIM = GM_WIDTH // GM_GROUPS
GM_CHUNK = 128

MLA_HEADS = 8
MLA_NOPE = 64
MLA_ROPE = 32
MLA_V = 64
MLA_Q_RANK = D_MODEL // 4
MLA_KV_RANK = D_MODEL // 8
ROPE_BASE = 10000.0
AB_IN = 2 * GM_WIDTH + MLA_Q_RANK + MLA_KV_RANK + MLA_ROPE
AB_MIX = GM_WIDTH + MLA_HEADS * MLA_V
AB_SPLITS = (GM_WIDTH, 2 * GM_WIDTH, 2 * GM_WIDTH + MLA_Q_RANK,
             2 * GM_WIDTH + MLA_Q_RANK + MLA_KV_RANK)

NSA_HEADS = 16
NSA_GROUPS = 2
NSA_HPG = NSA_HEADS // NSA_GROUPS
NSA_DH = 64
NSA_CMP_LEN = 32
NSA_CMP_STRIDE = 16
NSA_CMP_HIDDEN = 256
NSA_SEL_LEN = 64
NSA_TOPK = 8
NSA_SEL_QBLOCK = 64
NSA_WINDOW = 512
NSA_BRANCHES = 3
NSA_KV = NSA_GROUPS * NSA_DH
C_MIX = NSA_HEADS * NSA_DH
C_IN = C_MIX + 6 * NSA_KV + NSA_BRANCHES * NSA_HEADS
NSA_SPLITS = tuple(C_MIX + i * NSA_KV for i in range(7))
NSA_FORCE = 1e4

MOE_GROUPS = 4
MOE_EPG = 8
MOE_EXPERTS = MOE_GROUPS * MOE_EPG
MOE_TOPK = 2
MOE_HIDDEN = D_MODEL // 4


def layer_norm(x, g, b):
    xf = x.astype(jnp.float32)
    mu = xf.mean(-1, keepdims=True)
    var = jnp.square(xf - mu).mean(-1, keepdims=True)
    return ((xf - mu) * lax.rsqrt(var + LN_EPS) * g + b).astype(x.dtype)

def rms_norm(x, g):
    xf = x.astype(jnp.float32)
    return (xf * lax.rsqrt(jnp.mean(xf * xf, -1, keepdims=True) + LN_EPS) * g).astype(x.dtype)

def rope(x, pos):
    half = x.shape[-1] // 2
    freq = jnp.exp(-math.log(ROPE_BASE) * jnp.arange(half, dtype=jnp.float32) / half)
    ang = pos.astype(jnp.float32)[:, :, None, None] * freq
    cos, sin = jnp.cos(ang), jnp.sin(ang)
    x1 = x[..., :half].astype(jnp.float32)
    x2 = x[..., half:].astype(jnp.float32)
    return jnp.concatenate([x1 * cos - x2 * sin, x1 * sin + x2 * cos], -1).astype(x.dtype)

def gmlp_mix(u, v, ln_g, ln_b, w_s, b_s):
    B, S, _ = u.shape
    nc = S // GM_CHUNK
    vn = layer_norm(v, ln_g, ln_b).reshape(B, nc, GM_CHUNK, GM_GROUPS, GM_GROUP_DIM)
    causal = jnp.tril(jnp.ones((GM_CHUNK, GM_CHUNK), dtype=bool))
    ws = jnp.where(causal, w_s, 0.0).astype(vn.dtype)
    s = jnp.einsum('gts,bnsgc->bntgc', ws, vn) + jnp.transpose(b_s)[:, :, None]
    return u * s.reshape(B, S, GM_WIDTH)

def mla_mix(c_q, c_kv, k_r, pos, q_norm_g, kv_norm_g, w_uq, w_uk, w_uv):
    B, S, _ = c_q.shape
    q = (rms_norm(c_q, q_norm_g) @ w_uq).reshape(B, S, MLA_HEADS, MLA_NOPE + MLA_ROPE)
    q_nope = q[..., :MLA_NOPE]
    q_rope = rope(q[..., MLA_NOPE:], pos)
    ckv = rms_norm(c_kv, kv_norm_g)
    k_nope = (ckv @ w_uk).reshape(B, S, MLA_HEADS, MLA_NOPE)
    v = (ckv @ w_uv).reshape(B, S, MLA_HEADS, MLA_V)
    k_rope = rope(k_r[:, :, None, :], pos)[:, :, 0]
    scale = (MLA_NOPE + MLA_ROPE) ** -0.5
    outs = []
    for i in range(S // Q_BLOCK):
        q0, q1 = i * Q_BLOCK, (i + 1) * Q_BLOCK
        s = (jnp.einsum('bqhd,bkhd->bhqk', q_nope[:, q0:q1], k_nope[:, :q1])
             + jnp.einsum('bqhr,bkr->bhqk', q_rope[:, q0:q1], k_rope[:, :q1]))
        mask = (q0 + jnp.arange(Q_BLOCK))[:, None] >= jnp.arange(q1)[None, :]
        s = jnp.where(mask, s.astype(jnp.float32) * scale, NEG)
        p = jax.nn.softmax(s, axis=-1).astype(v.dtype)
        outs.append(jnp.einsum('bhqk,bkhd->bqhd', p, v[:, :q1]))
    return jnp.concatenate(outs, axis=1).reshape(B, S, MLA_HEADS * MLA_V)

def ab_mixer(x, pos, w_in, gm_ln_g, gm_ln_b, gm_ws, gm_bs, q_norm_g, kv_norm_g,
             w_uq, w_uk, w_uv, w_o):
    h = x @ w_in
    u, v, c_q, c_kv, k_r = jnp.split(h, AB_SPLITS, axis=-1)
    y_a = gmlp_mix(jax.nn.gelu(u), jax.nn.gelu(v), gm_ln_g, gm_ln_b, gm_ws, gm_bs)
    y_b = mla_mix(c_q, c_kv, k_r, pos, q_norm_g, kv_norm_g, w_uq, w_uk, w_uv)
    return jnp.concatenate([y_a, y_b], axis=-1) @ w_o

def compress_kv(k, pos_emb, w1, w2):
    B, S, G, D = k.shape
    r = NSA_CMP_LEN // NSA_CMP_STRIDE
    sub = k.reshape(B, S // NSA_CMP_STRIDE, NSA_CMP_STRIDE, G, D)
    nc = S // NSA_CMP_STRIDE - r + 1
    blocks = jnp.concatenate([sub[:, j:j + nc] for j in range(r)], axis=2) + pos_emb[:, None, :]
    flat = blocks.transpose(0, 1, 3, 2, 4).reshape(B, nc, G, NSA_CMP_LEN * D)
    return jax.nn.gelu(flat @ w1) @ w2

def nsa_compressed(q, k_cmp, v_cmp):
    S, nc = q.shape[1], k_cmp.shape[1]
    s = jnp.einsum('btgid,bngd->bgitn', q, k_cmp).astype(jnp.float32) * NSA_DH ** -0.5
    end = jnp.arange(nc) * NSA_CMP_STRIDE + NSA_CMP_LEN - 1
    mask = jnp.arange(S)[:, None] >= end[None, :]
    p = jnp.where(mask, jax.nn.softmax(jnp.where(mask, s, NEG), axis=-1), 0.0)
    o = jnp.einsum('bgitn,bngd->btgid', p.astype(v_cmp.dtype), v_cmp)
    return o, p

def nsa_select_blocks(p_cmp):
    S, nc = p_cmp.shape[3], p_cmp.shape[4]
    nsel = S // NSA_SEL_LEN
    c0 = jnp.arange(nc) * NSA_CMP_STRIDE
    s0 = jnp.arange(nsel) * NSA_SEL_LEN
    cover = ((c0[:, None] < s0[None, :] + NSA_SEL_LEN)
             & (c0[:, None] + NSA_CMP_LEN > s0[None, :])).astype(jnp.float32)
    imp = jnp.einsum('bgitn,nj->bgtj', p_cmp, cover)
    jj = jnp.arange(nsel)[None, :]
    tb = (jnp.arange(S) // NSA_SEL_LEN)[:, None]
    forced = (jj == 0) | (jj == tb) | (jj == tb - 1)
    score = jnp.where(forced, NSA_FORCE, jnp.where(jj <= tb, imp, -NSA_FORCE))
    _, idx = lax.top_k(score, min(NSA_TOPK, nsel))
    return idx

def nsa_selected(q, k_s, v_s, sel_idx):
    B, S, G, HPG, D = q.shape
    K = sel_idx.shape[-1]
    nsel = S // NSA_SEL_LEN
    kb = k_s.reshape(B, nsel, NSA_SEL_LEN, G, D).transpose(0, 3, 1, 2, 4)
    vb = v_s.reshape(B, nsel, NSA_SEL_LEN, G, D).transpose(0, 3, 1, 2, 4)
    nqb = S // NSA_SEL_QBLOCK
    q_b = q.reshape(B, nqb, NSA_SEL_QBLOCK, G, HPG, D).transpose(1, 0, 2, 3, 4, 5)
    idx_b = sel_idx.reshape(B, G, nqb, NSA_SEL_QBLOCK, K).transpose(2, 0, 1, 3, 4)
    bi = jnp.arange(B)[:, None, None, None]
    gi = jnp.arange(G)[None, :, None, None]

    def one_block(args):
        i, qi, idx = args
        tq = i * NSA_SEL_QBLOCK + jnp.arange(NSA_SEL_QBLOCK)
        kg = kb[bi, gi, idx]
        vg = vb[bi, gi, idx]
        kpos = idx[..., None] * NSA_SEL_LEN + jnp.arange(NSA_SEL_LEN)
        mask = kpos <= tq[None, None, :, None, None]
        s = jnp.einsum('bqgid,bgqkld->bgiqkl', qi, kg).astype(jnp.float32) * NSA_DH ** -0.5
        s = jnp.where(mask[:, :, None], s, NEG)
        p = jax.nn.softmax(s.reshape(B, G, HPG, NSA_SEL_QBLOCK, K * NSA_SEL_LEN), axis=-1)
        p = p.reshape(s.shape).astype(vg.dtype)
        return jnp.einsum('bgiqkl,bgqkld->bqgid', p, vg)

    o = lax.map(one_block, (jnp.arange(nqb), q_b, idx_b))
    return o.transpose(1, 0, 2, 3, 4, 5).reshape(B, S, G, HPG, D)

def nsa_window(q, k_w, v_w):
    B, S, G, HPG, D = q.shape
    nb = S // Q_BLOCK
    span = NSA_WINDOW + Q_BLOCK
    kp = jnp.pad(k_w, ((0, 0), (NSA_WINDOW, 0), (0, 0), (0, 0)))
    vp = jnp.pad(v_w, ((0, 0), (NSA_WINDOW, 0), (0, 0), (0, 0)))
    q_b = q.reshape(B, nb, Q_BLOCK, G, HPG, D).transpose(1, 0, 2, 3, 4, 5)

    def one_block(args):
        i, qi = args
        start = i * Q_BLOCK
        kb = lax.dynamic_slice_in_dim(kp, start, span, axis=1)
        vb = lax.dynamic_slice_in_dim(vp, start, span, axis=1)
        tq = (start + jnp.arange(Q_BLOCK))[:, None]
        kpos = (start - NSA_WINDOW + jnp.arange(span))[None, :]
        mask = (kpos <= tq) & (kpos > tq - NSA_WINDOW) & (kpos >= 0)
        s = jnp.einsum('bqgid,bkgd->bgiqk', qi, kb).astype(jnp.float32) * NSA_DH ** -0.5
        p = jax.nn.softmax(jnp.where(mask, s, NEG), axis=-1).astype(vb.dtype)
        return jnp.einsum('bgiqk,bkgd->bqgid', p, vb)

    o = lax.map(one_block, (jnp.arange(nb), q_b))
    return o.transpose(1, 0, 2, 3, 4, 5).reshape(B, S, G, HPG, D)

def nsa_mixer(x, w_in, cmp_pos, w_ck1, w_ck2, w_cv1, w_cv2, gate_b, w_o):
    B, S, _ = x.shape
    h = x @ w_in
    q, kc, vc, ks, vs, kw, vw, g = jnp.split(h, NSA_SPLITS, axis=-1)
    q = q.reshape(B, S, NSA_GROUPS, NSA_HPG, NSA_DH)

    def kv(t):
        return t.reshape(B, S, NSA_GROUPS, NSA_DH)

    k_cmp = compress_kv(kv(kc), cmp_pos[0], w_ck1, w_ck2)
    v_cmp = compress_kv(kv(vc), cmp_pos[1], w_cv1, w_cv2)
    o_cmp, p_cmp = nsa_compressed(q, k_cmp, v_cmp)
    sel_idx = nsa_select_blocks(p_cmp)
    o_slc = nsa_selected(q, kv(ks), kv(vs), sel_idx)
    o_win = nsa_window(q, kv(kw), kv(vw))
    gates = jax.nn.sigmoid(g + gate_b).reshape(B, S, NSA_BRANCHES, NSA_GROUPS, NSA_HPG, 1)
    o = gates[:, :, 0] * o_cmp + gates[:, :, 1] * o_slc + gates[:, :, 2] * o_win
    return o.reshape(B, S, C_MIX) @ w_o

def hier_moe(x, w_rg, b_rg, w_re, b_re, w_gate, w_up, w_down):
    B, S, D = x.shape
    T = B * S
    xt = x.reshape(T, D)
    g_logits = (xt @ w_rg + b_rg).astype(jnp.float32)
    g_prob = jax.nn.softmax(g_logits, axis=-1)
    g_sel = jnp.argmax(g_logits, axis=-1)
    g_w = jnp.take_along_axis(g_prob, g_sel[:, None], axis=-1)
    e_logits = (xt @ w_re + b_re).astype(jnp.float32).reshape(T, MOE_GROUPS, MOE_EPG)
    e_sel = jnp.take_along_axis(e_logits, g_sel[:, None, None], axis=1)[:, 0]
    top_p, top_i = lax.top_k(jax.nn.softmax(e_sel, axis=-1), MOE_TOPK)
    top_p = top_p / top_p.sum(-1, keepdims=True)
    w_grp = (jax.nn.one_hot(top_i, MOE_EPG, dtype=jnp.float32) * top_p[..., None]).sum(1) * g_w
    y = jnp.zeros_like(xt)
    for gi in range(MOE_GROUPS):
        e0 = gi * MOE_EPG
        wg = jnp.where(g_sel[:, None] == gi, w_grp, 0.0).astype(x.dtype)
        hg = (jax.nn.silu(jnp.einsum('td,edf->tef', xt, w_gate[e0:e0 + MOE_EPG]))
              * jnp.einsum('td,edf->tef', xt, w_up[e0:e0 + MOE_EPG]))
        y = y + jnp.einsum('tef,efd->td', hg * wg[..., None], w_down[e0:e0 + MOE_EPG])
    return y.reshape(B, S, D)

def first_inputs(seed: int = 0) -> dict:
    key = jax.random.key(seed)
    keys = iter(jax.random.split(key, 48))

    def nrm(shape, scale):
        return jax.random.normal(next(keys), shape, jnp.float32) * scale

    def gain(shape):
        return 1.0 + nrm(shape, 0.1)

    x = nrm((BATCH, SEQ, D_MODEL), 1.0)
    offset = jax.random.randint(next(keys), (BATCH, 1), 0, 4096, dtype=jnp.int32)
    positions = (offset + jnp.arange(SEQ, dtype=jnp.int32)[None, :]).astype(jnp.int32)
    return {
        'x': x,
        'positions': positions,
        'ab_w_in': nrm((N_EVEN, D_MODEL, AB_IN), D_MODEL ** -0.5),
        'ab_gm_ln_g': gain((N_EVEN, GM_WIDTH)),
        'ab_gm_ln_b': nrm((N_EVEN, GM_WIDTH), 0.02),
        'ab_gm_ws': nrm((N_EVEN, GM_GROUPS, GM_CHUNK, GM_CHUNK), GM_CHUNK ** -0.5),
        'ab_gm_bs': gain((N_EVEN, GM_GROUPS, GM_CHUNK)),
        'ab_mla_q_norm': gain((N_EVEN, MLA_Q_RANK)),
        'ab_mla_kv_norm': gain((N_EVEN, MLA_KV_RANK)),
        'ab_mla_w_uq': nrm((N_EVEN, MLA_Q_RANK, MLA_HEADS * (MLA_NOPE + MLA_ROPE)), MLA_Q_RANK ** -0.5),
        'ab_mla_w_uk': nrm((N_EVEN, MLA_KV_RANK, MLA_HEADS * MLA_NOPE), MLA_KV_RANK ** -0.5),
        'ab_mla_w_uv': nrm((N_EVEN, MLA_KV_RANK, MLA_HEADS * MLA_V), MLA_KV_RANK ** -0.5),
        'ab_w_o': nrm((N_EVEN, AB_MIX, D_MODEL), AB_MIX ** -0.5 * DN_BETA),
        'c_w_in': nrm((N_ODD, D_MODEL, C_IN), D_MODEL ** -0.5),
        'c_cmp_pos': nrm((N_ODD, 2, NSA_CMP_LEN, NSA_DH), 0.1),
        'c_w_ck1': nrm((N_ODD, NSA_CMP_LEN * NSA_DH, NSA_CMP_HIDDEN), (NSA_CMP_LEN * NSA_DH) ** -0.5),
        'c_w_ck2': nrm((N_ODD, NSA_CMP_HIDDEN, NSA_DH), NSA_CMP_HIDDEN ** -0.5),
        'c_w_cv1': nrm((N_ODD, NSA_CMP_LEN * NSA_DH, NSA_CMP_HIDDEN), (NSA_CMP_LEN * NSA_DH) ** -0.5),
        'c_w_cv2': nrm((N_ODD, NSA_CMP_HIDDEN, NSA_DH), NSA_CMP_HIDDEN ** -0.5),
        'c_gate_b': nrm((N_ODD, NSA_BRANCHES * NSA_HEADS), 0.1),
        'c_w_o': nrm((N_ODD, C_MIX, D_MODEL), C_MIX ** -0.5 * DN_BETA),
        'moe_w_rg': nrm((DEPTH, D_MODEL, MOE_GROUPS), D_MODEL ** -0.5),
        'moe_b_rg': nrm((DEPTH, MOE_GROUPS), 0.01),
        'moe_w_re': nrm((DEPTH, D_MODEL, MOE_EXPERTS), D_MODEL ** -0.5),
        'moe_b_re': nrm((DEPTH, MOE_EXPERTS), 0.01),
        'moe_w_gate': nrm((DEPTH, MOE_EXPERTS, D_MODEL, MOE_HIDDEN), D_MODEL ** -0.5),
        'moe_w_up': nrm((DEPTH, MOE_EXPERTS, D_MODEL, MOE_HIDDEN), D_MODEL ** -0.5),
        'moe_w_down': nrm((DEPTH, MOE_EXPERTS, MOE_HIDDEN, D_MODEL), MOE_HIDDEN ** -0.5 * DN_BETA),
        'ln1_g': gain((DEPTH, D_MODEL)),
        'ln1_b': nrm((DEPTH, D_MODEL), 0.02),
        'ln2_g': gain((DEPTH, D_MODEL)),
        'ln2_b': nrm((DEPTH, D_MODEL), 0.02),
    }

def first_block(x, positions, ab_w_in, ab_gm_ln_g, ab_gm_ln_b, ab_gm_ws, ab_gm_bs,
              ab_mla_q_norm, ab_mla_kv_norm, ab_mla_w_uq, ab_mla_w_uk, ab_mla_w_uv, ab_w_o,
              c_w_in, c_cmp_pos, c_w_ck1, c_w_ck2, c_w_cv1, c_w_cv2, c_gate_b, c_w_o,
              moe_w_rg, moe_b_rg, moe_w_re, moe_b_re, moe_w_gate, moe_w_up, moe_w_down,
              ln1_g, ln1_b, ln2_g, ln2_b):
    for layer in range(DEPTH):
        j = layer // 2
        if layer % 2 == 0:
            mix = ab_mixer(x, positions, ab_w_in[j], ab_gm_ln_g[j], ab_gm_ln_b[j], ab_gm_ws[j],
                           ab_gm_bs[j], ab_mla_q_norm[j], ab_mla_kv_norm[j], ab_mla_w_uq[j],
                           ab_mla_w_uk[j], ab_mla_w_uv[j], ab_w_o[j])
        else:
            mix = nsa_mixer(x, c_w_in[j], c_cmp_pos[j], c_w_ck1[j], c_w_ck2[j], c_w_cv1[j],
                            c_w_cv2[j], c_gate_b[j], c_w_o[j])
        x = layer_norm(DN_ALPHA * x + mix, ln1_g[layer], ln1_b[layer])
        ffn = hier_moe(x, moe_w_rg[layer], moe_b_rg[layer], moe_w_re[layer], moe_b_re[layer],
                       moe_w_gate[layer], moe_w_up[layer], moe_w_down[layer])
        x = layer_norm(DN_ALPHA * x + ffn, ln2_g[layer], ln2_b[layer])
    return x


CTX_LEN = 256
GRID_W = 64
HEAD_DIM = 64
N_Q_HEADS = 8
N_KV_HEADS = 2
GQA_GROUP = N_Q_HEADS // N_KV_HEADS
Q_WIDTH = N_Q_HEADS * HEAD_DIM
KV_WIDTH = N_KV_HEADS * HEAD_DIM
CONV_WIDTH = D_MODEL - Q_WIDTH
CONV_KERNEL = 31
IN_COLS = Q_WIDTH + 2 * KV_WIDTH + 2 * CONV_WIDTH
ROPE_THETA = 10000.0
ATTN_SCALE = HEAD_DIM ** -0.5
PEER_HEADS = 8
PEER_KEYS = 128
PEER_N = PEER_KEYS * PEER_KEYS
PEER_QDIM = 128
PEER_HALF = PEER_QDIM // 2
PEER_TOPK = 16
PEER_CHUNK = 128
EPS = 1e-6


def rms(x):
    xf = x.astype(jnp.float32)
    return (xf * lax.rsqrt(jnp.mean(xf * xf, axis=-1, keepdims=True) + EPS)).astype(x.dtype)

def layer_norm_2(x, g, b):
    xf = x.astype(jnp.float32)
    mu = jnp.mean(xf, axis=-1, keepdims=True)
    var = jnp.mean(jnp.square(xf - mu), axis=-1, keepdims=True)
    return ((xf - mu) * lax.rsqrt(var + 1e-5)).astype(x.dtype) * g + b

def modulate(x, shift, scale):
    return rms(x) * (1 + scale) + shift

def rope_tables(row, col):
    n = HEAD_DIM // 4
    inv = ROPE_THETA ** (-jnp.arange(n, dtype=jnp.float32) / n)
    ang = jnp.concatenate([row.astype(jnp.float32)[:, None] * inv,
                           col.astype(jnp.float32)[:, None] * inv], axis=-1)
    return jnp.cos(ang), jnp.sin(ang)

def apply_rope(x, cos, sin):
    half = HEAD_DIM // 2
    x1, x2 = x[..., :half], x[..., half:]
    c = cos[None, :, None, :].astype(x.dtype)
    s = sin[None, :, None, :].astype(x.dtype)
    return jnp.concatenate([x1 * c - x2 * s, x1 * s + x2 * c], axis=-1)

def split_cols(p):
    return jnp.split(p, [Q_WIDTH, Q_WIDTH + KV_WIDTH, Q_WIDTH + 2 * KV_WIDTH], axis=-1)

def gqa_core(q, k, v):
    s = jnp.einsum('bqhgd,bkhd->bhgqk', q, k).astype(jnp.float32) * ATTN_SCALE
    p = jax.nn.softmax(s, axis=-1).astype(v.dtype)
    return jnp.einsum('bhgqk,bkhd->bqhgd', p, v)

def attend_latent(q, k_all, v_all):
    B, S = q.shape[:2]
    nb = S // Q_BLOCK
    qb = q.reshape(B, nb, Q_BLOCK, N_KV_HEADS, GQA_GROUP, HEAD_DIM).transpose(1, 0, 2, 3, 4, 5)
    o = lax.map(lambda qi: gqa_core(qi, k_all, v_all), qb)
    return o.transpose(1, 0, 2, 3, 4, 5).reshape(B, S, Q_WIDTH)

def attend_context(q, k, v):
    B, L = q.shape[:2]
    o = gqa_core(q.reshape(B, L, N_KV_HEADS, GQA_GROUP, HEAD_DIM), k, v)
    return o.reshape(B, L, Q_WIDTH)

def conformer_conv(u, conv_w, conv_b, ln_g, ln_b):
    a, gate = jnp.split(u, 2, axis=-1)
    g = a * jax.nn.sigmoid(gate)
    y = lax.conv_general_dilated(
        g, conv_w[:, None, :], window_strides=(1,),
        padding=[(CONV_KERNEL // 2, CONV_KERNEL // 2)],
        dimension_numbers=('NWC', 'WIO', 'NWC'),
        feature_group_count=CONV_WIDTH) + conv_b
    return jax.nn.silu(layer_norm_2(y, ln_g, ln_b))

def merge_groups(o_attn, o_conv, beta_attn, beta_conv, w_o):
    o = jnp.concatenate([rms(o_attn) * beta_attn, rms(o_conv) * beta_conv], axis=-1)
    return o @ w_o

def peer(h, w_pq, sub_keys, u_tab, v_tab):
    B, T, D = h.shape
    q = (h @ w_pq).reshape(B, T, PEER_HEADS, 2, PEER_HALF)
    s = jnp.einsum('bthcd,hckd->bthck', q, sub_keys).astype(jnp.float32)
    top_s, top_i = lax.top_k(s, PEER_TOPK)
    cand = top_s[..., 0, :, None] + top_s[..., 1, None, :]
    best_s, best_j = lax.top_k(cand.reshape(B, T, PEER_HEADS, PEER_TOPK * PEER_TOPK), PEER_TOPK)
    i1 = jnp.take_along_axis(top_i[..., 0, :], best_j // PEER_TOPK, axis=-1)
    i2 = jnp.take_along_axis(top_i[..., 1, :], best_j % PEER_TOPK, axis=-1)
    expert = i1 * PEER_KEYS + i2
    w = jax.nn.softmax(best_s, axis=-1)
    n_chunks = (B * T) // PEER_CHUNK
    hx = h.reshape(n_chunks, PEER_CHUNK, D)
    ex = expert.reshape(n_chunks, PEER_CHUNK, PEER_HEADS * PEER_TOPK)
    wx = w.reshape(n_chunks, PEER_CHUNK, PEER_HEADS * PEER_TOPK)

    def chunk(args):
        hc, ec, wc = args
        u = jnp.take(u_tab, ec, axis=0)
        act = jax.nn.gelu(jnp.einsum('cd,ced->ce', hc, u), approximate=False)
        v = jnp.take(v_tab, ec, axis=0)
        return jnp.einsum('ce,ced->cd', (act * wc).astype(h.dtype), v)

    return lax.map(chunk, (hx, ex, wx)).reshape(B, T, D)

def second_inputs(seed: int = 0) -> dict:
    key = jax.random.key(seed)
    ks = jax.random.split(key, 22)
    D = D_MODEL

    def nrm(k, shape, s):
        return jax.random.normal(k, shape, jnp.float32) * s

    return {
        "x": nrm(ks[0], (BATCH, SEQ, D), 1.0),
        "c": nrm(ks[1], (BATCH, D), 1.0),
        "ctx": nrm(ks[2], (BATCH, CTX_LEN, D), 1.0),
        "c_ctx": nrm(ks[3], (D,), 1.0),
        "w_mod": nrm(ks[4], (DEPTH, D, 6 * D), 0.5 * D ** -0.5),
        "b_mod": nrm(ks[5], (DEPTH, 6 * D), 0.02),
        "w_in": nrm(ks[6], (DEPTH, D, IN_COLS), D ** -0.5),
        "q_gain": 1.0 + nrm(ks[7], (DEPTH, HEAD_DIM), 0.02),
        "k_gain": 1.0 + nrm(ks[8], (DEPTH, HEAD_DIM), 0.02),
        "conv_w": nrm(ks[9], (DEPTH, CONV_KERNEL, CONV_WIDTH), CONV_KERNEL ** -0.5),
        "conv_b": nrm(ks[10], (DEPTH, CONV_WIDTH), 0.02),
        "ln_g": 1.0 + nrm(ks[11], (DEPTH, CONV_WIDTH), 0.02),
        "ln_b": nrm(ks[12], (DEPTH, CONV_WIDTH), 0.02),
        "beta_attn": 1.0 + nrm(ks[13], (DEPTH, Q_WIDTH), 0.02),
        "beta_conv": 1.0 + nrm(ks[14], (DEPTH, CONV_WIDTH), 0.02),
        "w_o": nrm(ks[15], (DEPTH, D, D), D ** -0.5),
        "peer_wq": nrm(ks[16], (DEPTH, D, PEER_HEADS * PEER_QDIM), D ** -0.5),
        "peer_keys": nrm(ks[17], (DEPTH, PEER_HEADS, 2, PEER_KEYS, PEER_HALF), PEER_HALF ** -0.5),
        "peer_u": nrm(ks[18], (DEPTH, PEER_N, D), D ** -0.5),
        "peer_v": nrm(ks[19], (DEPTH, PEER_N, D), 0.5),
        "final_g": 1.0 + nrm(ks[20], (D,), 0.02),
    }

def second_block(x, c, ctx, c_ctx, w_mod, b_mod, w_in, q_gain, k_gain, conv_w, conv_b, ln_g, ln_b,
              beta_attn, beta_conv, w_o, peer_wq, peer_keys, peer_u, peer_v, final_g):
    B, S, D = x.shape
    L = ctx.shape[1]
    ROWS = S // GRID_W
    row = jnp.repeat(jnp.arange(ROWS), GRID_W)
    col = jnp.tile(jnp.arange(GRID_W), ROWS)
    cos, sin = rope_tables(row, col)
    sc = jax.nn.silu(c)
    sc_ctx = jax.nn.silu(c_ctx)
    h_ctx = ctx
    for l in range(DEPTH):
        last = l == DEPTH - 1
        sh1, s1, g1, sh2, s2, g2 = jnp.split((sc @ w_mod[l] + b_mod[l])[:, None, :], 6, axis=-1)
        csh1, cs1, cg1, csh2, cs2, cg2 = jnp.split(sc_ctx @ w_mod[l] + b_mod[l], 6, axis=-1)

        hc = modulate(h_ctx, csh1, cs1)
        if last:
            kc, vc = jnp.split(hc @ w_in[l][:, Q_WIDTH:Q_WIDTH + 2 * KV_WIDTH], 2, axis=-1)
        else:
            qc, kc, vc, uc = split_cols(hc @ w_in[l])
            qc = rms(qc.reshape(B, L, N_Q_HEADS, HEAD_DIM)) * q_gain[l]
        kc = rms(kc.reshape(B, L, N_KV_HEADS, HEAD_DIM)) * k_gain[l]
        vc = vc.reshape(B, L, N_KV_HEADS, HEAD_DIM)

        hx = modulate(x, sh1, s1)
        q, k, v, u = split_cols(hx @ w_in[l])
        q = apply_rope(rms(q.reshape(B, S, N_Q_HEADS, HEAD_DIM)) * q_gain[l], cos, sin)
        k = apply_rope(rms(k.reshape(B, S, N_KV_HEADS, HEAD_DIM)) * k_gain[l], cos, sin)
        v = v.reshape(B, S, N_KV_HEADS, HEAD_DIM)
        o_attn = attend_latent(q, jnp.concatenate([kc, k], axis=1), jnp.concatenate([vc, v], axis=1))
        o_conv = conformer_conv(u, conv_w[l], conv_b[l], ln_g[l], ln_b[l])
        x = x + g1 * merge_groups(o_attn, o_conv, beta_attn[l], beta_conv[l], w_o[l])

        x = x + g2 * peer(modulate(x, sh2, s2), peer_wq[l], peer_keys[l], peer_u[l], peer_v[l])

        if not last:
            oc_attn = attend_context(qc, kc, vc)
            oc_conv = conformer_conv(uc, conv_w[l], conv_b[l], ln_g[l], ln_b[l])
            h_ctx = h_ctx + cg1 * merge_groups(oc_attn, oc_conv, beta_attn[l], beta_conv[l], w_o[l])
            h_ctx = h_ctx + cg2 * peer(modulate(h_ctx, csh2, cs2), peer_wq[l], peer_keys[l], peer_u[l], peer_v[l])

    return rms(x) * final_g


def setup_inputs(seed=0):
    out = dict(first_inputs(seed))
    for name, value in second_inputs(seed + 1).items():
        if name != "x":
            out[name + "_2"] = value
    return out


def reference(
    x, positions, ab_w_in, ab_gm_ln_g, ab_gm_ln_b, ab_gm_ws, ab_gm_bs, ab_mla_q_norm,
    ab_mla_kv_norm, ab_mla_w_uq, ab_mla_w_uk, ab_mla_w_uv, ab_w_o, c_w_in, c_cmp_pos, c_w_ck1,
    c_w_ck2, c_w_cv1, c_w_cv2, c_gate_b, c_w_o, moe_w_rg, moe_b_rg, moe_w_re, moe_b_re,
    moe_w_gate, moe_w_up, moe_w_down, ln1_g, ln1_b, ln2_g, ln2_b, c_2, ctx_2, c_ctx_2, w_mod_2,
    b_mod_2, w_in_2, q_gain_2, k_gain_2, conv_w_2, conv_b_2, ln_g_2, ln_b_2, beta_attn_2,
    beta_conv_2, w_o_2, peer_wq_2, peer_keys_2, peer_u_2, peer_v_2, final_g_2,
):
    x = first_block(
        x, positions, ab_w_in, ab_gm_ln_g, ab_gm_ln_b, ab_gm_ws, ab_gm_bs, ab_mla_q_norm,
        ab_mla_kv_norm, ab_mla_w_uq, ab_mla_w_uk, ab_mla_w_uv, ab_w_o, c_w_in, c_cmp_pos,
        c_w_ck1, c_w_ck2, c_w_cv1, c_w_cv2, c_gate_b, c_w_o, moe_w_rg, moe_b_rg, moe_w_re,
        moe_b_re, moe_w_gate, moe_w_up, moe_w_down, ln1_g, ln1_b, ln2_g, ln2_b,
    )
    return second_block(
        x, c_2, ctx_2, c_ctx_2, w_mod_2, b_mod_2, w_in_2, q_gain_2, k_gain_2, conv_w_2,
        conv_b_2, ln_g_2, ln_b_2, beta_attn_2, beta_conv_2, w_o_2, peer_wq_2, peer_keys_2,
        peer_u_2, peer_v_2, final_g_2,
    )


_drawn_inputs = setup_inputs


def setup_inputs(seed=0):
    import zlib

    import numpy as np

    out = dict(_drawn_inputs(seed))
    spreads = {}
    factors = {'ab_gm_ln_g': 2.713,
     'ab_gm_ln_b': 5.992,
     'ab_mla_q_norm': 4.85,
     'ab_mla_kv_norm': 3.336,
     'c_cmp_pos': 3.599,
     'c_gate_b': 4.971,
     'moe_b_rg': 4.641,
     'moe_b_re': 6.495,
     'q_gain_2': 8.0,
     'k_gain_2': 8.0,
     'conv_b_2': 3.816,
     'ln_g_2': 4.524,
     'ln_b_2': 5.206,
     'beta_attn_2': 5.353,
     'beta_conv_2': 5.39,
     'final_g_2': 2.839}
    for name, (base, spread) in spreads.items():
        noise = np.random.default_rng([zlib.crc32(name.encode()), seed]).standard_normal(out[name].shape)
        drawn = base * np.exp(spread * noise) if base else spread * noise
        out[name] = __import__('jax').numpy.asarray(drawn.astype(out[name].dtype))
    for name, factor in factors.items():
        out[name] = (out[name] * factor).astype(out[name].dtype)
    return out
```

```python
import math
from contextlib import ExitStack

import numpy as np

import concourse.bass as bass
from concourse import mybir

F32 = mybir.dt.float32
U32 = mybir.dt.uint32
I32 = mybir.dt.int32
ALU = mybir.AluOpType
ACT = mybir.ActivationFunctionType
AX_X = mybir.AxisListType.X

P = 128
SEQ = 256
NT = SEQ // P
D = 1024
KD = D // P
CHUNK = 256
BANK = 512
LOWEST = -3.0e38
NEG = -1e30
LN_EPS = 1e-5
RMS_EPS = 1e-6
DEPTH = 2
ALPHA = (2.0 * DEPTH) ** 0.25

GM_W, GM_G = 512, 4
Q_RANK, KV_RANK, ROPE = 256, 128, 32
MLA_H, NOPE, MLA_V = 8, 64, 64
MLA_D = NOPE + ROPE
NSA_H, NSA_G, DH = 16, 2, 64
CMP_LEN, CMP_STRIDE, CMP_HID = 32, 16, 256
N_CMP = SEQ // CMP_STRIDE - CMP_LEN // CMP_STRIDE + 1
MOE_G, MOE_E, MOE_HID = 4, 8, 256
N_EXP = MOE_G * MOE_E

Q_HEADS, KV_HEADS = 8, 2
QW, KVW, CONV_W, CONV_K = 512, 128, 512, 31
PEER_H, PEER_K, PEER_TOP = 8, 128, 16


class Program:

    def __init__(self, nc, ctx):
        self.nc, self.ctx = nc, ctx
        self.engine = {"tensor": nc.tensor, "vector": nc.vector, "scalar": nc.scalar,
                       "gpsimd": nc.gpsimd, "sync": nc.sync}
        self.done = {e: ctx.enter_context(nc.semaphore(f"{e}_done")) for e in self.engine}
        self.count = {e: 0 for e in self.engine}
        self.passed = {e: {} for e in self.engine}

    def wait(self, engine, tokens):
        for sem, value in tokens:
            if value > self.passed[engine].get(sem.name, 0):
                self.passed[engine][sem.name] = value
                self.engine[engine].wait_ge(sem, value)

    def op(self, engine, issue, *after):
        if engine != "tensor" and self.count[engine]:
            after += ((self.done[engine], self.count[engine]),)
        self.wait(engine, after)
        self.count[engine] += 1
        issue(self.engine[engine]).then_inc(self.done[engine], 1)
        return (self.done[engine], self.count[engine])

    def quiet(self, engine, issue, *after):
        self.wait(engine, after)
        issue(self.engine[engine])

    def dma(self, queue, dst, src, sem):
        self.engine[queue].dma_start(dst, src).then_inc(sem, 16)

    def latest(self, engine):
        return (self.done[engine], self.count[engine])

    def stage(self):
        tokens = [t for t in map(self.latest, ("tensor", "vector", "scalar", "gpsimd")) if t[1]]
        for e in ("tensor", "vector", "scalar", "gpsimd"):
            self.wait(e, tokens)


class Ring:

    def __init__(self, prog, name, queue, slots, width):
        self.prog, self.queue, self.n = prog, queue, slots
        self.buf = [prog.ctx.enter_context(prog.nc.sbuf_tensor(f"{name}{i}", [P, width], F32))
                    for i in range(slots)]
        self.sem = [prog.ctx.enter_context(prog.nc.semaphore(f"{name}_filled{i}"))
                    for i in range(slots)]
        self.fills = [0] * slots
        self.free = [()] * slots
        self.at = 0

    def load(self, *moves):
        s = self.at % self.n
        self.at += 1
        self.prog.wait(self.queue, self.free[s])
        self.free[s] = None
        for source, place in moves:
            self.fills[s] += 16
            self.prog.dma(self.queue, place(self.buf[s]), source, self.sem[s])
        return s, self.buf[s], (self.sem[s], self.fills[s])

    def release(self, s, *tokens):
        self.free[s] = tokens


def build(nc, A, out):
    with ExitStack() as ctx:
        _build(nc, ctx, A, out)


def _build(nc, ctx, A, out):
    p = Program(nc, ctx)

    def sb(name, shape, dt=F32):
        return ctx.enter_context(nc.sbuf_tensor(name, shape, dt))

    def PE(f, *after):
        return p.op("tensor", f, *after)

    def V(f, *after):
        return p.op("vector", f, *after)

    def S(f, *after):
        return p.op("scalar", f, *after)

    def G(f, *after):
        return p.op("gpsimd", f, *after)

    psum = [ctx.enter_context(nc.psum_tensor(f"bank{i}", [P, BANK], F32)) for i in range(8)]
    bank_free = [() for _ in range(8)]

    weights = Ring(p, "weight", "sync", 7, KD * CHUNK)
    vectors = Ring(p, "vector_param", "gpsimd", 4, D)

    x_rows = sb("x_rows", [P, NT, D])
    ctx_rows = sb("ctx_rows", [P, NT, D])
    x_cols = sb("x_cols", [P, KD, SEQ])
    ident = sb("ident", [P, P])
    ones = sb("ones", [P, P])
    iota = sb("iota", [P, P])
    causal = sb("causal", [P, NT, SEQ])
    ARENA = 21504
    arena = sb("arena", [P, ARENA])
    top = [0]

    def fresh():
        p.stage()
        top[0] = 0

    def room(shape, parts=P, dt=F32):
        n = int(np.prod(shape))
        a = arena[0:parts, top[0]:top[0] + n]
        top[0] += n
        assert top[0] <= ARENA, top[0]
        if dt is not F32:
            a = a.bitcast(dt)
        if len(shape) == 2:
            a = a.rearrange("p (a b) -> p a b", a=shape[0])
        elif len(shape) == 3:
            a = a.rearrange("p (a b c) -> p a b c", a=shape[0], b=shape[1])
        elif len(shape) == 4:
            a = a.rearrange("p (a b c d) -> p a b c d", a=shape[0], b=shape[1], c=shape[2])
        return a

    def constant(name, tile):
        s = ctx.enter_context(nc.semaphore(f"{name}_loaded"))
        p.dma("scalar", tile, A[name], s)
        return (s, 16)

    t_ident = constant("c_ident", ident[:])
    t_iota = constant("c_iota", iota[:])
    t_causal = constant("c_causal", causal[:])
    t_ones = V(lambda e: e.memset(ones[:], 1.0))
    t_x = constant("x", x_rows[:])
    t_ctx = constant("ctx_2", ctx_rows[:])

    def bcast(ap, shape):
        return ap.broadcast_to(shape)

    def product(bank_ap, pairs, *after):
        for i, (lhsT, rhs, *tok) in enumerate(pairs):
            last = i == len(pairs) - 1
            f = lambda e, l=lhsT, r=rhs, a=(i == 0), z=last: e.matmul(bank_ap, l, r, start=a, stop=z)
            if last:
                return PE(f, *after, *tok)
            p.quiet("tensor", f, *after, *tok)

    evac_turn = [0]

    def copy_out(dst, src, *after):
        evac_turn[0] += 1
        if evac_turn[0] % 2:
            return S(lambda e: e.activation(dst, src, ACT.Copy), *after)
        return V(lambda e: e.tensor_copy(dst, src), *after)

    def to_cols(dst, rows, n, banks, *after, evac=None):
        tokens = []
        for j, k0 in enumerate(range(0, n, 2)):
            b = banks[j % len(banks)]
            ks = range(k0, min(k0 + 2, n))
            for k in ks:
                for t in range(NT):
                    o = psum[b][:, (k - k0) * SEQ + t * P:(k - k0) * SEQ + (t + 1) * P]
                    tok = PE(lambda e, o=o, i=rows(k, t): e.transpose(o, i, ident[:]),
                             *after, t_ident, *bank_free[b])
            if evac is None:
                src = psum[b][:, 0:len(ks) * SEQ].rearrange("p (k t) -> p k t", t=SEQ)
                done = [copy_out(dst[:, k0:k0 + len(ks), :], src, tok)]
            else:
                done = [evac(k, psum[b][:, (k - k0) * SEQ:(k - k0 + 1) * SEQ], tok) for k in ks]
            bank_free[b] = tuple(done)
            tokens += done
        return tokens

    def load_chunk(w, c0, cn):
        s, buf, tok = weights.load(
            (w[:, c0:c0 + cn].rearrange("(k p) n -> p k n", p=P),
             lambda b: b[:, 0:KD * cn].rearrange("p (k n) -> p k n", k=KD)))
        return s, buf[:, 0:KD * cn].rearrange("p (k n) -> p k n", k=KD), tok

    def project_rows(cols, w, c0, cn, bank, *after):
        s, wt, tok = load_chunk(w, c0, cn)
        for t in range(NT):
            o = psum[bank][:, t * CHUNK:t * CHUNK + cn]
            done = product(o, [(cols[:, k, t * P:(t + 1) * P], wt[:, k, :]) for k in range(KD)],
                           *after, tok, *bank_free[bank])
        weights.release(s, done)
        return psum[bank][:].rearrange("p (t n) -> p t n", t=NT)[:, :, 0:cn], done

    def project_cols(cols, w, c0, bank, *after):
        s, wt, tok = load_chunk(w, c0, CHUNK)
        for j in range(2):
            o = psum[bank][:, j * SEQ:(j + 1) * SEQ]
            done = product(o, [(wt[:, k, j * P:(j + 1) * P], cols[:, k, :]) for k in range(KD)],
                           *after, tok, *bank_free[bank])
        weights.release(s, done)
        return psum[bank][:].rearrange("p (j t) -> p j t", j=2), done

    def vector_row(*sources):
        at, moves = 0, []
        for v in sources:
            n = v.shape[0]
            moves.append((v.partition_broadcast(P), lambda b, a=at, n=n: b[:, a:a + n]))
            at += n
        return vectors.load(*moves)

    small = sb("small", [P, 128])
    small_at = [0]

    def tiny(n):
        if small_at[0] + n > 128:
            small_at[0] = 0
        a = small[:, small_at[0]:small_at[0] + n]
        small_at[0] += n
        return a

    def inv_root(dst, src, eps, *after):
        tok = V(lambda e: e.tensor_scalar(dst, src, eps, None, ALU.add), *after)
        tok = S(lambda e: e.activation(dst, dst, ACT.Sqrt), tok)
        return V(lambda e: e.reciprocal(dst, dst), tok)

    def normalise(dst, src, width, *after):
        n = -(-width // 512)
        w = width // n
        stats, mv, rstd = tiny(6 * n), tiny(2), tiny(1)
        for i in range(n):
            tok = V(lambda e, i=i: e.bn_stats(stats[:, 6 * i:6 * i + 6], src[:, w * i:w * (i + 1)]),
                    *after)
        tok = V(lambda e: e.bn_aggr(mv, stats), tok)
        tok = inv_root(rstd, mv[:, 1:2], LN_EPS, tok)
        return V(lambda e: e.tensor_scalar(dst, src, mv[:, 0:1], rstd, ALU.subtract, ALU.mult), tok)

    def rms_factor(src, width, scratch, eps, *after):
        ms, r = tiny(1), tiny(1)
        tok = V(lambda e: e.tensor_tensor_reduce(scratch, src, src, 1.0 / width, 0.0, ALU.mult,
                                                 ALU.add, ms), *after)
        return r, inv_root(r, ms, eps, tok)

    def affine_rows(rows, g, b, scratch_tok):
        sg, bg, tg = vector_row(g)
        sb_, bb, tb = vector_row(b)
        toks = []
        for t in range(NT):
            a = V(lambda e, t=t: e.tensor_tensor(rows[:, t, :], rows[:, t, :], bg[:, 0:g.shape[0]], ALU.mult),
                  scratch_tok[t], tg)
            toks.append(V(lambda e, t=t: e.tensor_tensor(rows[:, t, :], rows[:, t, :], bb[:, 0:g.shape[0]],
                                                         ALU.add), a, tb))
        vectors.release(sg, toks[-1])
        vectors.release(sb_, toks[-1])
        return toks

    def post_norm(g, b, residual_toks):
        toks = [normalise(x_rows[:, t, :], x_rows[:, t, :], D, residual_toks[t]) for t in range(NT)]
        return affine_rows(x_rows, g, b, toks)

    def add_scaled_residual(c0, cn, ps, done):
        return [V(lambda e, t=t: e.scalar_tensor_tensor(
            out=x_rows[:, t, c0:c0 + cn], in0=x_rows[:, t, c0:c0 + cn], scalar=ALPHA,
            in1=ps[:, t, :], op0=ALU.mult, op1=ALU.add), done) for t in range(NT)]

    def attention(tile, heads, nk, q_of, k_of, v_of, scale, mask, finish, bufs, *after):
        masked, prob, prob_t, neg_max, sums = bufs
        hg = BANK // nk
        kt = nk // P
        n = heads // hg
        order = [h0 + h for h0 in range(0, heads, 8) for h in (0, 2, 4, 6, 1, 3, 5, 7)]
        exp_tok, t_tok, mm_tok = {}, {}, {}
        pt_free, prob_free = {}, {}
        out_free = [(), ()]

        def scores(g):
            b = g % 2
            for i in range(hg):
                tok = PE(lambda e, i=i: e.matmul(psum[b][:, i * nk:(i + 1) * nk], q_of(order[g * hg + i]),
                                                 k_of(order[g * hg + i]), start=True, stop=True),
                         *after, *bank_free[b])
            s3 = psum[b][:].rearrange("p (h k) -> p h k", h=hg)
            h0 = order[g * hg]
            nm = neg_max[:, h0:h0 + 2 * hg - 1:2]
            if mask is not None:
                m3 = masked[b].rearrange("p (h k) -> p h k", h=hg)
                tok = V(lambda e: e.scalar_tensor_tensor(
                    out=m3, in0=s3, scalar=scale, in1=bcast(mask.unsqueeze(1), [P, hg, nk]),
                    op0=ALU.mult, op1=ALU.add), tok, t_causal, *exp_tok.get(g - 2, ()))
                bank_free[b] = (tok,)
                tok = V(lambda e: e.tensor_reduce(nm, m3, AX_X, ALU.max, negate=True), tok)
                src, sc = m3, 1.0
            else:
                tok = V(lambda e: e.tensor_reduce(nm, s3, AX_X, ALU.max, negate=True), tok)
                tok = V(lambda e: e.tensor_scalar(nm, nm, scale, None, ALU.mult), tok)
                src, sc = s3, scale
            pr = prob[g % 3].rearrange("p (h k) -> p h k", h=hg)
            for i in range(hg):
                h = h0 + 2 * i
                tok2 = S(lambda e: e.activation(pr[:, i, :], src[:, i, :], ACT.Exp, bias=neg_max[:, h:h + 1],
                                                scale=sc, accum_out=sums[:, h:h + 1]),
                         tok, *prob_free.get(g - 3, ()))
            if mask is None:
                bank_free[b] = (tok2,)
            exp_tok[g] = (tok2,)

        def flips(g):
            b = 2 + g % 2
            for i in range(4):
                tok = PE(lambda e, i=i: e.transpose(psum[b][:, i * P:(i + 1) * P],
                                                    prob[g % 3][:, i * P:(i + 1) * P], ident[:]),
                         *exp_tok[g], *bank_free[b])
            prob_free[g] = (tok,)
            tok = copy_out(prob_t[g % 3], psum[b][:], tok, *pt_free.get(g - 3, ()))
            bank_free[b] = (tok,)
            t_tok[g] = tok

        def values(g):
            for i in range(hg):
                h = order[g * hg + i]
                b = 4 + (h // 8) % 2
                o = psum[b][:, (h % 8) * DH:(h % 8 + 1) * DH]
                tok = product(o, [(prob_t[g % 3][:, (i * kt + j) * P:(i * kt + j + 1) * P], v_of(h, j))
                                  for j in range(kt)], t_tok[g], *bank_free[b])
                if (g * hg + i) % 8 == 7:
                    h -= h % 8
                    bank_free[b] = finish(h, psum[b][:].rearrange("p (h d) -> p h d", h=8),
                                          sums[:, h:h + 8], tok)
            pt_free[g] = (tok,)

        for g in range(n + 2):
            if g < n:
                scores(g)
            if 1 <= g <= n:
                flips(g - 1)
            if g >= 2:
                values(g - 2)

    def attention_buffers():
        return ([room([BANK]) for _ in range(2)], [room([BANK]) for _ in range(3)],
                [room([BANK]) for _ in range(3)], room([NSA_H]), room([NSA_H]))

    def mixer_0():
        fresh()
        w_in = A["ab_w_in"][0]
        t_cols = to_cols(x_cols, lambda k, t: x_rows[:, t, k * P:(k + 1) * P], KD, (0, 1, 2, 3), t_x)
        u, v = room([NT, GM_W]), room([NT, GM_W])
        cq, ckv = room([NT, Q_RANK]), room([NT, KV_RANK + ROPE])
        mix = room([NT, D])
        toks = {}
        for j, (c0, cn, dst, at) in enumerate([
                (1024, 256, cq, 0), (1280, 160, ckv, 0), (512, 256, v, 0), (768, 256, v, 256),
                (0, 256, u, 0), (256, 256, u, 256)]):
            b = 4 + j % 2
            ps, done = project_rows(x_cols, w_in, c0, cn, b, *t_cols)
            d = dst[:, :, at:at + cn]
            if dst is u or dst is v:
                tok = S(lambda e, d=d, ps=ps: e.activation(d, ps, ACT.Gelu_apprx_tanh), done)
            else:
                tok = V(lambda e, d=d, ps=ps: e.tensor_copy(d, ps), done)
            bank_free[b] = (tok,)
            toks[j] = tok

        half = ROPE // 2
        pos_i, pos = room([NT], dt=I32), room([NT])
        freq = room([half])
        ang, turns, cos, sin = (room([NT, half]) for _ in range(4))
        s_pos = ctx.enter_context(nc.semaphore("positions_loaded"))
        p.wait("scalar", [p.latest("vector")])
        p.dma("scalar", pos_i, A["positions"], s_pos)
        p.dma("scalar", freq, A["c_freq"], s_pos)
        tok = V(lambda e: e.tensor_copy(pos, pos_i), (s_pos, 32))
        tok = V(lambda e: e.tensor_tensor(ang, bcast(pos.unsqueeze(2), [P, NT, half]),
                                          bcast(freq.unsqueeze(1), [P, NT, half]), ALU.mult), tok)
        tok = V(lambda e: e.tensor_scalar(turns, ang, 1.0 / (2 * math.pi), None, ALU.mult), tok)
        magic = 1.5 * 2.0 ** 23
        tok = V(lambda e: e.tensor_scalar(turns, turns, magic, None, ALU.add), tok)
        tok = V(lambda e: e.tensor_scalar(turns, turns, magic, None, ALU.subtract), tok)
        rest = 2 * math.pi
        for bits in (10, 10, None):
            part = rest if bits is None else float(np.floor(rest * 2.0 ** (bits - math.floor(math.log2(rest))))
                                                   / 2.0 ** (bits - math.floor(math.log2(rest))))
            rest -= part
            tok = V(lambda e, c=part: e.scalar_tensor_tensor(out=ang, in0=turns, scalar=-c, in1=ang,
                                                             op0=ALU.mult, op1=ALU.add), tok)
        pi = float(np.nextafter(np.float32(math.pi), np.float32(0)))
        wrap = turns
        t1 = V(lambda e: e.tensor_scalar(cos, ang, math.pi / 2, None, ALU.add), tok)
        t1 = V(lambda e: e.tensor_scalar(wrap, cos, pi, -2 * math.pi, ALU.is_gt, ALU.mult), t1)
        t1 = V(lambda e: e.tensor_tensor(cos, cos, wrap, ALU.add), t1)
        t1 = V(lambda e: e.tensor_scalar(cos, cos, pi, -pi, ALU.min, ALU.max), t1)
        t2 = V(lambda e: e.tensor_scalar(sin, ang, pi, -pi, ALU.min, ALU.max), t1)
        t_cs = S(lambda e: e.activation(cos, cos, ACT.Sin), t2)
        t_cs = S(lambda e: e.activation(sin, sin, ACT.Sin), t2, t_cs)

        scratch = room([GM_W])
        sg, gains, t_gain = vector_row(A["ab_mla_q_norm"][0], A["ab_mla_kv_norm"][0])
        nt = []
        for t in range(NT):
            for src, w, g0, dep in ((cq[:, t, :], Q_RANK, 0, toks[0]), (ckv[:, t, 0:KV_RANK], KV_RANK, Q_RANK, toks[1])):
                r, tok = rms_factor(src, w, scratch[:, 0:w], LN_EPS, dep)
                nt.append(V(lambda e, src=src, r=r, g0=g0, w=w: e.scalar_tensor_tensor(
                    out=src, in0=src, scalar=r, in1=gains[:, g0:g0 + w], op0=ALU.mult, op1=ALU.mult), tok, t_gain))
        vectors.release(sg, nt[-1])
        lat = room([3, SEQ])
        t_lat = to_cols(lat, lambda k, t: (cq[:, t, k * P:(k + 1) * P] if k < 2 else ckv[:, t, 0:KV_RANK]),
                        3, (0, 1), *nt)
        q_rows, k_rows = room([NT, MLA_H, MLA_D]), room([NT, MLA_H, MLA_D])
        v_rows = room([NT, MLA_H * MLA_V])
        QD = MLA_H * MLA_D
        s1, wq, t_wq = weights.load((A["ab_mla_w_uq"][0].rearrange("(k p) n -> p k n", p=P),
                                     lambda b: b[:, 0:2 * QD].rearrange("p (k n) -> p k n", k=2)))
        wq = wq[:, 0:2 * QD].rearrange("p (k n) -> p k n", k=2)
        s2, wkv, t_wkv = weights.load((A["ab_mla_w_uk"][0], lambda b: b[:, 0:512]),
                                      (A["ab_mla_w_uv"][0], lambda b: b[:, 512:1024]))
        t_rows = []
        for t in range(NT):
            ts = slice(t * P, (t + 1) * P)
            qf = q_rows[:, t].rearrange("p h d -> p (h d)")
            for i in range(2):
                done = product(psum[2 + i][:, 0:QD // 2], [(lat[:, k, ts], wq[:, k, i * QD // 2:(i + 1) * QD // 2])
                                                           for k in range(2)], *t_lat, t_wq, *bank_free[2 + i])
                bank_free[2 + i] = (copy_out(qf[:, i * QD // 2:(i + 1) * QD // 2], psum[2 + i][:, 0:QD // 2], done),)
                t_rows += bank_free[2 + i]
            for i in range(2):
                done = product(psum[6 + i][:, :], [(lat[:, 2, ts], wkv[:, i * 512:(i + 1) * 512])],
                               *t_lat, t_wkv, *bank_free[6 + i])
                if i == 0:
                    src = psum[6][:, :].rearrange("p (h d) -> p h d", h=MLA_H)
                    bank_free[6] = (copy_out(k_rows[:, t, :, 0:NOPE], src, done),)
                else:
                    bank_free[7] = (copy_out(v_rows[:, t, :], psum[7][:, :], done),)
                t_rows += bank_free[6 + i]
        weights.release(s1, done)
        weights.release(s2, done)
        a1, a2 = room([MLA_H, half]), room([MLA_H, half])
        t_rope = []
        tok = None
        for t in range(NT):
            for x1, x2, h, o1, o2 in (
                    (q_rows[:, t, :, NOPE:NOPE + half], q_rows[:, t, :, NOPE + half:MLA_D], MLA_H,
                     q_rows[:, t, :, NOPE:NOPE + half], q_rows[:, t, :, NOPE + half:MLA_D]),
                    (ckv[:, t, KV_RANK:KV_RANK + half].unsqueeze(1), ckv[:, t, KV_RANK + half:].unsqueeze(1), 1,
                     k_rows[:, t, 0:1, NOPE:NOPE + half], k_rows[:, t, 0:1, NOPE + half:MLA_D])):
                c = bcast(cos[:, t, :].unsqueeze(1), [P, h, half])
                s = bcast(sin[:, t, :].unsqueeze(1), [P, h, half])
                tok = rotate(x1, x2, o1, o2, c, s, a1[:, 0:h], a2[:, 0:h], t_cs, *t_rows)
            tok = V(lambda e, t=t: e.tensor_copy(k_rows[:, t, 1:, NOPE:],
                                                 bcast(k_rows[:, t, 0:1, NOPE:], [P, MLA_H - 1, ROPE])), tok)
            t_rope.append(tok)
        qc, kc = room([MLA_H, SEQ]), room([MLA_H, SEQ])
        t_qk = []
        for j, (dst, src) in enumerate(((qc, q_rows), (kc, k_rows))):
            for h0 in range(0, MLA_H, 2):
                b = 2 + (h0 // 2) % 2
                for h in (h0, h0 + 1):
                    for t in range(NT):
                        o = psum[b][0:MLA_D, (h - h0) * SEQ + t * P:(h - h0) * SEQ + (t + 1) * P]
                        tok = PE(lambda e, o=o, i=src[:, t, h, :]: e.transpose(o, i, ident[:]),
                                 t_rope[-1], *bank_free[b])
                tok = copy_out(dst[0:MLA_D, h0:h0 + 2, :],
                               psum[b][0:MLA_D, :].rearrange("p (h t) -> p h t", h=2), tok)
                bank_free[b] = (tok,)
                t_qk.append(tok)

        sp, wsp, t_wsp = weights.load((A["gm_ws_t"].rearrange("g s t -> s g t"),
                                       lambda b: b[:, 0:512].rearrange("p (g t) -> p g t", g=GM_G)),
                                      (A["gm_bs_t"], lambda b: b[:, 512:516]),
                                      (A["c_upper"], lambda b: b[:, 520:648]))
        ws = room([GM_G, P])
        t_ws = V(lambda e: e.tensor_tensor(ws, wsp[:, 0:512].rearrange("p (g t) -> p g t", g=GM_G),
                                           bcast(wsp[:, 520:648].unsqueeze(1), [P, GM_G, P]), ALU.mult), t_wsp)
        t_v = [normalise(v[:, t, :], v[:, t, :], GM_W, toks[3]) for t in range(NT)]
        t_v = affine_rows(v, A["ab_gm_ln_g"][0], A["ab_gm_ln_b"][0], t_v)
        t_mix = []
        for t in range(NT):
            for g in range(GM_G):
                done = product(psum[6 + t][:, g * P:(g + 1) * P], [(ws[:, g, :], v[:, t, g * P:(g + 1) * P])],
                               t_v[t], t_ws, *bank_free[6 + t])
            for g in range(GM_G):
                gs = slice(g * P, (g + 1) * P)
                tok = V(lambda e, t=t, g=g, gs=gs: e.scalar_tensor_tensor(
                    out=mix[:, t, gs], in0=psum[6 + t][:, gs], scalar=wsp[:, 512 + g:513 + g],
                    in1=u[:, t, gs], op0=ALU.add, op1=ALU.mult), done, toks[5])
            bank_free[6 + t] = (tok,)
            t_mix.append(tok)
        weights.release(sp, t_mix[-1])

        bufs = attention_buffers()
        inv = room([8])
        for t in range(NT):
            def finish(h0, ps, sums, tok, t=t):
                tok = V(lambda e: e.reciprocal(inv, sums), tok)
                tok = V(lambda e: e.tensor_tensor(
                    mix[:, t, GM_W:].rearrange("p (h d) -> p h d", h=8), ps,
                    bcast(inv.unsqueeze(2), [P, 8, DH]), ALU.mult), tok)
                t_mix.append(tok)
                return (tok,)
            nk = (t + 1) * P
            attention(t, MLA_H, nk, lambda h, t=t: qc[0:MLA_D, h, t * P:(t + 1) * P],
                      lambda h, nk=nk: kc[0:MLA_D, h, 0:nk],
                      lambda h, j: v_rows[:, j, h * DH:(h + 1) * DH],
                      float(MLA_D) ** -0.5, causal[:, t, 0:nk], finish, bufs, *t_qk)
        toks = output_projection(mix, A["ab_w_o"][0], add_scaled_residual, x_cols, *t_mix)
        return post_norm(A["ln1_g"][0], A["ln1_b"][0], toks)

    def rotate(x1, x2, o1, o2, c, s, a1, a2, *after):
        t1 = V(lambda e: e.tensor_tensor(a1, x1, s, ALU.mult), *after)
        t2 = V(lambda e: e.tensor_tensor(a2, x2, s, ALU.mult), *after)
        t3 = V(lambda e: e.tensor_tensor(o1, x1, c, ALU.mult), t1, t2)
        t3 = V(lambda e: e.tensor_tensor(o1, o1, a2, ALU.subtract), t3)
        t4 = V(lambda e: e.tensor_tensor(o2, x2, c, ALU.mult), t3)
        return V(lambda e: e.tensor_tensor(o2, o2, a1, ALU.add), t4)

    def output_projection(mix_rows, w, add, cols, *after, evac=None):
        t_cols = to_cols(cols, lambda k, t: mix_rows[:, t, k * P:(k + 1) * P], KD, (0, 1, 2, 3), *after,
                         evac=evac)
        toks = None
        for j, c0 in enumerate(range(0, D, CHUNK)):
            b = 4 + j % 2
            ps, done = project_rows(cols, w, c0, CHUNK, b, *t_cols)
            toks = add(c0, CHUNK, ps, done)
            bank_free[b] = tuple(toks)
        return toks

    def moe(layer, t_in):
        fresh()
        t_cols = to_cols(x_cols, lambda k, t: x_rows[:, t, k * P:(k + 1) * P], KD, (0, 1, 2, 3), *t_in)
        NL = MOE_G + N_EXP
        s, wr, t_wr = weights.load((A["router_w"][layer].rearrange("(k p) n -> p k n", p=P),
                                    lambda b: b[:, 0:KD * NL].rearrange("p (k n) -> p k n", k=KD)))
        wr = wr[:, 0:KD * NL].rearrange("p (k n) -> p k n", k=KD)
        sv, rb, t_rb = vector_row(A["router_b"][layer])
        for t in range(NT):
            done = product(psum[6][:, t * NL:(t + 1) * NL],
                           [(x_cols[:, k, t * P:(t + 1) * P], wr[:, k, :]) for k in range(KD)],
                           *t_cols, t_wr, *bank_free[6])
        weights.release(s, done)
        lg = room([NT, NL])
        tok = V(lambda e: e.tensor_tensor(lg, psum[6][:, 0:NT * NL].rearrange("p (t n) -> p t n", t=NT),
                                          bcast(rb[:, 0:NL].unsqueeze(1), [P, NT, NL]), ALU.add), done, t_rb)
        bank_free[6] = (tok,)
        vectors.release(sv, tok)
        g8, gm8, em8 = room([NT, 8]), room([NT, 8]), room([NT, 8])
        gi, ei = room([NT, 8], dt=U32), room([NT, 8], dt=U32)
        tok = V(lambda e: e.memset(g8, LOWEST), tok)
        tok = V(lambda e: e.tensor_copy(g8[:, :, 0:MOE_G], lg[:, :, 0:MOE_G]), tok)
        for t in range(NT):
            tok = V(lambda e, t=t: e.max(gm8[:, t, :], g8[:, t, :]), tok)
            tok = V(lambda e, t=t: e.max_index(gi[:, t, :], gm8[:, t, :], g8[:, t, :]), tok)
        gsel, ohg = room([NT]), room([NT, MOE_G])
        tok = V(lambda e: e.tensor_copy(gsel, gi[:, :, 0]), tok)
        tok = V(lambda e: e.tensor_tensor(ohg, bcast(iota[:, 0:MOE_G].unsqueeze(1), [P, NT, MOE_G]),
                                          bcast(gsel.unsqueeze(2), [P, NT, MOE_G]), ALU.is_equal), tok, t_iota)
        ge, gsum = room([NT, MOE_G]), room([NT])
        tok = V(lambda e: e.tensor_tensor(ge, lg[:, :, 0:MOE_G], bcast(gm8[:, :, 0:1], [P, NT, MOE_G]),
                                          ALU.subtract), tok)
        t_ge = S(lambda e: e.activation(ge, ge, ACT.Exp), tok)
        esel, picked = room([NT, MOE_E]), room([NT, MOE_E, MOE_G])
        for t in range(NT):
            tok = V(lambda e, t=t: e.tensor_tensor(
                picked[:, t], lg[:, t, MOE_G:].rearrange("p (g e) -> p e g", g=MOE_G),
                bcast(ohg[:, t, :].unsqueeze(1), [P, MOE_E, MOE_G]), ALU.mult), tok)
        tok = V(lambda e: e.tensor_reduce(esel, picked, AX_X, ALU.add), tok)
        for t in range(NT):
            tok = V(lambda e, t=t: e.max(em8[:, t, :], esel[:, t, :]), tok)
            tok = V(lambda e, t=t: e.max_index(ei[:, t, :], em8[:, t, :], esel[:, t, :]), tok)
        p2, p1, eif = room([NT]), room([NT]), room([NT, 2])
        tok = V(lambda e: e.tensor_tensor(p2, em8[:, :, 1], em8[:, :, 0], ALU.subtract), tok)
        t_p2 = S(lambda e: e.activation(p2, p2, ACT.Exp), tok)
        tok = V(lambda e: e.tensor_copy(eif, ei[:, :, 0:2]), tok)
        tok = V(lambda e: e.tensor_reduce(gsum, ge, AX_X, ALU.add), tok, t_ge)
        tok = V(lambda e: e.scalar_tensor_tensor(out=p1, in0=p2, scalar=1.0, in1=gsum, op0=ALU.add,
                                                 op1=ALU.mult), tok, t_p2)
        tok = V(lambda e: e.reciprocal(p1, p1), tok)
        tok = V(lambda e: e.tensor_tensor(p2, p2, p1, ALU.mult), tok)
        oh1, oh2, wmoe = room([NT, MOE_E]), room([NT, MOE_E]), room([NT, MOE_G, MOE_E])
        for oh, j, pr in ((oh1, 0, p1), (oh2, 1, p2)):
            tok = V(lambda e, oh=oh, j=j: e.tensor_tensor(
                oh, bcast(iota[:, 0:MOE_E].unsqueeze(1), [P, NT, MOE_E]),
                bcast(eif[:, :, j:j + 1], [P, NT, MOE_E]), ALU.is_equal), tok)
            tok = V(lambda e, oh=oh, pr=pr: e.tensor_tensor(oh, oh, bcast(pr.unsqueeze(2), [P, NT, MOE_E]),
                                                            ALU.mult), tok)
        tok = V(lambda e: e.tensor_tensor(oh1, oh1, oh2, ALU.add), tok)
        for t in range(NT):
            tok = V(lambda e, t=t: e.tensor_tensor(
                wmoe[:, t], bcast(ohg[:, t, :].unsqueeze(2), [P, MOE_G, MOE_E]),
                bcast(oh1[:, t, :].unsqueeze(1), [P, MOE_G, MOE_E]), ALU.mult), tok)
        wflat = wmoe.rearrange("p t g e -> p t (g e)")
        for t in range(NT):
            tok = V(lambda e, t=t: e.tensor_scalar(x_rows[:, t, :], x_rows[:, t, :], ALPHA, None, ALU.mult),
                    *t_cols, tok)
        t_res = [tok] * NT

        silu = [room([2, SEQ]) for _ in range(2)]
        hid = [room([2, SEQ]) for _ in range(2)]
        hid_tok, down, hid_free = {}, {}, {}

        def up(e_):
            i = e_ % 2
            ps = []
            for b, w in ((2 * i, A["moe_gate"]), (2 * i + 1, A["moe_up"])):
                s, buf, tk = weights.load((w[layer, e_], lambda b: b[:, :]))
                wt = buf[:, :].rearrange("p (k n) -> p k n", k=KD)
                for j in range(2):
                    done = product(psum[b][:, j * SEQ:(j + 1) * SEQ],
                                   [(wt[:, k, j * P:(j + 1) * P], x_cols[:, k, :]) for k in range(KD)],
                                   *t_cols, tk, *bank_free[b])
                weights.release(s, done)
                ps.append((psum[b][:, :].rearrange("p (j t) -> p j t", j=2), done))
            down[e_] = weights.load((A["moe_w_down"][layer, e_].rearrange("(j p) n -> p j n", p=P),
                                     lambda b: b[:, :].rearrange("p (j n) -> p j n", j=2)))
            a = S(lambda e: e.activation(silu[i], ps[0][0], ACT.Silu), ps[0][1], *hid_free.get(e_ - 2, ()))
            bank_free[2 * i] = (a,)
            h = V(lambda e: e.tensor_tensor(hid[i], silu[i], ps[1][0], ALU.mult), a, ps[1][1],
                  *hid_free.get(e_ - 2, ()))
            bank_free[2 * i + 1] = (h,)
            hid_tok[e_] = h

        def out_(e_):
            i = e_ % 2
            s, buf, tk = down[e_]
            wt = buf[:, :].rearrange("p (j n) -> p j n", j=2)
            for t in range(NT):
                for h in range(2):
                    b = 4 + 2 * t + h
                    done = product(psum[b][:, :], [(hid[i][:, j, t * P:(t + 1) * P], wt[:, j, h * 512:(h + 1) * 512])
                                                   for j in range(2)], hid_tok[e_], tk, *bank_free[b])
                    xs = x_rows[:, t, h * 512:(h + 1) * 512]
                    t_res[t] = V(lambda e, xs=xs, b=b, t=t: e.scalar_tensor_tensor(
                        out=xs, in0=psum[b][:, :], scalar=wflat[:, t, e_:e_ + 1], in1=xs,
                        op0=ALU.mult, op1=ALU.add), done, t_res[t])
                    bank_free[b] = (t_res[t],)
            weights.release(s, done)
            hid_free[e_] = (done,)

        for e_ in range(N_EXP + 1):
            if e_ < N_EXP:
                up(e_)
            if e_ >= 1:
                out_(e_ - 1)
        return post_norm(A["ln2_g"][layer], A["ln2_b"][layer], [t_res[1], t_res[1]])

    def store(rows, *after):
        s = ctx.enter_context(nc.semaphore("stored"))
        p.wait("sync", after)
        p.dma("sync", out.rearrange("b (t p) d -> p (b t) d", p=P), rows, s)
        p.wait("sync", [(s, 16)])

    def mixer_1(t_in):
        fresh()
        w_in = A["c_w_in"][0]
        t_cols = to_cols(x_cols, lambda k, t: x_rows[:, t, k * P:(k + 1) * P], KD, (0, 1, 2, 3), *t_in)
        q = room([NSA_H // 2, SEQ])
        kv = {n: room([NSA_G, SEQ]) for n in ("ks", "kw")}
        vals = {n: room([NT, P]) for n in ("vs", "vw")}
        raw = {n: room([NSA_G, SEQ], parts=DH) for n in ("kc", "vc")}
        gates = room([NT, 3 * NSA_H])
        o_rows = room([NT, D])
        t_q = []
        for j in range(4):
            b = 4 + j % 2
            ps, done = project_cols(x_cols, w_in, j * CHUNK, b, *t_cols)
            tok = copy_out(q[:, 2 * j:2 * j + 2, :], ps, done)
            bank_free[b] = (tok,)
            t_q.append(tok)
        t_kv = {}
        for pair, c0 in ((("kc", "vc"), 1024), (("ks", "vs"), 1280), (("kw", "vw"), 1536)):
            s, wt, tw = load_chunk(w_in, c0, CHUNK)
            for i, n in enumerate(pair):
                b = 4 + i
                if n in vals:
                    for t in range(NT):
                        done = product(psum[b][:, t * P:(t + 1) * P],
                                       [(x_cols[:, k, t * P:(t + 1) * P], wt[:, k, i * P:(i + 1) * P])
                                        for k in range(KD)], *t_cols, tw, *bank_free[b])
                    tok = copy_out(vals[n], psum[b][:, 0:NT * P].rearrange("p (t n) -> p t n", t=NT), done)
                else:
                    for g in range(NSA_G):
                        for half in ((0, DH) if n in kv else (0,)):
                            done = product(psum[b][half:half + DH, g * SEQ:(g + 1) * SEQ],
                                           [(wt[:, k, i * P + g * DH:i * P + (g + 1) * DH], x_cols[:, k, :])
                                            for k in range(KD)], *t_cols, tw, *bank_free[b])
                    m = P if n in kv else DH
                    dst = kv[n] if n in kv else raw[n]
                    tok = copy_out(dst, psum[b][0:m, :].rearrange("p (g t) -> p g t", g=NSA_G), done)
                bank_free[b] = (tok,)
                t_kv[n] = tok
            weights.release(s, done)
        NG = 3 * NSA_H
        sv, gb, t_gb = vector_row(A["c_gate_b"][0])
        ps, done = project_rows(x_cols, w_in, 1792, NG, 4, *t_cols)
        tok = V(lambda e: e.tensor_tensor(gates, ps, bcast(gb[:, 0:NG].unsqueeze(1), [P, NT, NG]), ALU.add),
                done, t_gb)
        bank_free[4] = (tok,)
        vectors.release(sv, tok)
        t_gate = S(lambda e: e.activation(gates, gates, ACT.Sigmoid), tok)

        NB = NSA_G * N_CMP
        k_cmp = room([NB])
        v_cmp = room([NSA_G, DH])
        blocks = room([CMP_LEN, NB], parts=DH)
        hidden = room([2, NB])
        pos_col = room([2, CMP_LEN], parts=DH)
        s_pc = ctx.enter_context(nc.semaphore("cmp_pos_loaded"))
        p.wait("scalar", [p.latest("vector")])
        p.dma("scalar", pos_col, A["cmp_pos_t"], s_pc)
        PER = 8
        for i, (n, w1, w2) in enumerate((("kc", "c_w_ck1", "c_w_ck2"), ("vc", "c_w_cv1", "c_w_cv2"))):
            src = raw[n].rearrange("p g (m b) -> p g m b", b=CMP_STRIDE)
            for a in range(CMP_LEN // CMP_STRIDE):
                for g in range(NSA_G):
                    dst = blocks[:, a * CMP_STRIDE:(a + 1) * CMP_STRIDE, g * N_CMP:(g + 1) * N_CMP]
                    tok = V(lambda e, a=a, g=g, dst=dst: e.tensor_tensor(
                        dst, src[:, g, a:a + N_CMP, :].rearrange("p m b -> p b m"),
                        bcast(pos_col[:, i, a * CMP_STRIDE:(a + 1) * CMP_STRIDE].unsqueeze(2),
                              [DH, CMP_STRIDE, N_CMP]), ALU.add), t_kv[n], (s_pc, 16), p.latest("tensor"))
            slots = [weights.load((A[w1][0, l0 * DH:(l0 + PER) * DH, :].rearrange("(l d) n -> d l n", d=DH),
                                   lambda b: b[0:DH, :].rearrange("p (l n) -> p l n", l=PER)))
                     for l0 in range(0, CMP_LEN, PER)]
            for j in range(2):
                pairs = []
                for l in range(CMP_LEN):
                    s, buf, tw = slots[l // PER]
                    c0 = (l % PER) * CMP_HID + j * P
                    pairs.append((buf[0:DH, c0:c0 + P], blocks[:, l, :], tw))
                done = product(psum[6][:, j * NB:(j + 1) * NB], pairs, tok, *bank_free[6])
            for s, _, _ in slots:
                weights.release(s, done)
            tok = S(lambda e: e.activation(hidden, psum[6][:, 0:2 * NB].rearrange("p (j n) -> p j n", j=2),
                                           ACT.Gelu_apprx_tanh), done)
            bank_free[6] = (tok,)
            s, buf, tw = weights.load((A[w2][0].rearrange("(j p) n -> p j n", p=P),
                                       lambda b: b[:, 0:2 * DH].rearrange("p (j n) -> p j n", j=2)))
            if n == "kc":
                for half in (0, DH):
                    done = product(psum[7][half:half + DH, 0:NB],
                                   [(buf[:, j * DH:(j + 1) * DH], hidden[:, j, :]) for j in range(2)],
                                   tok, tw, *bank_free[7])
                tok = t_kc = copy_out(k_cmp, psum[7][:, 0:NB], done)
            else:
                for g in range(NSA_G):
                    done = product(psum[7][0:N_CMP, g * DH:(g + 1) * DH],
                                   [(hidden[:, j, g * N_CMP:(g + 1) * N_CMP], buf[:, j * DH:(j + 1) * DH])
                                    for j in range(2)], tok, tw, *bank_free[7])
                tok = t_vc = copy_out(v_cmp[0:N_CMP], psum[7][0:N_CMP, 0:NSA_G * DH]
                                      .rearrange("p (g d) -> p g d", g=NSA_G), done)
            bank_free[7] = (tok,)
            weights.release(s, done)

        def q_of(h, ts):
            half = (h % 2) * DH
            return q[half:half + DH, h // 2, ts]

        cmask = room([NT, 3, N_CMP])
        s_cm = ctx.enter_context(nc.semaphore("cmp_mask_loaded"))
        p.dma("scalar", cmask, A["c_cmp_mask"], s_cm)
        sc, csum, cmax = room([NSA_H, N_CMP]), room([NSA_H]), room([NSA_H])
        pt = room([4, P])
        factor = room([8])
        part = room([8, DH])
        t_o = []
        for t in range(NT):
            ts = slice(t * P, (t + 1) * P)
            shape = [P, NSA_H, N_CMP]
            for odd in range(2):
                b, half, nh = 6 + odd, odd * DH, NSA_H // 2
                for i in range(nh):
                    h = 2 * i + odd
                    g = h // 8
                    done = product(psum[b][:, i * N_CMP:(i + 1) * N_CMP],
                                   [(q_of(h, ts), k_cmp[half:half + DH, g * N_CMP:(g + 1) * N_CMP])],
                                   *t_q, t_kc, *bank_free[b])
                tok = V(lambda e: e.scalar_tensor_tensor(
                    out=sc[:, odd::2, :], in0=psum[b][:, 0:nh * N_CMP].rearrange("p (h n) -> p h n", h=nh),
                    scalar=DH ** -0.5, in1=bcast(cmask[:, t, 0:1, :], [P, nh, N_CMP]), op0=ALU.mult,
                    op1=ALU.add), done, (s_cm, 16), p.latest("tensor"))
                bank_free[b] = (tok,)
            tok = V(lambda e: e.tensor_reduce(cmax, sc, AX_X, ALU.max), tok)
            tok = V(lambda e: e.tensor_tensor(sc, sc, bcast(cmax.unsqueeze(2), shape), ALU.subtract), tok)
            tok = S(lambda e: e.activation(sc, sc, ACT.Exp), tok)
            tok = V(lambda e, t=t: e.tensor_tensor(sc, sc, bcast(cmask[:, t, 1:2, :], shape), ALU.mult), tok)
            t_sc = tok
            tok = V(lambda e: e.tensor_reduce(csum, sc, AX_X, ALU.add), tok)
            tok = V(lambda e, t=t: e.tensor_scalar(csum, csum, cmask[:, t, 2, 0:1], None, ALU.add), tok)
            tok = V(lambda e: e.reciprocal(csum, csum), tok)
            tok = t_fac = V(lambda e, t=t: e.tensor_tensor(csum, csum, gates[:, t, 0:NSA_H], ALU.mult), tok, t_gate)
            for h0 in range(0, NSA_H, 4):
                b = h0 // 4 % 2
                for i in range(4):
                    tok = PE(lambda e, i=i: e.transpose(psum[b][0:N_CMP, i * P:(i + 1) * P], sc[:, h0 + i, :],
                                                        ident[:]), t_sc, *bank_free[b])
                tok = copy_out(pt[0:N_CMP], psum[b][0:N_CMP, :].rearrange("p (i t) -> p i t", i=4), tok,
                               p.latest("tensor"))
                bank_free[b] = (tok,)
                ob = 2 + h0 // 8
                for i in range(4):
                    h = h0 + i
                    done = product(psum[ob][:, (h % 8) * DH:(h % 8 + 1) * DH],
                                   [(pt[0:N_CMP, i, :], v_cmp[0:N_CMP, h // 8, :])], tok, t_vc, *bank_free[ob])
                if h0 % 8 == 4:
                    hb = h0 - 4
                    tok = V(lambda e, t=t, hb=hb, ob=ob: e.tensor_tensor(
                        o_rows[:, t, hb * DH:(hb + 8) * DH].rearrange("p (h d) -> p h d", h=8),
                        psum[ob][:, :].rearrange("p (h d) -> p h d", h=8),
                        bcast(csum[:, hb:hb + 8].unsqueeze(2), [P, 8, DH]), ALU.mult), done, t_fac)
                    bank_free[ob] = (tok,)
        bufs = attention_buffers()
        for br, (kn, vn) in enumerate((("ks", "vs"), ("kw", "vw"))):
            for t in range(NT):
                def finish(h0, ps, sums, tok, t=t, br=br):
                    tok = V(lambda e: e.reciprocal(factor, sums), tok)
                    g0 = (br + 1) * NSA_H + h0
                    tok = V(lambda e: e.tensor_tensor(factor, factor, gates[:, t, g0:g0 + 8], ALU.mult), tok)
                    tok = V(lambda e: e.tensor_tensor(part, ps, bcast(factor.unsqueeze(2), [P, 8, DH]),
                                                      ALU.mult), tok)
                    o = o_rows[:, t, h0 * DH:(h0 + 8) * DH].rearrange("p (h d) -> p h d", h=8)
                    t_o.append(V(lambda e: e.tensor_tensor(o, o, part, ALU.add), tok))
                    return (tok,)
                ts, nk = slice(t * P, (t + 1) * P), (t + 1) * P
                attention(t, NSA_H, nk, lambda h, ts=ts: q_of(h, ts),
                          lambda h, nk=nk, kn=kn: kv[kn][(h % 2) * DH:(h % 2 + 1) * DH, h // 8, 0:nk],
                          lambda h, j, vn=vn: vals[vn][:, j, (h // 8) * DH:(h // 8 + 1) * DH],
                          DH ** -0.5, causal[:, t, 0:nk], finish, bufs, *t_q, *t_kv.values())
        toks = output_projection(o_rows, A["c_w_o"][0], add_scaled_residual, x_cols, *t_o)
        return post_norm(A["ln1_g"][1], A["ln1_b"][1], toks)

    NMOD = 6 * KD
    mod = [sb(f"mod{l}", [P, NMOD, 2]) for l in range(DEPTH)]
    gate_rows = sb("gate_rows", [P, 2, D])
    rope_cos, rope_sin = sb("rope_cos", [P, NT, DH // 2]), sb("rope_sin", [P, NT, DH // 2])
    param_sems = {}

    def modulation():
        c2, bm = room([KD, 2]), room([DEPTH, NMOD])
        s_c = ctx.enter_context(nc.semaphore("conditions_loaded"))
        p.wait("scalar", [p.latest("vector"), p.latest("tensor")])
        for dst, n in ((c2, "cond"), (bm, "b_mod_t"), (rope_cos[:], "c_rope_cos"), (rope_sin[:], "c_rope_sin")):
            p.dma("scalar", dst, A[n], s_c)
        t_c = S(lambda e: e.activation(c2, c2, ACT.Silu), (s_c, 64))
        for l in range(DEPTH):
            for j in range(NMOD // 2):
                s, wt, tw = load_chunk(A["w_mod_2"][l], j * CHUNK, CHUNK)
                for i in range(2):
                    m = 2 * j + i
                    done = product(psum[7][:, 2 * m:2 * m + 2],
                                   [(wt[:, k, i * P:(i + 1) * P], c2[:, k, :]) for k in range(KD)],
                                   t_c, tw, *bank_free[7])
                weights.release(s, done)
            ps = psum[7][:, 0:2 * NMOD].rearrange("p (m s) -> p m s", s=2)
            tok = V(lambda e, l=l: e.tensor_tensor(mod[l][:], ps, bcast(bm[:, l, :].unsqueeze(2), [P, NMOD, 2]),
                                                   ALU.add), done)
            bank_free[7] = (tok,)
            for m in (KD, 4 * KD):
                tok = V(lambda e, l=l, m=m: e.tensor_scalar(mod[l][:, m:m + KD, :], mod[l][:, m:m + KD, :],
                                                            1.0, None, ALU.add), tok)
        return tok

    def spread_gates(l, stream, after):
        diag = room([KD, P])
        for i, m in enumerate((2 * KD, 5 * KD)):
            tok = V(lambda e, m=m: e.tensor_tensor(diag, bcast(ident[:].unsqueeze(1), [P, KD, P]),
                                                   bcast(mod[l][:, m:m + KD, stream].unsqueeze(2), [P, KD, P]),
                                                   ALU.mult), after, t_ident, p.latest("tensor"))
            for h in range(2):
                done = product(psum[6 + h][:, :], [(ones[:], diag[:, 4 * h:4 * h + 4, :])], tok, t_ones,
                               *bank_free[6 + h])
                after = copy_out(gate_rows[:, i, h * 512:(h + 1) * 512], psum[6 + h][:, :], done)
                bank_free[6 + h] = (after,)
            after = p.latest("vector")
            tok = after
        return (p.latest("vector"), p.latest("scalar"))

    def modulated_cols(dst, rows, l, shift, stream, after):
        normed = room([NT, D])
        toks = []
        for t in range(NT):
            r, tok = rms_factor(rows[:, t, :], D, normed[:, t, :], RMS_EPS, *after)
            toks.append(V(lambda e, t=t, r=r: e.tensor_scalar(normed[:, t, :], rows[:, t, :], r, None, ALU.mult),
                          tok))

        def evac(k, ps, tok):
            sc, sh = mod[l][:, shift + KD + k, stream:stream + 1], mod[l][:, shift + k, stream:stream + 1]
            if k // 2 % 2:
                return S(lambda e: e.activation(dst[:, k, :], ps, ACT.Identity, bias=sh, scale=sc), tok)
            return V(lambda e: e.tensor_scalar(dst[:, k, :], ps, sc, sh, ALU.mult, ALU.add), tok)
        return to_cols(dst, lambda k, t: normed[:, t, k * P:(k + 1) * P], KD, (0, 1, 2, 3), *toks, evac=evac)

    key_cols = sb("key_cols", [P, KV_HEADS, 2 * SEQ])
    val_rows = sb("val_rows", [P, 2 * NT, KVW])

    def qkv(cols, l, with_q, rotary, key_at, after):
        NHEAD = Q_HEADS + KV_HEADS
        qk = room([NT, NHEAD, DH])
        w_in = A["w_in_2"][l]
        flat = qk.rearrange("p t h d -> p t (h d)")
        toks = []
        for j, c0 in enumerate((0, 256, 512) if with_q else (512,)):
            b = 4 + j % 2
            ps, done = project_rows(cols, w_in, c0, CHUNK, b, *after)
            if c0 < QW:
                tok = (copy_out(flat[:, :, c0:c0 + CHUNK], ps, done),)
            else:
                tok = (copy_out(flat[:, :, QW:QW + KVW], ps[:, :, 0:KVW], done),)
                tok += (copy_out(val_rows[:, key_at // P:key_at // P + NT, :], ps[:, :, KVW:], *tok),)
            bank_free[b] = tok
            toks += tok
        h0 = 0 if with_q else Q_HEADS
        nh = NHEAD - h0
        sg, gains, t_g = vectors.load(
            (A["q_gain_2"][l].partition_broadcast(P), lambda b: b[:, 0:DH]),
            (A["k_gain_2"][l].partition_broadcast(P), lambda b: b[:, DH:2 * DH]))
        sq, ms = room([NHEAD, DH]), room([NHEAD])
        a1, a2 = room([NHEAD, DH // 2]), room([NHEAD, DH // 2])
        kdup = room([KV_HEADS, 2, DH])
        q_cols = room([Q_HEADS // 2, SEQ])
        out_toks = []
        for t in range(NT):
            x = qk[:, t, h0:, :]
            tok = V(lambda e: e.tensor_tensor(sq[:, h0:], x, x, ALU.mult), *toks)
            tok = V(lambda e: e.tensor_reduce(ms[:, h0:], sq[:, h0:], AX_X, ALU.add), tok)
            tok = V(lambda e: e.tensor_scalar(ms[:, h0:], ms[:, h0:], 1.0 / DH, RMS_EPS, ALU.mult, ALU.add), tok)
            tok = S(lambda e: e.activation(ms[:, h0:], ms[:, h0:], ACT.Sqrt), tok)
            tok = V(lambda e: e.reciprocal(ms[:, h0:], ms[:, h0:]), tok)
            tok = V(lambda e: e.tensor_tensor(x, x, bcast(ms[:, h0:].unsqueeze(2), [P, nh, DH]), ALU.mult), tok)
            for a, b, g0 in ((h0, Q_HEADS, 0), (Q_HEADS, NHEAD, DH)):
                if b > a:
                    y = qk[:, t, a:b, :]
                    tok = V(lambda e, y=y, g0=g0, n=b - a: e.tensor_tensor(
                        y, y, bcast(gains[:, g0:g0 + DH].unsqueeze(1), [P, n, DH]), ALU.mult), tok, t_g)
            if rotary:
                hf = DH // 2
                c = bcast(rope_cos[:, t, :].unsqueeze(1), [P, nh, hf])
                s = bcast(rope_sin[:, t, :].unsqueeze(1), [P, nh, hf])
                tok = rotate(x[:, :, 0:hf], x[:, :, hf:], x[:, :, 0:hf], x[:, :, hf:], c, s,
                             a1[:, h0:], a2[:, h0:], tok)
            tok = V(lambda e, t=t: e.tensor_copy(kdup, bcast(qk[:, t, Q_HEADS:, :].unsqueeze(2),
                                                             [P, KV_HEADS, 2, DH])), tok, p.latest("tensor"))
            for g in range(KV_HEADS):
                done = PE(lambda e, g=g: e.transpose(psum[6][:, g * P:(g + 1) * P],
                                                     kdup[:, g].rearrange("p a d -> p (a d)"), ident[:]),
                          tok, *bank_free[6])
            k0 = key_at + t * P
            kt = copy_out(key_cols[:, :, k0:k0 + P], psum[6][:, 0:2 * P].rearrange("p (g t) -> p g t", g=2), done)
            bank_free[6] = (kt,)
            out_toks.append(kt)
            if with_q:
                for j in range(Q_HEADS // 2):
                    done = PE(lambda e, j=j, t=t: e.transpose(
                        psum[7][:, j * P:(j + 1) * P], flat[:, t, j * P:(j + 1) * P], ident[:]),
                        tok, *bank_free[7])
                kt = copy_out(q_cols[:, :, t * P:(t + 1) * P],
                              psum[7][:, :].rearrange("p (j t) -> p j t", t=P), done)
                bank_free[7] = (kt,)
                out_toks.append(kt)
        vectors.release(sg, p.latest("vector"))
        return q_cols, out_toks + toks

    def conformer(cols, l, dst, after):
        NC = CONV_W // P
        PAD = CONV_K // 2
        w_in = A["w_in_2"][l]
        g = room([NC, SEQ + 2 * PAD])
        y = room([NC, SEQ])
        a, gt = room([NC, SEQ]), room([2, SEQ])
        cw = room([NC, CONV_K + 1])
        s_cw = ctx.enter_context(nc.semaphore(f"conv_w_loaded_{len(param_sems)}"))
        param_sems[len(param_sems)] = s_cw
        p.wait("scalar", [p.latest("vector"), p.latest("tensor")])
        p.dma("scalar", cw, A["conv_wb_t"][l], s_cw)
        tok = V(lambda e: e.memset(g, 0.0))
        U0 = QW + 2 * KVW
        t_a = []
        for j in range(2):
            ps, done = project_cols(cols, w_in, U0 + j * CHUNK, 4, *after)
            t_a.append(copy_out(a[:, 2 * j:2 * j + 2, :], ps, done))
            bank_free[4] = (t_a[-1],)
            ps, done = project_cols(cols, w_in, U0 + CONV_W + j * CHUNK, 5, *after)
            tok = S(lambda e, ps=ps: e.activation(gt, ps, ACT.Sigmoid), done, p.latest("vector"))
            bank_free[5] = (tok,)
            tok = V(lambda e, j=j: e.tensor_tensor(g[:, 2 * j:2 * j + 2, PAD:PAD + SEQ], a[:, 2 * j:2 * j + 2, :],
                                                   gt, ALU.mult), tok, t_a[-1])
        for i in range(CONV_K):
            for c in range(NC):
                w, src = cw[:, c, i:i + 1], g[:, c, i:i + SEQ]
                if i == 0:
                    tok = V(lambda e, c=c, w=w, src=src: e.tensor_scalar(
                        y[:, c, :], src, w, cw[:, c, CONV_K:], ALU.mult, ALU.add), tok, (s_cw, 16))
                else:
                    tok = V(lambda e, c=c, w=w, src=src: e.scalar_tensor_tensor(
                        out=y[:, c, :], in0=src, scalar=w, in1=y[:, c, :], op0=ALU.mult, op1=ALU.add), tok)
        t_rows = []
        for t in range(NT):
            for c in range(NC):
                done = PE(lambda e, c=c, t=t: e.transpose(psum[6 + t][:, c * P:(c + 1) * P],
                                                          y[:, c, t * P:(t + 1) * P], ident[:]),
                          tok, *bank_free[6 + t])
            t_rows.append(copy_out(dst[:, t, :], psum[6 + t][:, :], done))
            bank_free[6 + t] = (t_rows[-1],)
        t_rows = [normalise(dst[:, t, :], dst[:, t, :], CONV_W, t_rows[t]) for t in range(NT)]
        t_rows = affine_rows(dst, A["ln_g_2"][l], A["ln_b_2"][l], t_rows)
        return S(lambda e: e.activation(dst, dst, ACT.Silu), *t_rows)

    def merge(l, o_attn, o_conv, rows, after):
        beta = room([KD])
        s_b = ctx.enter_context(nc.semaphore(f"beta_loaded_{len(param_sems)}"))
        param_sems[len(param_sems)] = s_b
        p.wait("scalar", [p.latest("vector"), p.latest("tensor")])
        p.dma("scalar", beta, A["beta_t"][l], s_b)
        scratch = room([QW])
        toks = []
        for src in (o_attn, o_conv):
            for t in range(NT):
                r, tok = rms_factor(src[:, t, :], QW, scratch, RMS_EPS, *after)
                toks.append(V(lambda e, src=src, t=t, r=r: e.tensor_scalar(src[:, t, :], src[:, t, :], r, None,
                                                                           ALU.mult), tok))

        def evac(k, ps, tok):
            if k // 2 % 2:
                return S(lambda e: e.activation(x_cols[:, k, :], ps, ACT.Copy, scale=beta[:, k:k + 1]), tok, (s_b, 16))
            return V(lambda e: e.tensor_scalar(x_cols[:, k, :], ps, beta[:, k:k + 1], None, ALU.mult), tok, (s_b, 16))

        t_cols = to_cols(x_cols, lambda k, t: (o_attn[:, t, k * P:(k + 1) * P] if k < QW // P else
                                               o_conv[:, t, (k * P - QW):(k * P - QW) + P]),
                         KD, (0, 1, 2, 3), *toks, evac=evac)
        part = room([NT, CHUNK])
        for j, c0 in enumerate(range(0, D, CHUNK)):
            b = 4 + j % 2
            ps, done = project_rows(x_cols, A["w_o_2"][l], c0, CHUNK, b, *t_cols)
            tok = V(lambda e, ps=ps, c0=c0: e.tensor_tensor(
                part, ps, bcast(gate_rows[:, 0:1, c0:c0 + CHUNK], [P, NT, CHUNK]), ALU.mult), done)
            bank_free[b] = (tok,)
            r = rows[:, :, c0:c0 + CHUNK]
            tok = V(lambda e, r=r: e.tensor_tensor(r, r, part, ALU.add), tok)
        return tok

    def attend(l, rows, stream, nk, t_gates, after):
        fresh()
        t_cols = modulated_cols(x_cols, rows, l, 0, stream, after)
        top[0] = 0
        p.stage()
        key_at = 0 if stream else SEQ
        q_cols, t_qkv = qkv(x_cols, l, True, not stream, key_at, t_cols)
        o_attn, o_conv = room([NT, QW]), room([NT, CONV_W])
        inv = room([8])
        bufs = attention_buffers()
        t_o = []
        for t in range(NT):
            def finish(h0, ps, sums, tok, t=t):
                tok = V(lambda e: e.reciprocal(inv, sums), tok)
                t_o.append(V(lambda e: e.tensor_tensor(o_attn[:, t, :].rearrange("p (h d) -> p h d", h=8), ps,
                                                       bcast(inv.unsqueeze(2), [P, 8, DH]), ALU.mult), tok))
                return (t_o[-1],)
            G4 = Q_HEADS // KV_HEADS
            attention(t, Q_HEADS, nk, lambda h, t=t: q_cols[(h % 2) * DH:(h % 2 + 1) * DH, h // 2, t * P:(t + 1) * P],
                      lambda h: key_cols[(h % 2) * DH:(h % 2 + 1) * DH, h // G4, 0:nk],
                      lambda h, j: val_rows[:, j, (h // G4) * DH:(h // G4 + 1) * DH],
                      DH ** -0.5, None, finish, bufs, *t_qkv)
        t_conv = conformer(x_cols, l, o_conv, t_cols)
        return merge(l, o_attn, o_conv, rows, [*t_o, t_conv, *t_gates])

    def peer(l, rows, stream, t_in):
        fresh()
        t_cols = modulated_cols(x_cols, rows, l, 3 * KD, stream, [t_in])
        top[0] = 0
        p.stage()
        HT = PEER_H * PEER_TOP
        slots = room([3, SEQ])
        kept = top[0]
        q = room([PEER_H, SEQ])
        keys = room([PEER_H, PEER_K])
        s_k = ctx.enter_context(nc.semaphore(f"peer_keys_loaded_{l}{stream}"))
        p.wait("scalar", [p.latest("vector"), p.latest("tensor")])
        p.dma("scalar", keys, A["peer_keys_t"][l], s_k)
        t_q = []
        for j in range(4):
            b = 4 + j % 2
            ps, done = project_cols(x_cols, A["peer_wq_2"][l], j * CHUNK, b, *t_cols)
            t_q.append(copy_out(q[:, 2 * j:2 * j + 2, :], ps, done))
            bank_free[b] = (t_q[-1],)
        NS = 2 * PEER_H
        score = room([NS, PEER_K])
        best2 = room([NS, PEER_TOP])
        key_u = room([NS, PEER_TOP], dt=U32)
        key_f = room([NS, PEER_TOP])
        cand = room([PEER_H, PEER_TOP, PEER_TOP])
        pick = room([HT, PEER_TOP])
        best, place_u = room([PEER_H, PEER_TOP]), room([PEER_H, PEER_TOP], dt=U32)
        row_u, col_u = room([HT], dt=U32), room([HT], dt=U32)
        row_f, col_f = room([HT]), room([HT])
        chosen = room([2, HT])
        wsum = room([PEER_H])

        def top16(values, best, index, after):
            n = len(values)
            for i in range(n):
                after = V(lambda e, i=i: e.max(best(i)[:, 0:8], values[i]), after)
            for i in range(n):
                after = V(lambda e, i=i: e.max_index(index(i)[:, 0:8], best(i)[:, 0:8], values[i]), after)
            for i in range(n):
                after = V(lambda e, i=i: e.match_replace(values[i], best(i)[:, 0:8], values[i], LOWEST), after)
            for i in range(n):
                after = V(lambda e, i=i: e.max(best(i)[:, 8:16], values[i]), after)
            for i in range(n):
                after = V(lambda e, i=i: e.max_index(index(i)[:, 8:16], best(i)[:, 8:16], values[i]), after)
            return after

        t_slots = []
        for t in range(NT):
            ts = slice(t * P, (t + 1) * P)
            for b in range(4):
                c, h0 = b % 2, b // 2 * 4
                half = c * DH
                for h in range(h0, h0 + 4):
                    done = PE(lambda e: e.matmul(
                        psum[b][:, (h - h0) * P:(h - h0 + 1) * P], q[half:half + DH, h, ts],
                        keys[half:half + DH, h, :], start=True, stop=True), *t_q, (s_k, 16), *bank_free[b])
                tok = copy_out(score[:, 2 * h0 + c:2 * h0 + c + 7:2, :],
                               psum[b][:, :].rearrange("p (i k) -> p i k", k=PEER_K), done, p.latest("vector"))
                bank_free[b] = (tok,)
            tok = top16([score[:, i, :] for i in range(NS)], lambda i: best2[:, i, :], lambda i: key_u[:, i, :],
                        p.latest("scalar"))
            tok = V(lambda e: e.tensor_copy(key_f, key_u), tok)
            for h in range(PEER_H):
                shape = [P, PEER_TOP, PEER_TOP]
                tok = V(lambda e, h=h, shape=shape: e.tensor_tensor(
                    cand[:, h], bcast(best2[:, 2 * h, :].unsqueeze(2), shape),
                    bcast(best2[:, 2 * h + 1, :].unsqueeze(1), shape), ALU.add), tok)
            tok = top16([cand[:, h].rearrange("p a b -> p (a b)") for h in range(PEER_H)],
                        lambda h: best[:, h, :], lambda h: place_u[:, h, :], tok)
            w3 = best
            tok = V(lambda e: e.tensor_copy(wsum, best[:, :, 0]), tok)
            tok = V(lambda e: e.tensor_tensor(w3, w3, bcast(wsum.unsqueeze(2), [P, PEER_H, PEER_TOP]),
                                              ALU.subtract), tok)
            tok = S(lambda e: e.activation(w3, w3, ACT.Exp), tok)
            tok = V(lambda e: e.tensor_reduce(wsum, w3, AX_X, ALU.add), tok)
            tok = V(lambda e: e.reciprocal(wsum, wsum), tok)
            tok = V(lambda e: e.tensor_tensor(w3, w3, bcast(wsum.unsqueeze(2), [P, PEER_H, PEER_TOP]),
                                              ALU.mult), tok)
            flat_u = place_u.rearrange("p h k -> p (h k)")
            tok = V(lambda e: e.tensor_scalar(row_u, flat_u, 4, None, ALU.logical_shift_right), tok)
            tok = V(lambda e: e.tensor_scalar(col_u, flat_u, 15, None, ALU.bitwise_and), tok)
            tok = V(lambda e: e.tensor_copy(row_f, row_u), tok)
            tok = V(lambda e: e.tensor_copy(col_f, col_u), tok)
            for c, at in enumerate((row_f, col_f)):
                tok = V(lambda e, at=at: e.tensor_tensor(
                    pick, bcast(iota[:, 0:PEER_TOP].unsqueeze(1), [P, HT, PEER_TOP]),
                    bcast(at.unsqueeze(2), [P, HT, PEER_TOP]), ALU.is_equal), tok)
                for h in range(PEER_H):
                    ph = pick[:, h * PEER_TOP:(h + 1) * PEER_TOP, :]
                    tok = V(lambda e, ph=ph, i=2 * h + c: e.tensor_tensor(
                        ph, ph, bcast(key_f[:, i, :].unsqueeze(1), [P, PEER_TOP, PEER_TOP]), ALU.mult), tok)
                tok = V(lambda e, c=c: e.tensor_reduce(chosen[:, c, :], pick, AX_X, ALU.add), tok)
            for i, src in enumerate((chosen[:, 0, :], chosen[:, 1, :], w3.rearrange("p h k -> p (h k)"))):
                done = PE(lambda e, i=i, src=src: e.transpose(psum[6][:, i * P:(i + 1) * P], src, ident[:]),
                          tok, *bank_free[6])
            tok = copy_out(slots[:, :, ts], psum[6][:, 0:3 * P].rearrange("p (i t) -> p i t", i=3), done)
            bank_free[6] = (tok,)
            t_slots.append(tok)

        p.stage()
        top[0] = kept
        NQ = 4
        KQ = PEER_K // NQ
        TB = 8
        dense = [room([SEQ, KQ]) for _ in range(2)]
        hot2 = [room([TB, PEER_K]) for _ in range(2)]
        hot1 = [room([TB, KQ]) for _ in range(2)]
        act = [room([SEQ]) for _ in range(2)]
        scaled = [room([SEQ]) for _ in range(3)]
        dense_tok = {}
        built = [0]
        hot_free = [(), ()]
        scaled_free = {}
        read_dense = {}

        def build_batch(qt, j):
            i = built[0] % 2
            built[0] += 1
            t0 = j * TB
            key1, key2, w = (slots[:, c, t0:t0 + TB].unsqueeze(2) for c in range(3))
            s2, s1 = [P, TB, PEER_K], [P, TB, KQ]
            ta = V(lambda e: e.tensor_tensor(hot2[i], bcast(iota[:].unsqueeze(1), s2), bcast(key2, s2),
                                             ALU.is_equal), *t_slots, *hot_free[i])
            tb = V(lambda e: e.tensor_tensor(hot1[i], bcast(iota[:, qt * KQ:(qt + 1) * KQ].unsqueeze(1), s1),
                                             bcast(key1, s1), ALU.is_equal), ta)
            tb = V(lambda e: e.tensor_tensor(hot1[i], hot1[i], bcast(w, s1), ALU.mult), tb)
            b = 2 + i
            for m in range(TB):
                f = lambda e, m=m: e.matmul(psum[b][:, m * KQ:(m + 1) * KQ], hot2[i][:, m, :], hot1[i][:, m, :],
                                            start=True, stop=True)
                if m < TB - 1:
                    p.quiet("tensor", f, tb, *bank_free[b])
                else:
                    done = PE(f, tb)
            hot_free[i] = (done,)
            tok = S(lambda e: e.activation(dense[qt % 2][:, t0:t0 + TB, :],
                                           psum[b][:, 0:TB * KQ].rearrange("p (t k) -> p t k", t=TB), ACT.Copy),
                    done, *read_dense.get(qt - 2, ()))
            bank_free[b] = (tok,)
            dense_tok[qt] = tok

        NB_ = SEQ // TB
        for j in range(NB_):
            build_batch(0, j)

        slot_u, slot_v = {}, {}
        scaled_tok = {}

        def hidden(i1):
            pair, odd = divmod(i1, 2)
            if not odd:
                slot_u[pair] = weights.load((A["peer_u_t"][l, pair], lambda b: b[:, :]))
                slot_v[pair] = weights.load((A["peer_v_2"][l, pair * 2 * P:(pair + 1) * 2 * P, :]
                                             .rearrange("(a p) d -> p a d", p=P),
                                             lambda b: b[:, :].rearrange("p (a d) -> p a d", a=2)))
            s, buf, tw = slot_u[pair]
            ut = buf[:, odd * D:(odd + 1) * D].rearrange("p (k e) -> p k e", k=KD)
            b = odd
            done = product(psum[b][:, 0:SEQ], [(ut[:, k, :], x_cols[:, k, :]) for k in range(KD)],
                           tw, *t_cols, *bank_free[b])
            if odd:
                weights.release(s, done)
            tok = S(lambda e: e.activation(act[odd], psum[b][:, 0:SEQ], ACT.Gelu), done, scaled_tok.get(i1 - 2, p.latest("vector")))
            bank_free[b] = (tok,)
            qt, kk = divmod(i1, KQ)
            tok = V(lambda e: e.tensor_tensor(scaled[i1 % 3], act[odd], dense[qt % 2][:, :, kk], ALU.mult),
                    tok, dense_tok[qt], *scaled_free.get(i1 - 3, ()))
            scaled_tok[i1] = tok
            read_dense[qt] = (tok,)

        def outputs(i1):
            pair, odd = divmod(i1, 2)
            s, buf, tw = slot_v[pair]
            for t in range(NT):
                for h in range(2):
                    b = 4 + 2 * t + h
                    w0 = (scaled_tok[i1], tw) + (tuple(bank_free[b]) if i1 == 0 else ())
                    f = lambda e, t=t, h=h, b=b: e.matmul(
                        psum[b][:, :], scaled[i1 % 3][:, t * P:(t + 1) * P],
                        buf[:, odd * D + h * 512:odd * D + (h + 1) * 512],
                        start=(i1 == 0), stop=(i1 == PEER_K - 1))
                    done = PE(f, *w0)
            if odd:
                weights.release(s, done)
            scaled_free[i1] = (done,)
            return done

        for i1 in range(PEER_K + 1):
            if i1 < PEER_K:
                hidden(i1)
                qt, kk = divmod(i1, KQ)
                if qt + 1 < NQ:
                    build_batch(qt + 1, kk)
            if i1 >= 1:
                done = outputs(i1 - 1)
        part = room([512])
        for t in range(NT):
            for h in range(2):
                b = 4 + 2 * t + h
                hs = slice(h * 512, (h + 1) * 512)
                tok = V(lambda e, b=b, hs=hs: e.tensor_tensor(part, psum[b][:, :], gate_rows[:, 1, hs], ALU.mult),
                        done)
                bank_free[b] = (tok,)
                tok = V(lambda e, t=t, hs=hs: e.tensor_tensor(rows[:, t, hs], rows[:, t, hs], part, ALU.add), tok)
        return tok

    def second(t_in):
        fresh()
        t_mod = modulation()
        fresh()
        t_gates = spread_gates(0, 1, t_mod)
        t_c = attend(0, ctx_rows, 1, SEQ, t_gates, [t_ctx, t_mod])
        t_c = peer(0, ctx_rows, 1, t_c)
        t_x = p.latest("vector")
        for l in range(DEPTH):
            fresh()
            if l == 1:
                t_cc = modulated_cols(x_cols, ctx_rows, l, 0, 1, [t_c])
                top[0] = 0
                p.stage()
                qkv(x_cols, l, False, False, 0, t_cc)
                fresh()
            t_gates = spread_gates(l, 0, t_mod)
            t_x = attend(l, x_rows, 0, 2 * SEQ, t_gates, [t_x])
            t_x = peer(l, x_rows, 0, t_x)
        fresh()
        scratch = room([D])
        sv, fg, t_fg = vector_row(A["final_g_2"])
        toks = []
        for t in range(NT):
            r, tok = rms_factor(x_rows[:, t, :], D, scratch, RMS_EPS, t_x)
            toks.append(V(lambda e, t=t, r=r: e.scalar_tensor_tensor(
                out=x_rows[:, t, :], in0=x_rows[:, t, :], scalar=r, in1=fg[:, :], op0=ALU.mult, op1=ALU.mult),
                tok, t_fg))
        store(x_rows[:], *toks)

    t_in = mixer_0()
    t_in = moe(0, t_in)
    t_in = mixer_1(t_in)
    t_in = moe(1, t_in)
    second(t_in)


def host_layout(inputs):
    a = {n: np.asarray(v) for n, v in inputs.items()}

    def tiles(v):
        return v.reshape(NT, P, -1).transpose(1, 0, 2)

    d = {n: a[n] for n in (
        "ab_w_in", "ab_gm_ln_g", "ab_gm_ln_b", "ab_mla_q_norm", "ab_mla_kv_norm", "ab_mla_w_uq",
        "ab_mla_w_uk", "ab_mla_w_uv", "ab_w_o", "moe_w_down", "ln1_g", "ln1_b", "ln2_g", "ln2_b")}
    d["x"], d["ctx_2"] = tiles(a["x"]), tiles(a["ctx_2"])
    d["positions"] = a["positions"].reshape(NT, P).T
    d["gm_ws_t"] = a["ab_gm_ws"][0].transpose(0, 2, 1)
    d["gm_bs_t"] = a["ab_gm_bs"][0].T
    d["router_w"] = np.concatenate([a["moe_w_rg"], a["moe_w_re"]], axis=-1)
    d["router_b"] = np.concatenate([a["moe_b_rg"], a["moe_b_re"]], axis=-1)
    for new, old in (("moe_gate", "moe_w_gate"), ("moe_up", "moe_w_up")):
        w = a[old].reshape(DEPTH, N_EXP, KD, P, MOE_HID)
        d[new] = w.transpose(0, 1, 3, 2, 4).reshape(DEPTH, N_EXP, P, KD * MOE_HID)

    d["c_ident"] = np.eye(P, dtype=np.float32)
    d["c_iota"] = np.tile(np.arange(P, dtype=np.float32), (P, 1))
    d["c_upper"] = np.triu(np.ones((P, P), np.float32))
    q = np.arange(SEQ)
    d["c_causal"] = tiles(np.where(q[:, None] >= q[None, :], 0.0, NEG).astype(np.float32))
    half = ROPE // 2
    f = np.exp(np.float32(-math.log(10000.0)) * np.arange(half, dtype=np.float32) / np.float32(half))
    d["c_freq"] = np.tile(f.astype(np.float32), (P, 1))
    for n in ("c_w_in", "c_w_ck1", "c_w_ck2", "c_w_cv1", "c_w_cv2", "c_gate_b", "c_w_o", "w_mod_2", "w_in_2",
              "q_gain_2", "k_gain_2", "ln_g_2", "ln_b_2", "w_o_2", "peer_wq_2", "peer_v_2", "final_g_2"):
        d[n] = a[n]
    d["cmp_pos_t"] = a["c_cmp_pos"][0].transpose(2, 0, 1)
    end = np.arange(N_CMP) * CMP_STRIDE + CMP_LEN - 1
    ended = q[:, None] >= end[None, :]
    none = np.broadcast_to(~ended.any(1, keepdims=True), ended.shape)
    d["c_cmp_mask"] = np.stack([tiles(m.astype(np.float32)) for m in (np.where(ended, 0.0, NEG), ended, none)], 2)
    cond = np.stack([a["c_2"][0], a["c_ctx_2"]], -1)
    d["cond"] = cond.reshape(KD, P, 2).transpose(1, 0, 2)
    d["b_mod_t"] = a["b_mod_2"].reshape(DEPTH, 6 * KD, P).transpose(2, 0, 1)
    n4 = DH // 4
    inv = (np.float32(10000.0) ** (-np.arange(n4, dtype=np.float32) / np.float32(n4))).astype(np.float32)
    row, col = (np.repeat(np.arange(SEQ // 64), 64), np.tile(np.arange(64), SEQ // 64))
    ang = np.concatenate([row[:, None].astype(np.float32) * inv, col[:, None].astype(np.float32) * inv], -1)
    d["c_rope_cos"] = tiles(np.cos(ang).astype(np.float32))
    d["c_rope_sin"] = tiles(np.sin(ang).astype(np.float32))
    wb = np.concatenate([a["conv_w_2"], a["conv_b_2"][:, None, :]], 1)
    d["conv_wb_t"] = wb.reshape(DEPTH, CONV_K + 1, CONV_W // P, P).transpose(0, 3, 2, 1)
    beta = np.concatenate([a["beta_attn_2"], a["beta_conv_2"]], -1)
    d["beta_t"] = beta.reshape(DEPTH, KD, P).transpose(0, 2, 1)
    pk = a["peer_keys_2"]
    d["peer_keys_t"] = pk.transpose(0, 2, 4, 1, 3).reshape(DEPTH, P, PEER_H, PEER_K)
    u = a["peer_u_2"].reshape(DEPTH, PEER_K // 2, 2, P, KD, P)
    d["peer_u_t"] = u.transpose(0, 1, 5, 2, 4, 3).reshape(DEPTH, PEER_K // 2, P, 2 * D)
    return {n: np.ascontiguousarray(v) for n, v in d.items()}


def kernel(**inputs):
    import concourse.bacc as bacc
    from concourse.bass_utils import run_bass_kernel_spmd

    nc = bacc.Bacc("TRN2", target_bir_lowering=False, num_devices=1)
    arrays, aps = {}, {}
    for name, a in host_layout(inputs).items():
        arrays[f"in_{name}"] = a
        aps[name] = nc.dram_tensor(f"in_{name}", a.shape, mybir.dt.from_np(a.dtype), kind="ExternalInput").ap()
    out = nc.dram_tensor("out_0_dram", (1, SEQ, D), F32, kind="ExternalOutput").ap()
    build(nc, aps, out)
    r = run_bass_kernel_spmd(nc, [arrays], core_ids=[0])
    return r.results[0]["out_0_dram"]
```

```python
import math
from contextlib import ExitStack

import numpy as np

import concourse.bass as bass
from concourse import mybir

F32 = mybir.dt.float32
F32R = mybir.dt.float32r
BF16 = mybir.dt.bfloat16
U32 = mybir.dt.uint32
I32 = mybir.dt.int32
ALU = mybir.AluOpType
ACT = mybir.ActivationFunctionType
AX_X = mybir.AxisListType.X

P = 128
SEQ = 256
NT = SEQ // P
D = 1024
KD = D // P
CHUNK = 256
BANK = 512
UNIT = 1024
LOWEST = -3.0e38
NEG = -1e30
LN_EPS = 1e-5
RMS_EPS = 1e-6
DEPTH = 2
ALPHA = (2.0 * DEPTH) ** 0.25

GM_W, GM_G = 512, 4
Q_RANK, KV_RANK, ROPE = 256, 128, 32
MLA_H, NOPE, MLA_V = 8, 64, 64
MLA_D = NOPE + ROPE
NSA_H, NSA_G, DH = 16, 2, 64
CMP_LEN, CMP_STRIDE, CMP_HID = 32, 16, 256
N_CMP = SEQ // CMP_STRIDE - CMP_LEN // CMP_STRIDE + 1
MOE_G, MOE_E, MOE_HID = 4, 8, 256
N_EXP = MOE_G * MOE_E

Q_HEADS, KV_HEADS = 8, 2
QW, KVW, CONV_W, CONV_K = 512, 128, 512, 31
PEER_H, PEER_K, PEER_TOP = 8, 128, 16


class Program:

    def __init__(self, nc, ctx):
        self.nc, self.ctx = nc, ctx
        self.engine = {"tensor": nc.tensor, "vector": nc.vector, "scalar": nc.scalar,
                       "gpsimd": nc.gpsimd, "sync": nc.sync}
        self.done = {e: ctx.enter_context(nc.semaphore(f"{e}_done")) for e in self.engine}
        self.count = {e: 0 for e in self.engine}
        self.passed = {e: {} for e in self.engine}

    def wait(self, engine, tokens):
        for sem, value in tokens:
            if value > self.passed[engine].get(sem.name, 0):
                self.passed[engine][sem.name] = value
                self.engine[engine].wait_ge(sem, value)

    def op(self, engine, issue, *after):
        if engine != "tensor" and self.count[engine]:
            after += ((self.done[engine], self.count[engine]),)
        self.wait(engine, after)
        self.count[engine] += 1
        issue(self.engine[engine]).then_inc(self.done[engine], 1)
        return (self.done[engine], self.count[engine])

    def quiet(self, engine, issue, *after):
        self.wait(engine, after)
        issue(self.engine[engine])

    def dma(self, queue, dst, src, sem):
        self.engine[queue].dma_start(dst, src).then_inc(sem, 16)

    def latest(self, engine):
        return (self.done[engine], self.count[engine])

    def stage(self):
        tokens = [t for t in map(self.latest, ("tensor", "vector", "scalar", "gpsimd")) if t[1]]
        for e in ("tensor", "vector", "scalar", "gpsimd"):
            self.wait(e, tokens)


class Ring:

    def __init__(self, prog, name, queue, slots, width):
        self.prog, self.queue, self.n = prog, queue, slots
        self.buf = [prog.ctx.enter_context(prog.nc.sbuf_tensor(f"{name}{i}", [P, width], F32))
                    for i in range(slots)]
        self.sem = [prog.ctx.enter_context(prog.nc.semaphore(f"{name}_filled{i}"))
                    for i in range(slots)]
        self.fills = [0] * slots
        self.free = [()] * slots
        self.at = 0

    def load(self, *moves):
        s = self.at % self.n
        self.at += 1
        assert self.free[s] is not None, "the slot is in use"
        self.prog.wait(self.queue, self.free[s])
        self.free[s] = None
        for source, place in moves:
            self.fills[s] += 16
            self.prog.dma(self.queue, place(self.buf[s]), source, self.sem[s])
        return s, self.buf[s], (self.sem[s], self.fills[s])

    def release(self, s, *tokens):
        self.free[s] = tokens


def build(nc, A, out):
    with ExitStack() as ctx:
        _build(nc, ctx, A, out)


def _build(nc, ctx, A, out):
    p = Program(nc, ctx)

    def sb(name, shape, dt=F32):
        return ctx.enter_context(nc.sbuf_tensor(name, shape, dt))

    def PE(f, *after):
        return p.op("tensor", f, *after)

    def V(f, *after):
        return p.op("vector", f, *after)

    def S(f, *after):
        return p.op("scalar", f, *after)

    def G(f, *after):
        return p.op("gpsimd", f, *after)

    psum = [ctx.enter_context(nc.psum_tensor(f"bank{i}", [P, BANK], F32)) for i in range(8)]
    bank_free = [() for _ in range(8)]

    weights = Ring(p, "weight", "sync", 5, UNIT)
    vectors = Ring(p, "vector_param", "gpsimd", 2, D)

    def pair(name, shape):
        return sb(name + "_hi", shape, F32R)[:], sb(name + "_lo", shape, F32R)[:]

    SPLITS = 5
    splits = [pair(f"split{i}", [P, UNIT]) for i in range(SPLITS)]
    split_free = [() for _ in range(SPLITS)]
    split_at = [0]

    x_rows = sb("x_rows", [P, NT, D])
    ctx_rows = sb("ctx_rows", [P, NT, D])
    x_cols = pair("x_cols", [P, KD, SEQ])
    hidden_parts = [pair(f"hidden{i}", [P, 2, SEQ]) for i in range(2)]
    ident = sb("ident", [P, P])
    ones = sb("ones", [P, P])
    iota = sb("iota", [P, P])
    causal = sb("causal", [P, NT, SEQ])
    ARENA = 21376
    arena = sb("arena", [P, ARENA])
    top = [0]

    def fresh():
        p.stage()
        top[0] = 0

    def room(shape, parts=P, dt=F32):
        n = int(np.prod(shape))
        a = arena[0:parts, top[0]:top[0] + n]
        top[0] += n
        assert top[0] <= ARENA, top[0]
        if dt is BF16:
            a = a[:, 0:n // 2]
            top[0] -= n // 2
        if dt is not F32:
            a = a.bitcast(dt)
        if len(shape) == 2:
            a = a.rearrange("p (a b) -> p a b", a=shape[0])
        elif len(shape) == 3:
            a = a.rearrange("p (a b c) -> p a b c", a=shape[0], b=shape[1])
        elif len(shape) == 4:
            a = a.rearrange("p (a b c d) -> p a b c d", a=shape[0], b=shape[1], c=shape[2])
        return a

    def constant(name, tile):
        s = ctx.enter_context(nc.semaphore(f"{name}_loaded"))
        p.dma("scalar", tile, A[name], s)
        return (s, 16)

    t_ident = constant("c_ident", ident[:])
    t_iota = constant("c_iota", iota[:])
    t_causal = constant("c_causal", causal[:])
    t_ones = V(lambda e: e.memset(ones[:], 1.0))
    t_x = constant("x", x_rows[:])
    t_ctx = constant("ctx_2", ctx_rows[:])

    def bcast(ap, shape):
        return ap.broadcast_to(shape)

    def product(bank_ap, pairs, *after):
        for i, (lhsT, rhs, *tok) in enumerate(pairs):
            last = i == len(pairs) - 1
            f = lambda e, l=lhsT, r=rhs, a=(i == 0), z=last: e.matmul(bank_ap, l, r, start=a, stop=z)
            if last:
                return PE(f, *after, *tok)
            p.quiet("tensor", f, *after, *tok)

    def product3(bank_ap, pairs, *after):
        return product(bank_ap, [x for (l, r, *tok) in pairs for x in
                                 ((l[0], r[0], *tok), (l[0], r[1]), (l[1], r[0]))], *after)

    def at(parts, *index):
        return parts[0][index], parts[1][index]

    def split(parts, src, *after, engine=V):
        tok = S(lambda e: e.activation(parts[0], src, ACT.Copy), *after)
        return engine(lambda e: e.tensor_tensor(parts[1], src, parts[0].bitcast(F32), ALU.subtract), tok)

    announced, landed, ready = [], [], []

    def announce(*units):
        announced.extend(units)

    def shaped(buf, shape):
        n = int(np.prod(shape))
        return buf[:, 0:n] if len(shape) == 1 else buf[:, 0:n].rearrange("p (a b) -> p a b", a=shape[0])

    def feed():
        moved = True
        while moved:
            moved = False
            if announced and weights.free[weights.at % weights.n] is not None:
                source, shape = announced.pop(0)
                landed.append((shape, weights.load((source, lambda b: shaped(b, shape)))))
                moved = True
            i = split_at[0] % SPLITS
            if landed and split_free[i] is not None:
                shape, (s, buf, tok) = landed.pop(0)
                parts = shaped(splits[i][0], shape), shaped(splits[i][1], shape)
                tok = split(parts, shaped(buf, shape), tok, *split_free[i])
                weights.release(s, tok)
                split_free[i] = None
                split_at[0] += 1
                ready.append((parts, i, tok))
                moved = True

    def take(shape):
        feed()
        unit = ready.pop(0)
        assert list(unit[0][0].shape[1:]) == list(shape), (unit[0][0].shape, shape)
        return unit

    evac_turn = [0]

    def copy_out(dst, src, *after):
        evac_turn[0] += 1
        if evac_turn[0] % 2:
            return S(lambda e: e.activation(dst, src, ACT.Copy), *after)
        return V(lambda e: e.tensor_copy(dst, src), *after)

    def to_cols(dst, rows, n, banks, *after, evac=None):
        tokens = []
        for j, k0 in enumerate(range(0, n, 2)):
            b = banks[j % len(banks)]
            ks = range(k0, min(k0 + 2, n))
            for k in ks:
                for t in range(NT):
                    o = psum[b][:, (k - k0) * SEQ + t * P:(k - k0) * SEQ + (t + 1) * P]
                    tok = PE(lambda e, o=o, i=rows(k, t): e.transpose(o, i, ident[:]),
                             *after, t_ident, *bank_free[b])
            src = psum[b][:, 0:len(ks) * SEQ].rearrange("p (k t) -> p k t", t=SEQ)
            if evac is not None:
                done = [evac(k0, src, tok)]
            elif isinstance(dst, tuple):
                done = [split(at(dst, slice(None), slice(k0, k0 + len(ks))), src, tok)]
            else:
                done = [copy_out(dst[:, k0:k0 + len(ks), :], src, tok)]
            bank_free[b] = tuple(done)
            tokens += done
        return tokens

    HK = KD // 2

    def announce_chunks(w, *chunks):
        for c0, cn in chunks:
            announce(*[(w[i * HK * P:(i + 1) * HK * P, c0:c0 + cn].rearrange("(k p) n -> p k n", p=P), (HK, cn))
                       for i in range(2)])

    def take_chunk(cn):
        units = [take((HK, cn)) for _ in range(2)]
        return (lambda k, cols: at(units[k // HK][0], slice(None), k % HK, cols),
                [u[1] for u in units], [u[2] for u in units])

    def release_splits(numbers, *tokens):
        for i in numbers:
            split_free[i] = tokens

    def project_rows(cols, cn, bank, *after):
        wt, numbers, tok = take_chunk(cn)
        for t in range(NT):
            o = psum[bank][:, t * CHUNK:t * CHUNK + cn]
            done = product3(o, [(at(cols, slice(None), k, slice(t * P, (t + 1) * P)), wt(k, slice(0, cn)))
                                for k in range(KD)], *after, *tok, *bank_free[bank])
        release_splits(numbers, done)
        return psum[bank][:].rearrange("p (t n) -> p t n", t=NT)[:, :, 0:cn], done

    def project_cols(cols, bank, *after):
        wt, numbers, tok = take_chunk(CHUNK)
        for j in range(2):
            o = psum[bank][:, j * SEQ:(j + 1) * SEQ]
            done = product3(o, [(wt(k, slice(j * P, (j + 1) * P)), at(cols, slice(None), k)) for k in range(KD)],
                            *after, *tok, *bank_free[bank])
        release_splits(numbers, done)
        return psum[bank][:].rearrange("p (j t) -> p j t", j=2), done

    def vector_row(*sources):
        at, moves = 0, []
        for v in sources:
            n = v.shape[0]
            moves.append((v.partition_broadcast(P), lambda b, a=at, n=n: b[:, a:a + n]))
            at += n
        return vectors.load(*moves)

    small = sb("small", [P, 128])
    small_at = [0]

    def tiny(n):
        if small_at[0] + n > 128:
            small_at[0] = 0
        a = small[:, small_at[0]:small_at[0] + n]
        small_at[0] += n
        return a

    def inv_root(dst, src, eps, *after):
        tok = V(lambda e: e.tensor_scalar(dst, src, eps, None, ALU.add), *after)
        tok = S(lambda e: e.activation(dst, dst, ACT.Sqrt), tok)
        return V(lambda e: e.reciprocal(dst, dst), tok)

    def normalise(dst, src, width, *after):
        n = -(-width // 512)
        w = width // n
        stats, mv, rstd = tiny(6 * n), tiny(2), tiny(1)
        for i in range(n):
            tok = V(lambda e, i=i: e.bn_stats(stats[:, 6 * i:6 * i + 6], src[:, w * i:w * (i + 1)]),
                    *after)
        tok = V(lambda e: e.bn_aggr(mv, stats), tok)
        tok = inv_root(rstd, mv[:, 1:2], LN_EPS, tok)
        return V(lambda e: e.tensor_scalar(dst, src, mv[:, 0:1], rstd, ALU.subtract, ALU.mult), tok)

    def rms_factor(src, width, scratch, eps, *after):
        ms, r = tiny(1), tiny(1)
        tok = V(lambda e: e.tensor_tensor_reduce(scratch, src, src, 1.0 / width, 0.0, ALU.mult,
                                                 ALU.add, ms), *after)
        return r, inv_root(r, ms, eps, tok)

    def affine_rows(rows, g, b, scratch_tok):
        sg, bg, tg = vector_row(g)
        sb_, bb, tb = vector_row(b)
        toks = []
        for t in range(NT):
            a = V(lambda e, t=t: e.tensor_tensor(rows[:, t, :], rows[:, t, :], bg[:, 0:g.shape[0]], ALU.mult),
                  scratch_tok[t], tg)
            toks.append(V(lambda e, t=t: e.tensor_tensor(rows[:, t, :], rows[:, t, :], bb[:, 0:g.shape[0]],
                                                         ALU.add), a, tb))
        vectors.release(sg, toks[-1])
        vectors.release(sb_, toks[-1])
        return toks

    def post_norm(g, b, residual_toks):
        toks = [normalise(x_rows[:, t, :], x_rows[:, t, :], D, residual_toks[t]) for t in range(NT)]
        return affine_rows(x_rows, g, b, toks)

    def add_scaled_residual(c0, cn, ps, done):
        return [V(lambda e, t=t: e.scalar_tensor_tensor(
            out=x_rows[:, t, c0:c0 + cn], in0=x_rows[:, t, c0:c0 + cn], scalar=ALPHA,
            in1=ps[:, t, :], op0=ALU.mult, op1=ALU.add), done) for t in range(NT)]

    def attention(tile, heads, nk, q_of, k_of, v_of, scale, mask, finish, bufs, *after):
        masked, prob, prob_t, neg_max, sums = bufs
        hg = BANK // nk
        kt = nk // P
        n = heads // hg
        order = [h0 + h for h0 in range(0, heads, 8) for h in (0, 2, 4, 6, 1, 3, 5, 7)]
        exp_tok, t_tok, mm_tok = {}, {}, {}
        pt_free, prob_free = {}, {}
        out_free = [(), ()]

        def scores(g):
            b = g % 2
            for i in range(hg):
                tok = PE(lambda e, i=i: e.matmul(psum[b][:, i * nk:(i + 1) * nk], q_of(order[g * hg + i]),
                                                 k_of(order[g * hg + i]), start=True, stop=True),
                         *after, *bank_free[b])
            s3 = psum[b][:].rearrange("p (h k) -> p h k", h=hg)
            h0 = order[g * hg]
            nm = neg_max[:, h0:h0 + 2 * hg - 1:2]
            if mask is not None:
                m3 = masked[b].rearrange("p (h k) -> p h k", h=hg)
                tok = V(lambda e: e.scalar_tensor_tensor(
                    out=m3, in0=s3, scalar=scale, in1=bcast(mask.unsqueeze(1), [P, hg, nk]),
                    op0=ALU.mult, op1=ALU.add), tok, t_causal, *exp_tok.get(g - 2, ()))
                bank_free[b] = (tok,)
                tok = V(lambda e: e.tensor_reduce(nm, m3, AX_X, ALU.max, negate=True), tok)
                src, sc = m3, 1.0
            else:
                tok = V(lambda e: e.tensor_reduce(nm, s3, AX_X, ALU.max, negate=True), tok)
                tok = V(lambda e: e.tensor_scalar(nm, nm, scale, None, ALU.mult), tok)
                src, sc = s3, scale
            pr = prob[g % 3].rearrange("p (h k) -> p h k", h=hg)
            for i in range(hg):
                h = h0 + 2 * i
                tok2 = S(lambda e: e.activation(pr[:, i, :], src[:, i, :], ACT.Exp, bias=neg_max[:, h:h + 1],
                                                scale=sc, accum_out=sums[:, h:h + 1]),
                         tok, *prob_free.get(g - 3, ()))
            if mask is None:
                bank_free[b] = (tok2,)
            exp_tok[g] = (tok2,)

        def flips(g):
            b = 2 + g % 2
            for i in range(4):
                tok = PE(lambda e, i=i: e.transpose(psum[b][:, i * P:(i + 1) * P],
                                                    prob[g % 3][:, i * P:(i + 1) * P], ident[:]),
                         *exp_tok[g], *bank_free[b])
            prob_free[g] = (tok,)
            tok = copy_out(prob_t[g % 3], psum[b][:], tok, *pt_free.get(g - 3, ()))
            bank_free[b] = (tok,)
            t_tok[g] = tok

        def values(g):
            for i in range(hg):
                h = order[g * hg + i]
                b = 4 + (h // 8) % 2
                o = psum[b][:, (h % 8) * DH:(h % 8 + 1) * DH]
                tok = product(o, [(prob_t[g % 3][:, (i * kt + j) * P:(i * kt + j + 1) * P], v_of(h, j))
                                  for j in range(kt)], t_tok[g], *bank_free[b])
                if (g * hg + i) % 8 == 7:
                    h -= h % 8
                    bank_free[b] = finish(h, psum[b][:].rearrange("p (h d) -> p h d", h=8),
                                          sums[:, h:h + 8], tok)
            pt_free[g] = (tok,)

        for g in range(n + 2):
            if g < n:
                scores(g)
            if 1 <= g <= n:
                flips(g - 1)
            if g >= 2:
                values(g - 2)

    def attention_buffers():
        return ([room([BANK]) for _ in range(2)], [room([BANK]) for _ in range(3)],
                [room([BANK]) for _ in range(3)], room([NSA_H]), room([NSA_H]))

    def mixer_0():
        fresh()
        w_in = A["ab_w_in"][0]
        t_cols = to_cols(x_cols, lambda k, t: x_rows[:, t, k * P:(k + 1) * P], KD, (0, 1, 2, 3), t_x)
        u, v = room([NT, GM_W]), room([NT, GM_W])
        cq, ckv = room([NT, Q_RANK]), room([NT, KV_RANK + ROPE])
        mix = room([NT, D])
        toks = {}
        parts_of_h = [(1024, 256, cq, 0), (1280, 160, ckv, 0), (512, 256, v, 0), (768, 256, v, 256),
                      (0, 256, u, 0), (256, 256, u, 256)]
        announce_chunks(w_in, *[(c0, cn) for c0, cn, _, _ in parts_of_h])
        for j, (_, cn, dst, first) in enumerate(parts_of_h):
            b = 4 + j % 2
            ps, done = project_rows(x_cols, cn, b, *t_cols)
            d = dst[:, :, first:first + cn]
            if dst is u or dst is v:
                tok = S(lambda e, d=d, ps=ps: e.activation(d, ps, ACT.Gelu_apprx_tanh), done)
            else:
                tok = V(lambda e, d=d, ps=ps: e.tensor_copy(d, ps), done)
            bank_free[b] = (tok,)
            toks[j] = tok

        half = ROPE // 2
        pos_i, pos = room([NT], dt=I32), room([NT])
        freq = room([half])
        ang, turns, cos, sin = (room([NT, half]) for _ in range(4))
        s_pos = ctx.enter_context(nc.semaphore("positions_loaded"))
        p.wait("scalar", [p.latest("vector")])
        p.dma("scalar", pos_i, A["positions"], s_pos)
        p.dma("scalar", freq, A["c_freq"], s_pos)
        tok = V(lambda e: e.tensor_copy(pos, pos_i), (s_pos, 32))
        tok = V(lambda e: e.tensor_tensor(ang, bcast(pos.unsqueeze(2), [P, NT, half]),
                                          bcast(freq.unsqueeze(1), [P, NT, half]), ALU.mult), tok)
        tok = V(lambda e: e.tensor_scalar(turns, ang, 1.0 / (2 * math.pi), None, ALU.mult), tok)
        magic = 1.5 * 2.0 ** 23
        tok = V(lambda e: e.tensor_scalar(turns, turns, magic, None, ALU.add), tok)
        tok = V(lambda e: e.tensor_scalar(turns, turns, magic, None, ALU.subtract), tok)
        rest = 2 * math.pi
        for bits in (10, 10, None):
            part = rest if bits is None else float(np.floor(rest * 2.0 ** (bits - math.floor(math.log2(rest))))
                                                   / 2.0 ** (bits - math.floor(math.log2(rest))))
            rest -= part
            tok = V(lambda e, c=part: e.scalar_tensor_tensor(out=ang, in0=turns, scalar=-c, in1=ang,
                                                             op0=ALU.mult, op1=ALU.add), tok)
        pi = float(np.nextafter(np.float32(math.pi), np.float32(0)))
        wrap = turns
        t1 = V(lambda e: e.tensor_scalar(cos, ang, math.pi / 2, None, ALU.add), tok)
        t1 = V(lambda e: e.tensor_scalar(wrap, cos, pi, -2 * math.pi, ALU.is_gt, ALU.mult), t1)
        t1 = V(lambda e: e.tensor_tensor(cos, cos, wrap, ALU.add), t1)
        t1 = V(lambda e: e.tensor_scalar(cos, cos, pi, -pi, ALU.min, ALU.max), t1)
        t2 = V(lambda e: e.tensor_scalar(sin, ang, pi, -pi, ALU.min, ALU.max), t1)
        t_cs = S(lambda e: e.activation(cos, cos, ACT.Sin), t2)
        t_cs = S(lambda e: e.activation(sin, sin, ACT.Sin), t2, t_cs)

        scratch = room([GM_W])
        sg, gains, t_gain = vector_row(A["ab_mla_q_norm"][0], A["ab_mla_kv_norm"][0])
        nt = []
        for t in range(NT):
            for src, w, g0, dep in ((cq[:, t, :], Q_RANK, 0, toks[0]), (ckv[:, t, 0:KV_RANK], KV_RANK, Q_RANK, toks[1])):
                r, tok = rms_factor(src, w, scratch[:, 0:w], LN_EPS, dep)
                nt.append(V(lambda e, src=src, r=r, g0=g0, w=w: e.scalar_tensor_tensor(
                    out=src, in0=src, scalar=r, in1=gains[:, g0:g0 + w], op0=ALU.mult, op1=ALU.mult), tok, t_gain))
        vectors.release(sg, nt[-1])
        lat = room([3, SEQ])
        t_lat = to_cols(lat, lambda k, t: (cq[:, t, k * P:(k + 1) * P] if k < 2 else ckv[:, t, 0:KV_RANK]),
                        3, (0, 1), *nt)
        q_rows, k_rows = room([NT, MLA_H, MLA_D]), room([NT, MLA_H, MLA_D])
        v_rows = room([NT, MLA_H * MLA_V])
        QD = MLA_H * MLA_D
        wqs = [weights.load((A["ab_mla_w_uq"][0, k * P:(k + 1) * P, :], lambda b: b[:, 0:QD])) for k in range(2)]
        s2, wkv, t_wkv = weights.load((A["ab_mla_w_uk"][0], lambda b: b[:, 0:512]),
                                      (A["ab_mla_w_uv"][0], lambda b: b[:, 512:1024]))
        t_rows = []
        for t in range(NT):
            ts = slice(t * P, (t + 1) * P)
            qf = q_rows[:, t].rearrange("p h d -> p (h d)")
            for i in range(2):
                done = product(psum[2 + i][:, 0:QD // 2], [
                    (lat[:, k, ts], wqs[k][1][:, i * QD // 2:(i + 1) * QD // 2], wqs[k][2])
                    for k in range(2)], *t_lat, *bank_free[2 + i])
                bank_free[2 + i] = (copy_out(qf[:, i * QD // 2:(i + 1) * QD // 2], psum[2 + i][:, 0:QD // 2], done),)
                t_rows += bank_free[2 + i]
            for i in range(2):
                done = product(psum[6 + i][:, :], [(lat[:, 2, ts], wkv[:, i * 512:(i + 1) * 512])],
                               *t_lat, t_wkv, *bank_free[6 + i])
                if i == 0:
                    src = psum[6][:, :].rearrange("p (h d) -> p h d", h=MLA_H)
                    bank_free[6] = (copy_out(k_rows[:, t, :, 0:NOPE], src, done),)
                else:
                    bank_free[7] = (copy_out(v_rows[:, t, :], psum[7][:, :], done),)
                t_rows += bank_free[6 + i]
        for slot in (wqs[0][0], wqs[1][0], s2):
            weights.release(slot, done)
        a1, a2 = room([MLA_H, half]), room([MLA_H, half])
        t_rope = []
        tok = None
        for t in range(NT):
            for x1, x2, h, o1, o2 in (
                    (q_rows[:, t, :, NOPE:NOPE + half], q_rows[:, t, :, NOPE + half:MLA_D], MLA_H,
                     q_rows[:, t, :, NOPE:NOPE + half], q_rows[:, t, :, NOPE + half:MLA_D]),
                    (ckv[:, t, KV_RANK:KV_RANK + half].unsqueeze(1), ckv[:, t, KV_RANK + half:].unsqueeze(1), 1,
                     k_rows[:, t, 0:1, NOPE:NOPE + half], k_rows[:, t, 0:1, NOPE + half:MLA_D])):
                c = bcast(cos[:, t, :].unsqueeze(1), [P, h, half])
                s = bcast(sin[:, t, :].unsqueeze(1), [P, h, half])
                tok = rotate(x1, x2, o1, o2, c, s, a1[:, 0:h], a2[:, 0:h], t_cs, *t_rows)
            tok = V(lambda e, t=t: e.tensor_copy(k_rows[:, t, 1:, NOPE:],
                                                 bcast(k_rows[:, t, 0:1, NOPE:], [P, MLA_H - 1, ROPE])), tok)
            t_rope.append(tok)
        qc, kc = room([MLA_H, SEQ]), room([MLA_H, SEQ])
        t_qk = []
        for j, (dst, src) in enumerate(((qc, q_rows), (kc, k_rows))):
            for h0 in range(0, MLA_H, 2):
                b = 2 + (h0 // 2) % 2
                for h in (h0, h0 + 1):
                    for t in range(NT):
                        o = psum[b][0:MLA_D, (h - h0) * SEQ + t * P:(h - h0) * SEQ + (t + 1) * P]
                        tok = PE(lambda e, o=o, i=src[:, t, h, :]: e.transpose(o, i, ident[:]),
                                 t_rope[-1], *bank_free[b])
                tok = copy_out(dst[0:MLA_D, h0:h0 + 2, :],
                               psum[b][0:MLA_D, :].rearrange("p (h t) -> p h t", h=2), tok)
                bank_free[b] = (tok,)
                t_qk.append(tok)

        sp, wsp, t_wsp = weights.load((A["gm_ws_t"].rearrange("g s t -> s g t"),
                                       lambda b: b[:, 0:512].rearrange("p (g t) -> p g t", g=GM_G)),
                                      (A["gm_bs_t"], lambda b: b[:, 512:516]),
                                      (A["c_upper"], lambda b: b[:, 520:648]))
        ws = room([GM_G, P])
        t_ws = V(lambda e: e.tensor_tensor(ws, wsp[:, 0:512].rearrange("p (g t) -> p g t", g=GM_G),
                                           bcast(wsp[:, 520:648].unsqueeze(1), [P, GM_G, P]), ALU.mult), t_wsp)
        t_v = [normalise(v[:, t, :], v[:, t, :], GM_W, toks[3]) for t in range(NT)]
        t_v = affine_rows(v, A["ab_gm_ln_g"][0], A["ab_gm_ln_b"][0], t_v)
        t_mix = []
        for t in range(NT):
            for g in range(GM_G):
                done = product(psum[6 + t][:, g * P:(g + 1) * P], [(ws[:, g, :], v[:, t, g * P:(g + 1) * P])],
                               t_v[t], t_ws, *bank_free[6 + t])
            for g in range(GM_G):
                gs = slice(g * P, (g + 1) * P)
                tok = V(lambda e, t=t, g=g, gs=gs: e.scalar_tensor_tensor(
                    out=mix[:, t, gs], in0=psum[6 + t][:, gs], scalar=wsp[:, 512 + g:513 + g],
                    in1=u[:, t, gs], op0=ALU.add, op1=ALU.mult), done, toks[5])
            bank_free[6 + t] = (tok,)
            t_mix.append(tok)
        weights.release(sp, t_mix[-1])

        bufs = attention_buffers()
        inv = room([8])
        for t in range(NT):
            def finish(h0, ps, sums, tok, t=t):
                tok = V(lambda e: e.reciprocal(inv, sums), tok)
                tok = V(lambda e: e.tensor_tensor(
                    mix[:, t, GM_W:].rearrange("p (h d) -> p h d", h=8), ps,
                    bcast(inv.unsqueeze(2), [P, 8, DH]), ALU.mult), tok)
                t_mix.append(tok)
                return (tok,)
            nk = (t + 1) * P
            attention(t, MLA_H, nk, lambda h, t=t: qc[0:MLA_D, h, t * P:(t + 1) * P],
                      lambda h, nk=nk: kc[0:MLA_D, h, 0:nk],
                      lambda h, j: v_rows[:, j, h * DH:(h + 1) * DH],
                      float(MLA_D) ** -0.5, causal[:, t, 0:nk], finish, bufs, *t_qk)
        toks = output_projection(mix, A["ab_w_o"][0], add_scaled_residual, x_cols, *t_mix)
        return post_norm(A["ln1_g"][0], A["ln1_b"][0], toks)

    def rotate(x1, x2, o1, o2, c, s, a1, a2, *after):
        t1 = V(lambda e: e.tensor_tensor(a1, x1, s, ALU.mult), *after)
        t2 = V(lambda e: e.tensor_tensor(a2, x2, s, ALU.mult), *after)
        t3 = V(lambda e: e.tensor_tensor(o1, x1, c, ALU.mult), t1, t2)
        t3 = V(lambda e: e.tensor_tensor(o1, o1, a2, ALU.subtract), t3)
        t4 = V(lambda e: e.tensor_tensor(o2, x2, c, ALU.mult), t3)
        return V(lambda e: e.tensor_tensor(o2, o2, a1, ALU.add), t4)

    def output_projection(mix_rows, w, add, cols, *after, evac=None):
        t_cols = to_cols(cols, lambda k, t: mix_rows[:, t, k * P:(k + 1) * P], KD, (0, 1, 2, 3), *after,
                         evac=evac)
        toks = None
        announce_chunks(w, *[(c0, CHUNK) for c0 in range(0, D, CHUNK)])
        for j, c0 in enumerate(range(0, D, CHUNK)):
            b = 4 + j % 2
            ps, done = project_rows(cols, CHUNK, b, *t_cols)
            toks = add(c0, CHUNK, ps, done)
            bank_free[b] = tuple(toks)
        return toks

    def moe(layer, t_in):
        fresh()
        t_cols = to_cols(x_cols, lambda k, t: x_rows[:, t, k * P:(k + 1) * P], KD, (0, 1, 2, 3), *t_in)
        NL = MOE_G + N_EXP
        announce((A["router_w"][layer].rearrange("(k p) n -> p k n", p=P), (KD, NL)))
        ups = [[(A[w][layer, e_, j].rearrange("p (k f) -> p k f", k=KD), (KD, P))
                for j in range(2) for w in ("moe_gate", "moe_up")] for e_ in range(N_EXP)]
        downs = [[(A["moe_w_down"][layer, e_, j * P:(j + 1) * P, :], (D,)) for j in range(2)]
                 for e_ in range(N_EXP)]
        for now, before in zip(ups + [[]], [[]] + downs):
            announce(*now, *before)
        wr, number, t_wr = take((KD, NL))
        sv, rb, t_rb = vector_row(A["router_b"][layer])
        for t in range(NT):
            done = product3(psum[6][:, t * NL:(t + 1) * NL],
                            [(at(x_cols, slice(None), k, slice(t * P, (t + 1) * P)), at(wr, slice(None), k))
                             for k in range(KD)], *t_cols, t_wr, *bank_free[6])
        release_splits([number], done)
        lg = room([NT, NL])
        tok = V(lambda e: e.tensor_tensor(lg, psum[6][:, 0:NT * NL].rearrange("p (t n) -> p t n", t=NT),
                                          bcast(rb[:, 0:NL].unsqueeze(1), [P, NT, NL]), ALU.add), done, t_rb)
        bank_free[6] = (tok,)
        vectors.release(sv, tok)
        g8, gm8, em8 = room([NT, 8]), room([NT, 8]), room([NT, 8])
        gi, ei = room([NT, 8], dt=U32), room([NT, 8], dt=U32)
        tok = V(lambda e: e.memset(g8, LOWEST), tok)
        tok = V(lambda e: e.tensor_copy(g8[:, :, 0:MOE_G], lg[:, :, 0:MOE_G]), tok)
        for t in range(NT):
            tok = V(lambda e, t=t: e.max(gm8[:, t, :], g8[:, t, :]), tok)
            tok = V(lambda e, t=t: e.max_index(gi[:, t, :], gm8[:, t, :], g8[:, t, :]), tok)
        gsel, ohg = room([NT]), room([NT, MOE_G])
        tok = V(lambda e: e.tensor_copy(gsel, gi[:, :, 0]), tok)
        tok = V(lambda e: e.tensor_tensor(ohg, bcast(iota[:, 0:MOE_G].unsqueeze(1), [P, NT, MOE_G]),
                                          bcast(gsel.unsqueeze(2), [P, NT, MOE_G]), ALU.is_equal), tok, t_iota)
        ge, gsum = room([NT, MOE_G]), room([NT])
        tok = V(lambda e: e.tensor_tensor(ge, lg[:, :, 0:MOE_G], bcast(gm8[:, :, 0:1], [P, NT, MOE_G]),
                                          ALU.subtract), tok)
        t_ge = S(lambda e: e.activation(ge, ge, ACT.Exp), tok)
        esel, picked = room([NT, MOE_E]), room([NT, MOE_E, MOE_G])
        for t in range(NT):
            tok = V(lambda e, t=t: e.tensor_tensor(
                picked[:, t], lg[:, t, MOE_G:].rearrange("p (g e) -> p e g", g=MOE_G),
                bcast(ohg[:, t, :].unsqueeze(1), [P, MOE_E, MOE_G]), ALU.mult), tok)
        tok = V(lambda e: e.tensor_reduce(esel, picked, AX_X, ALU.add), tok)
        for t in range(NT):
            tok = V(lambda e, t=t: e.max(em8[:, t, :], esel[:, t, :]), tok)
            tok = V(lambda e, t=t: e.max_index(ei[:, t, :], em8[:, t, :], esel[:, t, :]), tok)
        p2, p1, eif = room([NT]), room([NT]), room([NT, 2])
        tok = V(lambda e: e.tensor_tensor(p2, em8[:, :, 1], em8[:, :, 0], ALU.subtract), tok)
        t_p2 = S(lambda e: e.activation(p2, p2, ACT.Exp), tok)
        tok = V(lambda e: e.tensor_copy(eif, ei[:, :, 0:2]), tok)
        tok = V(lambda e: e.tensor_reduce(gsum, ge, AX_X, ALU.add), tok, t_ge)
        tok = V(lambda e: e.scalar_tensor_tensor(out=p1, in0=p2, scalar=1.0, in1=gsum, op0=ALU.add,
                                                 op1=ALU.mult), tok, t_p2)
        tok = V(lambda e: e.reciprocal(p1, p1), tok)
        tok = V(lambda e: e.tensor_tensor(p2, p2, p1, ALU.mult), tok)
        oh1, oh2, wmoe = room([NT, MOE_E]), room([NT, MOE_E]), room([NT, MOE_G, MOE_E])
        for oh, j, pr in ((oh1, 0, p1), (oh2, 1, p2)):
            tok = V(lambda e, oh=oh, j=j: e.tensor_tensor(
                oh, bcast(iota[:, 0:MOE_E].unsqueeze(1), [P, NT, MOE_E]),
                bcast(eif[:, :, j:j + 1], [P, NT, MOE_E]), ALU.is_equal), tok)
            tok = V(lambda e, oh=oh, pr=pr: e.tensor_tensor(oh, oh, bcast(pr.unsqueeze(2), [P, NT, MOE_E]),
                                                            ALU.mult), tok)
        tok = V(lambda e: e.tensor_tensor(oh1, oh1, oh2, ALU.add), tok)
        for t in range(NT):
            tok = V(lambda e, t=t: e.tensor_tensor(
                wmoe[:, t], bcast(ohg[:, t, :].unsqueeze(2), [P, MOE_G, MOE_E]),
                bcast(oh1[:, t, :].unsqueeze(1), [P, MOE_G, MOE_E]), ALU.mult), tok)
        wflat = wmoe.rearrange("p t g e -> p t (g e)")
        for t in range(NT):
            tok = V(lambda e, t=t: e.tensor_scalar(x_rows[:, t, :], x_rows[:, t, :], ALPHA, None, ALU.mult),
                    *t_cols, tok)
        t_res = [tok] * NT

        silu = [room([2, SEQ]) for _ in range(2)]
        hid = [room([2, SEQ]) for _ in range(2)]
        hid_tok, hid_free = {}, {}

        def up(e_):
            i = e_ % 2
            for j in range(2):
                for b in (2 * i, 2 * i + 1):
                    wt, number, tk = take((KD, P))
                    done = product3(psum[b][:, j * SEQ:(j + 1) * SEQ],
                                    [(at(wt, slice(None), k), at(x_cols, slice(None), k)) for k in range(KD)],
                                    *t_cols, tk, *bank_free[b])
                    release_splits([number], done)
            gate, upper = (psum[2 * i + c][:, :].rearrange("p (j t) -> p j t", j=2) for c in range(2))
            a = S(lambda e: e.activation(silu[i], gate, ACT.Silu), done)
            bank_free[2 * i] = (a,)
            h = V(lambda e: e.tensor_tensor(hid[i], silu[i], upper, ALU.mult), a)
            bank_free[2 * i + 1] = (h,)
            hid_tok[e_] = split(hidden_parts[i], hid[i], h, *hid_free.get(e_ - 2, ()))

        def out_(e_):
            i = e_ % 2
            for j in range(2):
                wt, number, tk = take((D,))
                for t in range(NT):
                    for h in range(2):
                        b = 4 + 2 * t + h
                        l = at(hidden_parts[i], slice(None), j, slice(t * P, (t + 1) * P))
                        r = at(wt, slice(None), slice(h * 512, (h + 1) * 512))
                        for n, (x, y) in enumerate(((l[0], r[0]), (l[0], r[1]), (l[1], r[0]))):
                            done = PE(lambda e: e.matmul(psum[b][:, :], x, y, start=(j == 0 and n == 0),
                                                         stop=(j == 1 and n == 2)),
                                      hid_tok[e_], tk, *bank_free[b])
                        if j == 1:
                            xs = x_rows[:, t, h * 512:(h + 1) * 512]
                            t_res[t] = V(lambda e: e.scalar_tensor_tensor(
                                out=xs, in0=psum[b][:, :], scalar=wflat[:, t, e_:e_ + 1], in1=xs,
                                op0=ALU.mult, op1=ALU.add), done, t_res[t])
                            bank_free[b] = (t_res[t],)
                release_splits([number], done)
            hid_free[e_] = (done,)

        for e_ in range(N_EXP + 1):
            if e_ < N_EXP:
                up(e_)
            if e_ >= 1:
                out_(e_ - 1)
        return post_norm(A["ln2_g"][layer], A["ln2_b"][layer], [t_res[1], t_res[1]])

    def store(rows, *after):
        s = ctx.enter_context(nc.semaphore("stored"))
        p.wait("sync", after)
        p.dma("sync", out.rearrange("b (t p) d -> p (b t) d", p=P), rows, s)
        p.wait("sync", [(s, 16)])

    def mixer_1(t_in):
        fresh()
        w_in = A["c_w_in"][0]
        t_cols = to_cols(x_cols, lambda k, t: x_rows[:, t, k * P:(k + 1) * P], KD, (0, 1, 2, 3), *t_in)
        q = room([NSA_H // 2, SEQ])
        kv = {n: room([NSA_G, SEQ]) for n in ("ks", "kw")}
        vals = {n: room([NT, P]) for n in ("vs", "vw")}
        raw = {n: room([NSA_G, SEQ], parts=DH) for n in ("kc", "vc")}
        gates = room([NT, 3 * NSA_H])
        o_rows = room([NT, D])
        straight, swap = room([SEQ]), room([P])
        s_sw = ctx.enter_context(nc.semaphore("swap_loaded"))
        p.wait("scalar", [p.latest("vector"), p.latest("tensor")])
        p.dma("scalar", swap, A["c_swap"], s_sw)
        t_swap = (s_sw, 16)
        NG = 3 * NSA_H
        t_q = []
        announce_chunks(w_in, *[(c0, CHUNK) for c0 in range(0, 1792, CHUNK)], (1792, NG))
        for j in range(4):
            b = 4 + j % 2
            ps, done = project_cols(x_cols, b, *t_cols)
            tok = copy_out(q[:, 2 * j:2 * j + 2, :], ps, done)
            bank_free[b] = (tok,)
            t_q.append(tok)
        t_kv = {}
        for names in (("kc", "vc"), ("ks", "vs"), ("kw", "vw")):
            wt, numbers, tw = take_chunk(CHUNK)
            for i, n in enumerate(names):
                b = 4 + i
                if n in vals:
                    for t in range(NT):
                        done = product3(psum[b][:, t * P:(t + 1) * P],
                                        [(at(x_cols, slice(None), k, slice(t * P, (t + 1) * P)),
                                          wt(k, slice(i * P, (i + 1) * P)))
                                         for k in range(KD)], *t_cols, *tw, *bank_free[b])
                    tok = copy_out(vals[n], psum[b][:, 0:NT * P].rearrange("p (t n) -> p t n", t=NT), done)
                else:
                    done = product3(psum[b][:, 0:SEQ],
                                    [(wt(k, slice(i * P, (i + 1) * P)), at(x_cols, slice(None), k))
                                     for k in range(KD)], *tw, *t_cols, *bank_free[b])
                    tok = copy_out(straight, psum[b][:, 0:SEQ], done, p.latest("vector"), p.latest("scalar"),
                                   p.latest("tensor"))
                    done = product(psum[b][:, SEQ:], [(swap, straight)], tok, t_swap)
                    lower, upper = slice(0, DH), slice(DH, P)
                    if n in kv:
                        tok = V(lambda e: e.tensor_copy(kv[n][lower, 0, :], straight[lower, :]), done)
                        tok = V(lambda e: e.tensor_copy(kv[n][upper, 1, :], straight[upper, :]), tok)
                        tok = V(lambda e: e.tensor_copy(kv[n][upper, 0, :], psum[b][upper, SEQ:]), tok)
                        tok = V(lambda e: e.tensor_copy(kv[n][lower, 1, :], psum[b][lower, SEQ:]), tok)
                    else:
                        tok = V(lambda e: e.tensor_copy(raw[n][:, 0, :], straight[lower, :]), done)
                        tok = V(lambda e: e.tensor_copy(raw[n][:, 1, :], psum[b][lower, SEQ:]), tok)
                bank_free[b] = (tok,)
                t_kv[n] = tok
            release_splits(numbers, done)
        sv, gb, t_gb = vector_row(A["c_gate_b"][0])
        ps, done = project_rows(x_cols, NG, 4, *t_cols)
        tok = V(lambda e: e.tensor_tensor(gates, ps, bcast(gb[:, 0:NG].unsqueeze(1), [P, NT, NG]), ALU.add),
                done, t_gb)
        bank_free[4] = (tok,)
        vectors.release(sv, tok)
        t_gate = S(lambda e: e.activation(gates, gates, ACT.Sigmoid), tok)

        NB = NSA_G * N_CMP
        k_cmp = room([NB])
        v_cmp = room([NSA_G, DH])
        blocks = room([CMP_LEN, NB], parts=DH)
        hidden = room([2, NB])
        pos_col = room([2, CMP_LEN], parts=DH)
        s_pc = ctx.enter_context(nc.semaphore("cmp_pos_loaded"))
        p.wait("scalar", [p.latest("vector")])
        p.dma("scalar", pos_col, A["cmp_pos_t"], s_pc)
        hid_rows = room([CMP_HID])
        PER = 4
        for i, (n, w1, w2) in enumerate((("kc", "c_w_ck1", "c_w_ck2"), ("vc", "c_w_cv1", "c_w_cv2"))):
            src = raw[n].rearrange("p g (m b) -> p g m b", b=CMP_STRIDE)
            for a in range(CMP_LEN // CMP_STRIDE):
                for g in range(NSA_G):
                    dst = blocks[:, a * CMP_STRIDE:(a + 1) * CMP_STRIDE, g * N_CMP:(g + 1) * N_CMP]
                    tok = V(lambda e, a=a, g=g, dst=dst: e.tensor_tensor(
                        dst, src[:, g, a:a + N_CMP, :].rearrange("p m b -> p b m"),
                        bcast(pos_col[:, i, a * CMP_STRIDE:(a + 1) * CMP_STRIDE].unsqueeze(2),
                              [DH, CMP_STRIDE, N_CMP]), ALU.add), t_kv[n], (s_pc, 16), p.latest("tensor"))
            for l0 in range(0, CMP_LEN, PER):
                s, buf, tw = weights.load((A[w1][0, l0 * DH:(l0 + PER) * DH, :].rearrange("(l d) n -> d l n", d=DH),
                                           lambda b: b[0:DH, :].rearrange("p (l n) -> p l n", l=PER)))
                for l in range(l0, l0 + PER):
                    at_l = (l - l0) * CMP_HID
                    done = PE(lambda e: e.matmul(psum[6][0:NB, 0:CMP_HID], blocks[:, l, :],
                                                 buf[0:DH, at_l:at_l + CMP_HID], start=(l == 0),
                                                 stop=(l == CMP_LEN - 1)), tok, tw, *bank_free[6])
                weights.release(s, done)
            tok = S(lambda e: e.activation(hid_rows[0:NB], psum[6][0:NB, 0:CMP_HID], ACT.Gelu_apprx_tanh), done)
            bank_free[6] = (tok,)
            for j in range(2):
                done = PE(lambda e: e.transpose(psum[7][:, j * NB:(j + 1) * NB], hid_rows[0:NB, j * P:(j + 1) * P],
                                                ident[0:NB, 0:NB]), tok, *bank_free[7])
            tok = copy_out(hidden, psum[7][:, 0:2 * NB].rearrange("p (j n) -> p j n", j=2), done)
            bank_free[7] = (tok,)
            s, buf, tw = weights.load((A[w2][0].rearrange("(j p) n -> p j n", p=P),
                                       lambda b: b[:, 0:2 * DH].rearrange("p (j n) -> p j n", j=2)))
            if n == "kc":
                for half in (0, DH):
                    done = product(psum[7][half:half + DH, 0:NB],
                                   [(buf[:, j * DH:(j + 1) * DH], hidden[:, j, :]) for j in range(2)],
                                   tok, tw, *bank_free[7])
                tok = t_kc = copy_out(k_cmp, psum[7][:, 0:NB], done)
            else:
                for g in range(NSA_G):
                    done = product(psum[7][0:N_CMP, g * DH:(g + 1) * DH],
                                   [(hidden[:, j, g * N_CMP:(g + 1) * N_CMP], buf[:, j * DH:(j + 1) * DH])
                                    for j in range(2)], tok, tw, *bank_free[7])
                tok = t_vc = copy_out(v_cmp[0:N_CMP], psum[7][0:N_CMP, 0:NSA_G * DH]
                                      .rearrange("p (g d) -> p g d", g=NSA_G), done)
            bank_free[7] = (tok,)
            weights.release(s, done)

        def q_of(h, ts):
            half = (h % 2) * DH
            return q[half:half + DH, h // 2, ts]

        cmask = room([NT, 3, N_CMP])
        s_cm = ctx.enter_context(nc.semaphore("cmp_mask_loaded"))
        p.dma("scalar", cmask, A["c_cmp_mask"], s_cm)
        sc, csum, cmax = room([NSA_H, N_CMP]), room([NSA_H]), room([NSA_H])
        pt = room([4, P])
        factor = room([8])
        part = room([8, DH])
        t_o = []
        for t in range(NT):
            ts = slice(t * P, (t + 1) * P)
            shape = [P, NSA_H, N_CMP]
            for odd in range(2):
                b, half, nh = 6 + odd, odd * DH, NSA_H // 2
                for i in range(nh):
                    h = 2 * i + odd
                    g = h // 8
                    done = product(psum[b][:, i * N_CMP:(i + 1) * N_CMP],
                                   [(q_of(h, ts), k_cmp[half:half + DH, g * N_CMP:(g + 1) * N_CMP])],
                                   *t_q, t_kc, *bank_free[b])
                tok = V(lambda e: e.scalar_tensor_tensor(
                    out=sc[:, odd::2, :], in0=psum[b][:, 0:nh * N_CMP].rearrange("p (h n) -> p h n", h=nh),
                    scalar=DH ** -0.5, in1=bcast(cmask[:, t, 0:1, :], [P, nh, N_CMP]), op0=ALU.mult,
                    op1=ALU.add), done, (s_cm, 16), p.latest("tensor"))
                bank_free[b] = (tok,)
            tok = V(lambda e: e.tensor_reduce(cmax, sc, AX_X, ALU.max), tok)
            tok = V(lambda e: e.tensor_tensor(sc, sc, bcast(cmax.unsqueeze(2), shape), ALU.subtract), tok)
            tok = S(lambda e: e.activation(sc, sc, ACT.Exp), tok)
            tok = V(lambda e, t=t: e.tensor_tensor(sc, sc, bcast(cmask[:, t, 1:2, :], shape), ALU.mult), tok)
            t_sc = tok
            tok = V(lambda e: e.tensor_reduce(csum, sc, AX_X, ALU.add), tok)
            tok = V(lambda e, t=t: e.tensor_scalar(csum, csum, cmask[:, t, 2, 0:1], None, ALU.add), tok)
            tok = V(lambda e: e.reciprocal(csum, csum), tok)
            tok = t_fac = V(lambda e, t=t: e.tensor_tensor(csum, csum, gates[:, t, 0:NSA_H], ALU.mult), tok, t_gate)
            for h0 in range(0, NSA_H, 4):
                b = h0 // 4 % 2
                for i in range(4):
                    tok = PE(lambda e, i=i: e.transpose(psum[b][0:N_CMP, i * P:(i + 1) * P], sc[:, h0 + i, :],
                                                        ident[:]), t_sc, *bank_free[b])
                tok = copy_out(pt[0:N_CMP], psum[b][0:N_CMP, :].rearrange("p (i t) -> p i t", i=4), tok,
                               p.latest("tensor"))
                bank_free[b] = (tok,)
                ob = 2 + h0 // 8
                for i in range(4):
                    h = h0 + i
                    done = product(psum[ob][:, (h % 8) * DH:(h % 8 + 1) * DH],
                                   [(pt[0:N_CMP, i, :], v_cmp[0:N_CMP, h // 8, :])], tok, t_vc, *bank_free[ob])
                if h0 % 8 == 4:
                    hb = h0 - 4
                    tok = V(lambda e, t=t, hb=hb, ob=ob: e.tensor_tensor(
                        o_rows[:, t, hb * DH:(hb + 8) * DH].rearrange("p (h d) -> p h d", h=8),
                        psum[ob][:, :].rearrange("p (h d) -> p h d", h=8),
                        bcast(csum[:, hb:hb + 8].unsqueeze(2), [P, 8, DH]), ALU.mult), done, t_fac)
                    bank_free[ob] = (tok,)
        bufs = attention_buffers()
        for br, (kn, vn) in enumerate((("ks", "vs"), ("kw", "vw"))):
            for t in range(NT):
                def finish(h0, ps, sums, tok, t=t, br=br):
                    tok = V(lambda e: e.reciprocal(factor, sums), tok)
                    g0 = (br + 1) * NSA_H + h0
                    tok = V(lambda e: e.tensor_tensor(factor, factor, gates[:, t, g0:g0 + 8], ALU.mult), tok)
                    tok = V(lambda e: e.tensor_tensor(part, ps, bcast(factor.unsqueeze(2), [P, 8, DH]),
                                                      ALU.mult), tok)
                    o = o_rows[:, t, h0 * DH:(h0 + 8) * DH].rearrange("p (h d) -> p h d", h=8)
                    t_o.append(V(lambda e: e.tensor_tensor(o, o, part, ALU.add), tok))
                    return (tok,)
                ts, nk = slice(t * P, (t + 1) * P), (t + 1) * P
                attention(t, NSA_H, nk, lambda h, ts=ts: q_of(h, ts),
                          lambda h, nk=nk, kn=kn: kv[kn][(h % 2) * DH:(h % 2 + 1) * DH, h // 8, 0:nk],
                          lambda h, j, vn=vn: vals[vn][:, j, (h // 8) * DH:(h // 8 + 1) * DH],
                          DH ** -0.5, causal[:, t, 0:nk], finish, bufs, *t_q, *t_kv.values())
        toks = output_projection(o_rows, A["c_w_o"][0], add_scaled_residual, x_cols, *t_o)
        return post_norm(A["ln1_g"][1], A["ln1_b"][1], toks)

    NMOD = 6 * KD
    mod = [sb(f"mod{l}", [P, NMOD, 2]) for l in range(DEPTH)]
    gate_row = sb("gate_row", [P, D])
    rope_cos, rope_sin = sb("rope_cos", [P, NT, DH // 2]), sb("rope_sin", [P, NT, DH // 2])
    param_sems = {}

    def modulation():
        c2, bm = room([KD, 2]), room([DEPTH, NMOD])
        s_c = ctx.enter_context(nc.semaphore("conditions_loaded"))
        p.wait("scalar", [p.latest("vector"), p.latest("tensor")])
        for dst, n in ((c2, "cond"), (bm, "b_mod_t"), (rope_cos[:], "c_rope_cos"), (rope_sin[:], "c_rope_sin")):
            p.dma("scalar", dst, A[n], s_c)
        t_c = S(lambda e: e.activation(c2, c2, ACT.Silu), (s_c, 64))
        hk = KD // 2
        rows = room([NMOD * P])
        for l in range(DEPTH):
            for j in range(NMOD // 2):
                bank = j % 4
                for i in range(2):
                    s, buf, tw = weights.load((
                        A["w_mod_2"][l, i * hk * P:(i + 1) * hk * P, j * CHUNK:(j + 1) * CHUNK]
                        .rearrange("(k p) n -> p k n", p=P), lambda b: b[:, :].rearrange("p (k n) -> p k n", k=hk)))
                    for k in range(hk):
                        done = PE(lambda e: e.matmul(psum[bank][0:2, 0:CHUNK], c2[:, i * hk + k, :],
                                                     buf[:, k * CHUNK:(k + 1) * CHUNK], start=(i + k == 0),
                                                     stop=(i * hk + k == KD - 1)), t_c, tw, *bank_free[bank])
                    weights.release(s, done)
                tok = copy_out(rows[0:2, j * CHUNK:(j + 1) * CHUNK], psum[bank][0:2, 0:CHUNK], done,
                               p.latest("tensor"))
                bank_free[bank] = (tok,)
            both = (p.latest("vector"), p.latest("scalar"))
            for m in range(NMOD):
                done = PE(lambda e: e.transpose(psum[7][:, 2 * m:2 * m + 2], rows[0:2, m * P:(m + 1) * P],
                                                ident[0:2, 0:2]), *both, *bank_free[7])
            ps = psum[7][:, 0:2 * NMOD].rearrange("p (m s) -> p m s", s=2)
            tok = V(lambda e, l=l: e.tensor_tensor(mod[l][:], ps, bcast(bm[:, l, :].unsqueeze(2), [P, NMOD, 2]),
                                                   ALU.add), done)
            bank_free[7] = (tok,)
            for m in (KD, 4 * KD):
                tok = V(lambda e, l=l, m=m: e.tensor_scalar(mod[l][:, m:m + KD, :], mod[l][:, m:m + KD, :],
                                                            1.0, None, ALU.add), tok)
        return tok

    def spread_gate(l, stream, first, *after):
        diag = room([KD, P])
        tok = V(lambda e: e.tensor_tensor(diag, bcast(ident[:].unsqueeze(1), [P, KD, P]),
                                          bcast(mod[l][:, first:first + KD, stream].unsqueeze(2), [P, KD, P]),
                                          ALU.mult), *after, t_ident)
        for h in range(2):
            done = product(psum[6 + h][:, :], [(ones[:], diag[:, 4 * h:4 * h + 4, :])], tok, t_ones,
                           *bank_free[6 + h])
            tok2 = V(lambda e: e.tensor_copy(gate_row[:, h * 512:(h + 1) * 512], psum[6 + h][:, :]), done)
            bank_free[6 + h] = (tok2,)
        return tok2

    def modulated_cols(dst, rows, l, shift, stream, after):
        normed = room([NT, D])
        toks = []
        for t in range(NT):
            r, tok = rms_factor(rows[:, t, :], D, normed[:, t, :], RMS_EPS, *after)
            toks.append(V(lambda e, t=t, r=r: e.tensor_scalar(normed[:, t, :], rows[:, t, :], r, None, ALU.mult),
                          tok))

        moved = [room([2, SEQ]) for _ in range(2)]

        def evac(k0, ps, tok):
            m = moved[k0 // 2 % 2]
            for k in (k0, k0 + 1):
                sc, sh = mod[l][:, shift + KD + k, stream:stream + 1], mod[l][:, shift + k, stream:stream + 1]
                tok = V(lambda e: e.tensor_scalar(m[:, k - k0, :], ps[:, k - k0, :], sc, sh, ALU.mult, ALU.add),
                        tok)
            return split(at(dst, slice(None), slice(k0, k0 + 2)), m, tok)
        return to_cols(dst, lambda k, t: normed[:, t, k * P:(k + 1) * P], KD, (0, 1, 2, 3), *toks, evac=evac)

    key_cols = sb("key_cols", [P, KV_HEADS, 2 * SEQ])
    val_rows = sb("val_rows", [P, 2 * NT, KVW])

    def qkv(cols, l, with_q, rotary, key_at, after):
        NHEAD = Q_HEADS + KV_HEADS
        qk = room([NT, NHEAD, DH])
        w_in = A["w_in_2"][l]
        flat = qk.rearrange("p t h d -> p t (h d)")
        toks = []
        chunks = (0, 256, 512) if with_q else (512,)
        announce_chunks(w_in, *[(c0, CHUNK) for c0 in chunks])
        for j, c0 in enumerate(chunks):
            b = 4 + j % 2
            ps, done = project_rows(cols, CHUNK, b, *after)
            if c0 < QW:
                tok = (copy_out(flat[:, :, c0:c0 + CHUNK], ps, done),)
            else:
                tok = (copy_out(flat[:, :, QW:QW + KVW], ps[:, :, 0:KVW], done),)
                tok += (copy_out(val_rows[:, key_at // P:key_at // P + NT, :], ps[:, :, KVW:], *tok),)
            bank_free[b] = tok
            toks += tok
        h0 = 0 if with_q else Q_HEADS
        nh = NHEAD - h0
        sg, gains, t_g = vectors.load(
            (A["q_gain_2"][l].partition_broadcast(P), lambda b: b[:, 0:DH]),
            (A["k_gain_2"][l].partition_broadcast(P), lambda b: b[:, DH:2 * DH]))
        sq, ms = room([NHEAD, DH]), room([NHEAD])
        a1, a2 = room([NHEAD, DH // 2]), room([NHEAD, DH // 2])
        kdup = room([KV_HEADS, 2, DH])
        q_cols = room([Q_HEADS // 2, SEQ])
        out_toks = []
        for t in range(NT):
            x = qk[:, t, h0:, :]
            tok = V(lambda e: e.tensor_tensor(sq[:, h0:], x, x, ALU.mult), *toks)
            tok = V(lambda e: e.tensor_reduce(ms[:, h0:], sq[:, h0:], AX_X, ALU.add), tok)
            tok = V(lambda e: e.tensor_scalar(ms[:, h0:], ms[:, h0:], 1.0 / DH, RMS_EPS, ALU.mult, ALU.add), tok)
            tok = S(lambda e: e.activation(ms[:, h0:], ms[:, h0:], ACT.Sqrt), tok)
            tok = V(lambda e: e.reciprocal(ms[:, h0:], ms[:, h0:]), tok)
            tok = V(lambda e: e.tensor_tensor(x, x, bcast(ms[:, h0:].unsqueeze(2), [P, nh, DH]), ALU.mult), tok)
            for a, b, g0 in ((h0, Q_HEADS, 0), (Q_HEADS, NHEAD, DH)):
                if b > a:
                    y = qk[:, t, a:b, :]
                    tok = V(lambda e, y=y, g0=g0, n=b - a: e.tensor_tensor(
                        y, y, bcast(gains[:, g0:g0 + DH].unsqueeze(1), [P, n, DH]), ALU.mult), tok, t_g)
            if rotary:
                hf = DH // 2
                c = bcast(rope_cos[:, t, :].unsqueeze(1), [P, nh, hf])
                s = bcast(rope_sin[:, t, :].unsqueeze(1), [P, nh, hf])
                tok = rotate(x[:, :, 0:hf], x[:, :, hf:], x[:, :, 0:hf], x[:, :, hf:], c, s,
                             a1[:, h0:], a2[:, h0:], tok)
            tok = V(lambda e, t=t: e.tensor_copy(kdup, bcast(qk[:, t, Q_HEADS:, :].unsqueeze(2),
                                                             [P, KV_HEADS, 2, DH])), tok, p.latest("tensor"))
            for g in range(KV_HEADS):
                done = PE(lambda e, g=g: e.transpose(psum[6][:, g * P:(g + 1) * P],
                                                     kdup[:, g].rearrange("p a d -> p (a d)"), ident[:]),
                          tok, *bank_free[6])
            k0 = key_at + t * P
            kt = copy_out(key_cols[:, :, k0:k0 + P], psum[6][:, 0:2 * P].rearrange("p (g t) -> p g t", g=2), done)
            bank_free[6] = (kt,)
            out_toks.append(kt)
            if with_q:
                for j in range(Q_HEADS // 2):
                    done = PE(lambda e, j=j, t=t: e.transpose(
                        psum[7][:, j * P:(j + 1) * P], flat[:, t, j * P:(j + 1) * P], ident[:]),
                        tok, *bank_free[7])
                kt = copy_out(q_cols[:, :, t * P:(t + 1) * P],
                              psum[7][:, :].rearrange("p (j t) -> p j t", t=P), done)
                bank_free[7] = (kt,)
                out_toks.append(kt)
        vectors.release(sg, p.latest("vector"))
        return q_cols, out_toks + toks

    def conformer(cols, l, dst, after):
        NC = CONV_W // P
        PAD = CONV_K // 2
        w_in = A["w_in_2"][l]
        g = room([NC, SEQ + 2 * PAD])
        y = room([NC, SEQ])
        a, gt = room([NC, SEQ]), room([2, SEQ])
        cw = room([NC, CONV_K + 1])
        s_cw = ctx.enter_context(nc.semaphore(f"conv_w_loaded_{len(param_sems)}"))
        param_sems[len(param_sems)] = s_cw
        p.wait("scalar", [p.latest("vector"), p.latest("tensor")])
        p.dma("scalar", cw, A["conv_wb_t"][l], s_cw)
        tok = V(lambda e: e.memset(g, 0.0))
        U0 = QW + 2 * KVW
        t_a = []
        announce_chunks(w_in, *[(U0 + i * CONV_W + j * CHUNK, CHUNK) for j in range(2) for i in range(2)])
        for j in range(2):
            ps, done = project_cols(cols, 4, *after)
            t_a.append(copy_out(a[:, 2 * j:2 * j + 2, :], ps, done))
            bank_free[4] = (t_a[-1],)
            ps, done = project_cols(cols, 5, *after)
            tok = S(lambda e, ps=ps: e.activation(gt, ps, ACT.Sigmoid), done, p.latest("vector"))
            bank_free[5] = (tok,)
            tok = V(lambda e, j=j: e.tensor_tensor(g[:, 2 * j:2 * j + 2, PAD:PAD + SEQ], a[:, 2 * j:2 * j + 2, :],
                                                   gt, ALU.mult), tok, t_a[-1])
        for i in range(CONV_K):
            for c in range(NC):
                w, src = cw[:, c, i:i + 1], g[:, c, i:i + SEQ]
                if i == 0:
                    tok = V(lambda e, c=c, w=w, src=src: e.tensor_scalar(
                        y[:, c, :], src, w, cw[:, c, CONV_K:], ALU.mult, ALU.add), tok, (s_cw, 16))
                else:
                    tok = V(lambda e, c=c, w=w, src=src: e.scalar_tensor_tensor(
                        out=y[:, c, :], in0=src, scalar=w, in1=y[:, c, :], op0=ALU.mult, op1=ALU.add), tok)
        t_rows = []
        for t in range(NT):
            for c in range(NC):
                done = PE(lambda e, c=c, t=t: e.transpose(psum[6 + t][:, c * P:(c + 1) * P],
                                                          y[:, c, t * P:(t + 1) * P], ident[:]),
                          tok, *bank_free[6 + t])
            t_rows.append(copy_out(dst[:, t, :], psum[6 + t][:, :], done))
            bank_free[6 + t] = (t_rows[-1],)
        t_rows = [normalise(dst[:, t, :], dst[:, t, :], CONV_W, t_rows[t]) for t in range(NT)]
        t_rows = affine_rows(dst, A["ln_g_2"][l], A["ln_b_2"][l], t_rows)
        return S(lambda e: e.activation(dst, dst, ACT.Silu), *t_rows)

    def merge(l, o_attn, o_conv, rows, after):
        beta = room([KD])
        s_b = ctx.enter_context(nc.semaphore(f"beta_loaded_{len(param_sems)}"))
        param_sems[len(param_sems)] = s_b
        p.wait("scalar", [p.latest("vector"), p.latest("tensor")])
        p.dma("scalar", beta, A["beta_t"][l], s_b)
        scratch = room([QW])
        toks = []
        for src in (o_attn, o_conv):
            for t in range(NT):
                r, tok = rms_factor(src[:, t, :], QW, scratch, RMS_EPS, *after)
                toks.append(V(lambda e, src=src, t=t, r=r: e.tensor_scalar(src[:, t, :], src[:, t, :], r, None,
                                                                           ALU.mult), tok))

        moved = [room([2, SEQ]) for _ in range(2)]

        def evac(k0, ps, tok):
            m = moved[k0 // 2 % 2]
            tok = V(lambda e: e.tensor_tensor(m, ps, bcast(beta[:, k0:k0 + 2].unsqueeze(2), [P, 2, SEQ]),
                                              ALU.mult), tok, (s_b, 16))
            return split(at(x_cols, slice(None), slice(k0, k0 + 2)), m, tok)

        t_cols = to_cols(x_cols, lambda k, t: (o_attn[:, t, k * P:(k + 1) * P] if k < QW // P else
                                               o_conv[:, t, (k * P - QW):(k * P - QW) + P]),
                         KD, (0, 1, 2, 3), *toks, evac=evac)
        part = room([NT, CHUNK])
        announce_chunks(A["w_o_2"][l], *[(c0, CHUNK) for c0 in range(0, D, CHUNK)])
        for j, c0 in enumerate(range(0, D, CHUNK)):
            b = 4 + j % 2
            ps, done = project_rows(x_cols, CHUNK, b, *t_cols)
            tok = V(lambda e, ps=ps, c0=c0: e.tensor_tensor(
                part, ps, bcast(gate_row[:, c0:c0 + CHUNK].unsqueeze(1), [P, NT, CHUNK]), ALU.mult), done)
            bank_free[b] = (tok,)
            r = rows[:, :, c0:c0 + CHUNK]
            tok = V(lambda e, r=r: e.tensor_tensor(r, r, part, ALU.add), tok)
        return tok

    def attend(l, rows, stream, nk, after):
        fresh()
        t_gate = spread_gate(l, stream, 2 * KD, *after)
        t_cols = modulated_cols(x_cols, rows, l, 0, stream, after)
        top[0] = 0
        p.stage()
        key_at = 0 if stream else SEQ
        q_cols, t_qkv = qkv(x_cols, l, True, not stream, key_at, t_cols)
        o_attn, o_conv = room([NT, QW]), room([NT, CONV_W])
        inv = room([8])
        bufs = attention_buffers()
        t_o = []
        for t in range(NT):
            def finish(h0, ps, sums, tok, t=t):
                tok = V(lambda e: e.reciprocal(inv, sums), tok)
                t_o.append(V(lambda e: e.tensor_tensor(o_attn[:, t, :].rearrange("p (h d) -> p h d", h=8), ps,
                                                       bcast(inv.unsqueeze(2), [P, 8, DH]), ALU.mult), tok))
                return (t_o[-1],)
            G4 = Q_HEADS // KV_HEADS
            attention(t, Q_HEADS, nk, lambda h, t=t: q_cols[(h % 2) * DH:(h % 2 + 1) * DH, h // 2, t * P:(t + 1) * P],
                      lambda h: key_cols[(h % 2) * DH:(h % 2 + 1) * DH, h // G4, 0:nk],
                      lambda h, j: val_rows[:, j, (h // G4) * DH:(h // G4 + 1) * DH],
                      DH ** -0.5, None, finish, bufs, *t_qkv)
        t_conv = conformer(x_cols, l, o_conv, t_cols)
        return merge(l, o_attn, o_conv, rows, [*t_o, t_conv, t_gate])

    def peer(l, rows, stream, t_in):
        fresh()
        spread_gate(l, stream, 5 * KD, t_in)
        t_cols = modulated_cols(x_cols, rows, l, 3 * KD, stream, [t_in])
        top[0] = 0
        p.stage()
        HT = PEER_H * PEER_TOP
        slots = room([3, SEQ])
        kept = top[0]
        q = room([PEER_H, SEQ])
        keys = room([PEER_H, PEER_K])
        s_k = ctx.enter_context(nc.semaphore(f"peer_keys_loaded_{l}{stream}"))
        p.wait("scalar", [p.latest("vector"), p.latest("tensor")])
        p.dma("scalar", keys, A["peer_keys_t"][l], s_k)
        t_q = []
        announce_chunks(A["peer_wq_2"][l], *[(j * CHUNK, CHUNK) for j in range(4)])
        for j in range(4):
            b = 4 + j % 2
            ps, done = project_cols(x_cols, b, *t_cols)
            t_q.append(copy_out(q[:, 2 * j:2 * j + 2, :], ps, done))
            bank_free[b] = (t_q[-1],)
        NS = 2 * PEER_H
        score = room([NS, PEER_K])
        best2 = room([NS, PEER_TOP])
        key_u = room([NS, PEER_TOP], dt=U32)
        key_f = room([NS, PEER_TOP])
        cand = room([PEER_H, PEER_TOP, PEER_TOP])
        pick = room([HT, PEER_TOP])
        best, place_u = room([PEER_H, PEER_TOP]), room([PEER_H, PEER_TOP], dt=U32)
        row_u, col_u = room([HT], dt=U32), room([HT], dt=U32)
        row_f, col_f = room([HT]), room([HT])
        chosen = room([2, HT])
        wsum = room([PEER_H])

        def top16(values, best, index, after):
            n = len(values)
            for i in range(n):
                after = V(lambda e, i=i: e.max(best(i)[:, 0:8], values[i]), after)
            for i in range(n):
                after = V(lambda e, i=i: e.max_index(index(i)[:, 0:8], best(i)[:, 0:8], values[i]), after)
            for i in range(n):
                after = V(lambda e, i=i: e.match_replace(values[i], best(i)[:, 0:8], values[i], LOWEST), after)
            for i in range(n):
                after = V(lambda e, i=i: e.max(best(i)[:, 8:16], values[i]), after)
            for i in range(n):
                after = V(lambda e, i=i: e.max_index(index(i)[:, 8:16], best(i)[:, 8:16], values[i]), after)
            return after

        t_slots = []
        for t in range(NT):
            ts = slice(t * P, (t + 1) * P)
            for b in range(4):
                c, h0 = b % 2, b // 2 * 4
                half = c * DH
                for h in range(h0, h0 + 4):
                    done = PE(lambda e: e.matmul(
                        psum[b][:, (h - h0) * P:(h - h0 + 1) * P], q[half:half + DH, h, ts],
                        keys[half:half + DH, h, :], start=True, stop=True), *t_q, (s_k, 16), *bank_free[b])
                tok = copy_out(score[:, 2 * h0 + c:2 * h0 + c + 7:2, :],
                               psum[b][:, :].rearrange("p (i k) -> p i k", k=PEER_K), done, p.latest("vector"))
                bank_free[b] = (tok,)
            tok = top16([score[:, i, :] for i in range(NS)], lambda i: best2[:, i, :], lambda i: key_u[:, i, :],
                        p.latest("scalar"))
            tok = V(lambda e: e.tensor_copy(key_f, key_u), tok)
            for h in range(PEER_H):
                shape = [P, PEER_TOP, PEER_TOP]
                tok = V(lambda e, h=h, shape=shape: e.tensor_tensor(
                    cand[:, h], bcast(best2[:, 2 * h, :].unsqueeze(2), shape),
                    bcast(best2[:, 2 * h + 1, :].unsqueeze(1), shape), ALU.add), tok)
            tok = top16([cand[:, h].rearrange("p a b -> p (a b)") for h in range(PEER_H)],
                        lambda h: best[:, h, :], lambda h: place_u[:, h, :], tok)
            w3 = best
            tok = V(lambda e: e.tensor_copy(wsum, best[:, :, 0]), tok)
            tok = V(lambda e: e.tensor_tensor(w3, w3, bcast(wsum.unsqueeze(2), [P, PEER_H, PEER_TOP]),
                                              ALU.subtract), tok)
            tok = S(lambda e: e.activation(w3, w3, ACT.Exp), tok)
            tok = V(lambda e: e.tensor_reduce(wsum, w3, AX_X, ALU.add), tok)
            tok = V(lambda e: e.reciprocal(wsum, wsum), tok)
            tok = V(lambda e: e.tensor_tensor(w3, w3, bcast(wsum.unsqueeze(2), [P, PEER_H, PEER_TOP]),
                                              ALU.mult), tok)
            flat_u = place_u.rearrange("p h k -> p (h k)")
            tok = V(lambda e: e.tensor_scalar(row_u, flat_u, 4, None, ALU.logical_shift_right), tok)
            tok = V(lambda e: e.tensor_scalar(col_u, flat_u, 15, None, ALU.bitwise_and), tok)
            tok = V(lambda e: e.tensor_copy(row_f, row_u), tok)
            tok = V(lambda e: e.tensor_copy(col_f, col_u), tok)
            for c, place in enumerate((row_f, col_f)):
                tok = V(lambda e: e.tensor_tensor(
                    pick, bcast(iota[:, 0:PEER_TOP].unsqueeze(1), [P, HT, PEER_TOP]),
                    bcast(place.unsqueeze(2), [P, HT, PEER_TOP]), ALU.is_equal), tok)
                for h in range(PEER_H):
                    ph = pick[:, h * PEER_TOP:(h + 1) * PEER_TOP, :]
                    tok = V(lambda e, ph=ph, i=2 * h + c: e.tensor_tensor(
                        ph, ph, bcast(key_f[:, i, :].unsqueeze(1), [P, PEER_TOP, PEER_TOP]), ALU.mult), tok)
                tok = V(lambda e, c=c: e.tensor_reduce(chosen[:, c, :], pick, AX_X, ALU.add), tok)
            for i, src in enumerate((chosen[:, 0, :], chosen[:, 1, :], w3.rearrange("p h k -> p (h k)"))):
                done = PE(lambda e, i=i, src=src: e.transpose(psum[6][:, i * P:(i + 1) * P], src, ident[:]),
                          tok, *bank_free[6])
            tok = copy_out(slots[:, :, ts], psum[6][:, 0:3 * P].rearrange("p (i t) -> p i t", i=3), done)
            bank_free[6] = (tok,)
            t_slots.append(tok)

        p.stage()
        top[0] = kept
        NQ = 4
        KQ = PEER_K // NQ
        TB = SEQ // KQ
        dense = [room([SEQ, KQ]) for _ in range(2)]
        hot2 = [room([TB, PEER_K], dt=BF16) for _ in range(2)]
        apart = room([TB, PEER_K], dt=BF16)
        hot1 = room([TB, KQ], dt=BF16)
        hot1w = [room([TB, 3, KQ], dt=BF16) for _ in range(2)]
        w_parts = room([3, SEQ], dt=BF16)
        act = [room([SEQ]) for _ in range(2)]
        scaled = room([SEQ])
        w_rest = act[0]
        tok = V(lambda e: e.tensor_copy(w_parts[:, 0, :], slots[:, 2, :]), *t_slots)
        tok = V(lambda e: e.tensor_tensor(w_rest, slots[:, 2, :], w_parts[:, 0, :], ALU.subtract), tok)
        tok = V(lambda e: e.tensor_copy(w_parts[:, 1, :], w_rest), tok)
        tok = V(lambda e: e.tensor_tensor(w_rest, w_rest, w_parts[:, 1, :], ALU.subtract), tok)
        t_parts = V(lambda e: e.tensor_copy(w_parts[:, 2, :], w_rest), tok)
        dense_tok, read_dense = {}, {}
        hot_free, hot2_tok, hot1_tok = {}, {}, {}
        relu_tok = [()]

        S2 = [P, TB, PEER_K]

        def key_slots(n, c):
            t0 = n % KQ * TB
            return slots[:, c, t0:t0 + TB].unsqueeze(2)

        def second_distance(n):
            tok = G(lambda e: e.tensor_tensor(apart, bcast(iota[:].unsqueeze(1), S2), bcast(key_slots(n, 1), S2),
                                              ALU.subtract), *t_slots, *relu_tok[0])
            hot2_tok[n] = G(lambda e: e.tensor_tensor(apart, apart, apart, ALU.mult), tok)

        def second_hots(n):
            hot2_tok[n] = S(lambda e: e.activation(hot2[n % 2], apart, ACT.Relu, bias=1.0, scale=-1.0),
                            hot2_tok[n], *hot_free.get(n - 2, ()))
            relu_tok[0] = (hot2_tok[n],)

        def second_hots_at_once(n):
            hot2_tok[n] = V(lambda e: e.tensor_tensor(hot2[n % 2], bcast(iota[:].unsqueeze(1), S2),
                                                      bcast(key_slots(n, 1), S2), ALU.is_equal),
                            *t_slots, *hot_free.get(n - 2, ()))

        def first_hots(n):
            qt, t0 = n // KQ, n % KQ * TB
            s1, s3 = [P, TB, KQ], [P, TB, 3, KQ]
            tok = V(lambda e: e.tensor_tensor(hot1, bcast(iota[:, qt * KQ:(qt + 1) * KQ].unsqueeze(1), s1),
                                              bcast(key_slots(n, 0), s1), ALU.is_equal), *t_slots)
            parts = w_parts[:, :, t0:t0 + TB].rearrange("p c t -> p t c")
            hot1_tok[n] = V(lambda e: e.tensor_tensor(hot1w[n % 2], bcast(hot1.unsqueeze(2), s3),
                                                      bcast(parts.unsqueeze(3), s3), ALU.mult),
                            tok, t_parts, *hot_free.get(n - 2, ()))

        def build_batch(n):
            qt, j = divmod(n, KQ)
            i, t0, b = n % 2, j * TB, 2 + n % 2
            for m in range(TB):
                for c in range(3):
                    f = lambda e: e.matmul(psum[b][:, m * KQ:(m + 1) * KQ], hot2[i][:, m, :], hot1w[i][:, m, c, :],
                                           start=(c == 0), stop=(c == 2))
                    if m == TB - 1 and c == 2:
                        done = PE(f)
                    else:
                        p.quiet("tensor", f, hot2_tok[n], hot1_tok[n], *bank_free[b])
            hot_free[n] = (done,)
            tok = S(lambda e: e.activation(dense[qt % 2][:, t0:t0 + TB, :],
                                           psum[b][:, 0:TB * KQ].rearrange("p (t k) -> p t k", t=TB), ACT.Copy),
                    done, *read_dense.get(qt - 2, ()))
            bank_free[b] = (tok,)
            dense_tok[qt] = tok

        for n in range(KQ):
            second_hots_at_once(n)
            first_hots(n)
            build_batch(n)

        scaled_tok, scaled_free = {}, {}
        us = [(A["peer_u_t"][l, i].rearrange("p (k e) -> p k e", k=KD), (KD, P)) for i in range(PEER_K)]
        vs = [(A["peer_v_2"][l, i * P:(i + 1) * P, :], (D,)) for i in range(PEER_K)]
        for i in range(PEER_K + 2):
            announce(*us[i:i + 1], *(vs[i - 2:i - 1] if i >= 2 else ()))

        def scaled_parts(i1):
            return at(hidden_parts[i1 % 2], slice(None), i1 // 2 % 2)

        def hidden(i1):
            ut, number, tw = take((KD, P))
            b = i1 % 2
            done = product3(psum[b][:, 0:SEQ], [(at(ut, slice(None), k), at(x_cols, slice(None), k))
                                                for k in range(KD)], tw, *t_cols, *bank_free[b])
            release_splits([number], done)
            return done

        def weigh(i1, done):
            b = i1 % 2
            tok = S(lambda e: e.activation(act[b], psum[b][:, 0:SEQ], ACT.Gelu), done, scaled_tok.get(i1 - 2, done))
            bank_free[b] = (tok,)
            qt, kk = divmod(i1, KQ)
            tok = V(lambda e: e.tensor_tensor(scaled, act[b], dense[qt % 2][:, :, kk], ALU.mult),
                    tok, dense_tok[qt])
            read_dense[qt] = (tok,)
            scaled_tok[i1] = split(scaled_parts(i1), scaled, tok, *scaled_free.get(i1 - 4, ()))

        def outputs(i1):
            vt, number, tw = take((D,))
            for t in range(NT):
                for h in range(2):
                    b = 4 + 2 * t + h
                    w0 = (scaled_tok[i1], tw) + (tuple(bank_free[b]) if i1 == 0 else ())
                    x = at(scaled_parts(i1), slice(None), slice(t * P, (t + 1) * P))
                    y = at(vt, slice(None), slice(h * 512, (h + 1) * 512))
                    for n, (xx, yy) in enumerate(((x[0], y[0]), (x[0], y[1]), (x[1], y[0]))):
                        done = PE(lambda e: e.matmul(psum[b][:, :], xx, yy, start=(i1 == 0 and n == 0),
                                                     stop=(i1 == PEER_K - 1 and n == 2)), *w0)
            release_splits([number], done)
            scaled_free[i1] = (done,)
            return done

        second_distance(KQ)
        second_hots(KQ)
        first_hots(KQ)
        second_distance(KQ + 1)
        for i in range(PEER_K + 2):
            n = i + KQ
            if i < PEER_K:
                done_h = hidden(i)
            if n + 1 < PEER_K:
                second_hots(n + 1)
                first_hots(n + 1)
            if n + 2 < PEER_K:
                second_distance(n + 2)
            if i >= 2:
                done = outputs(i - 2)
            if i < PEER_K:
                weigh(i, done_h)
            if n < PEER_K:
                build_batch(n)
        top[0] -= 2 * SEQ + SEQ
        part = room([BANK])
        for t in range(NT):
            for h in range(2):
                b = 4 + 2 * t + h
                hs = slice(h * 512, (h + 1) * 512)
                tok = V(lambda e, b=b, hs=hs: e.tensor_tensor(part, psum[b][:, :], gate_row[:, hs], ALU.mult),
                        done)
                bank_free[b] = (tok,)
                tok = V(lambda e, t=t, hs=hs: e.tensor_tensor(rows[:, t, hs], rows[:, t, hs], part, ALU.add), tok)
        return tok

    def second(t_in):
        fresh()
        t_mod = modulation()
        t_c = attend(0, ctx_rows, 1, SEQ, [t_ctx, t_mod])
        t_c = peer(0, ctx_rows, 1, t_c)
        t_x = p.latest("vector")
        for l in range(DEPTH):
            if l == 1:
                fresh()
                t_cc = modulated_cols(x_cols, ctx_rows, l, 0, 1, [t_c])
                fresh()
                qkv(x_cols, l, False, False, 0, t_cc)
            t_x = attend(l, x_rows, 0, 2 * SEQ, [t_x])
            t_x = peer(l, x_rows, 0, t_x)
        fresh()
        scratch = room([D])
        sv, fg, t_fg = vector_row(A["final_g_2"])
        toks = []
        for t in range(NT):
            r, tok = rms_factor(x_rows[:, t, :], D, scratch, RMS_EPS, t_x)
            toks.append(V(lambda e, t=t, r=r: e.scalar_tensor_tensor(
                out=x_rows[:, t, :], in0=x_rows[:, t, :], scalar=r, in1=fg[:, :], op0=ALU.mult, op1=ALU.mult),
                tok, t_fg))
        store(x_rows[:], *toks)

    t_in = mixer_0()
    t_in = moe(0, t_in)
    t_in = mixer_1(t_in)
    t_in = moe(1, t_in)
    second(t_in)


def host_layout(inputs):
    a = {n: np.asarray(v) for n, v in inputs.items()}

    def tiles(v):
        return v.reshape(NT, P, -1).transpose(1, 0, 2)

    d = {n: a[n] for n in (
        "ab_w_in", "ab_gm_ln_g", "ab_gm_ln_b", "ab_mla_q_norm", "ab_mla_kv_norm", "ab_mla_w_uq",
        "ab_mla_w_uk", "ab_mla_w_uv", "ab_w_o", "moe_w_down", "ln1_g", "ln1_b", "ln2_g", "ln2_b")}
    d["x"], d["ctx_2"] = tiles(a["x"]), tiles(a["ctx_2"])
    d["positions"] = a["positions"].reshape(NT, P).T
    d["gm_ws_t"] = a["ab_gm_ws"][0].transpose(0, 2, 1)
    d["gm_bs_t"] = a["ab_gm_bs"][0].T
    d["router_w"] = np.concatenate([a["moe_w_rg"], a["moe_w_re"]], axis=-1)
    d["router_b"] = np.concatenate([a["moe_b_rg"], a["moe_b_re"]], axis=-1)
    for new, old in (("moe_gate", "moe_w_gate"), ("moe_up", "moe_w_up")):
        w = a[old].reshape(DEPTH, N_EXP, KD, P, MOE_HID // P, P)
        d[new] = w.transpose(0, 1, 4, 3, 2, 5).reshape(DEPTH, N_EXP, MOE_HID // P, P, KD * P)

    d["c_swap"] = np.roll(np.eye(P, dtype=np.float32), P // 2, 0)
    d["c_ident"] = np.eye(P, dtype=np.float32)
    d["c_iota"] = np.tile(np.arange(P, dtype=np.float32), (P, 1))
    d["c_upper"] = np.triu(np.ones((P, P), np.float32))
    q = np.arange(SEQ)
    d["c_causal"] = tiles(np.where(q[:, None] >= q[None, :], 0.0, NEG).astype(np.float32))
    half = ROPE // 2
    f = np.exp(np.float32(-math.log(10000.0)) * np.arange(half, dtype=np.float32) / np.float32(half))
    d["c_freq"] = np.tile(f.astype(np.float32), (P, 1))
    for n in ("c_w_in", "c_w_ck1", "c_w_ck2", "c_w_cv1", "c_w_cv2", "c_gate_b", "c_w_o", "w_mod_2", "w_in_2",
              "q_gain_2", "k_gain_2", "ln_g_2", "ln_b_2", "w_o_2", "peer_wq_2", "peer_v_2", "final_g_2"):
        d[n] = a[n]
    d["cmp_pos_t"] = a["c_cmp_pos"][0].transpose(2, 0, 1)
    end = np.arange(N_CMP) * CMP_STRIDE + CMP_LEN - 1
    ended = q[:, None] >= end[None, :]
    none = np.broadcast_to(~ended.any(1, keepdims=True), ended.shape)
    d["c_cmp_mask"] = np.stack([tiles(m.astype(np.float32)) for m in (np.where(ended, 0.0, NEG), ended, none)], 2)
    cond = np.stack([a["c_2"][0], a["c_ctx_2"]], -1)
    d["cond"] = cond.reshape(KD, P, 2).transpose(1, 0, 2)
    d["b_mod_t"] = a["b_mod_2"].reshape(DEPTH, 6 * KD, P).transpose(2, 0, 1)
    n4 = DH // 4
    inv = (np.float32(10000.0) ** (-np.arange(n4, dtype=np.float32) / np.float32(n4))).astype(np.float32)
    row, col = (np.repeat(np.arange(SEQ // 64), 64), np.tile(np.arange(64), SEQ // 64))
    ang = np.concatenate([row[:, None].astype(np.float32) * inv, col[:, None].astype(np.float32) * inv], -1)
    d["c_rope_cos"] = tiles(np.cos(ang).astype(np.float32))
    d["c_rope_sin"] = tiles(np.sin(ang).astype(np.float32))
    wb = np.concatenate([a["conv_w_2"], a["conv_b_2"][:, None, :]], 1)
    d["conv_wb_t"] = wb.reshape(DEPTH, CONV_K + 1, CONV_W // P, P).transpose(0, 3, 2, 1)
    beta = np.concatenate([a["beta_attn_2"], a["beta_conv_2"]], -1)
    d["beta_t"] = beta.reshape(DEPTH, KD, P).transpose(0, 2, 1)
    pk = a["peer_keys_2"]
    d["peer_keys_t"] = pk.transpose(0, 2, 4, 1, 3).reshape(DEPTH, P, PEER_H, PEER_K)
    u = a["peer_u_2"].reshape(DEPTH, PEER_K, P, KD, P)
    d["peer_u_t"] = u.transpose(0, 1, 4, 3, 2).reshape(DEPTH, PEER_K, P, D)
    return {n: np.ascontiguousarray(v) for n, v in d.items()}


def kernel(**inputs):
    import concourse.bacc as bacc
    from concourse.bass_utils import run_bass_kernel_spmd

    nc = bacc.Bacc("TRN2", target_bir_lowering=False, num_devices=1)
    arrays, aps = {}, {}
    for name, a in host_layout(inputs).items():
        arrays[f"in_{name}"] = a
        aps[name] = nc.dram_tensor(f"in_{name}", a.shape, mybir.dt.from_np(a.dtype), kind="ExternalInput").ap()
    out = nc.dram_tensor("out_0_dram", (1, SEQ, D), F32, kind="ExternalOutput").ap()
    build(nc, aps, out)
    r = run_bass_kernel_spmd(nc, [arrays], core_ids=[0])
    return r.results[0]["out_0_dram"]
```

```python
import math
from contextlib import ExitStack

import numpy as np

import concourse.bass as bass
from concourse import mybir

F32 = mybir.dt.float32
F32R = mybir.dt.float32r
F16 = mybir.dt.float16
U32 = mybir.dt.uint32
I32 = mybir.dt.int32
ALU = mybir.AluOpType
ACT = mybir.ActivationFunctionType
AX_X = mybir.AxisListType.X

P = 128
SEQ = 256
NT = SEQ // P
D = 1024
KD = D // P
CHUNK = 256
BANK = 512
UNIT = 1024
LOWEST = -3.0e38
NEG = -1e30
LN_EPS = 1e-5
RMS_EPS = 1e-6
DEPTH = 2
ALPHA = (2.0 * DEPTH) ** 0.25

GM_W, GM_G = 512, 4
Q_RANK, KV_RANK, ROPE = 256, 128, 32
MLA_H, NOPE, MLA_V = 8, 64, 64
MLA_D = NOPE + ROPE
NSA_H, NSA_G, DH = 16, 2, 64
CMP_LEN, CMP_STRIDE, CMP_HID = 32, 16, 256
N_CMP = SEQ // CMP_STRIDE - CMP_LEN // CMP_STRIDE + 1
MOE_G, MOE_E, MOE_HID = 4, 8, 256
N_EXP = MOE_G * MOE_E

Q_HEADS, KV_HEADS = 8, 2
QW, KVW, CONV_W, CONV_K = 512, 128, 512, 31
PEER_H, PEER_K, PEER_TOP = 8, 128, 16


class Program:

    def __init__(self, nc, ctx):
        self.nc, self.ctx = nc, ctx
        self.engine = {"tensor": nc.tensor, "vector": nc.vector, "scalar": nc.scalar,
                       "gpsimd": nc.gpsimd, "sync": nc.sync}
        self.done = {e: ctx.enter_context(nc.semaphore(f"{e}_done")) for e in self.engine}
        self.count = {e: 0 for e in self.engine}
        self.passed = {e: {} for e in self.engine}

    def wait(self, engine, tokens):
        for sem, value in tokens:
            if value > self.passed[engine].get(sem.name, 0):
                self.passed[engine][sem.name] = value
                self.engine[engine].wait_ge(sem, value)

    def op(self, engine, issue, *after, beside=False):
        if engine != "tensor" and self.count[engine] and not beside:
            after += ((self.done[engine], self.count[engine]),)
        self.wait(engine, after)
        self.count[engine] += 1
        issue(self.engine[engine]).then_inc(self.done[engine], 1)
        return (self.done[engine], self.count[engine])

    def quiet(self, engine, issue, *after):
        self.wait(engine, after)
        issue(self.engine[engine])

    def dma(self, queue, dst, src, sem):
        self.engine[queue].dma_start(dst, src).then_inc(sem, 16)

    def latest(self, engine):
        return (self.done[engine], self.count[engine])

    def stage(self):
        tokens = [t for t in map(self.latest, ("tensor", "vector", "scalar", "gpsimd")) if t[1]]
        for e in ("tensor", "vector", "scalar", "gpsimd"):
            self.wait(e, tokens)


class Ring:

    def __init__(self, prog, name, queue, slots, width):
        self.prog, self.queue, self.n = prog, queue, slots
        self.buf = [prog.ctx.enter_context(prog.nc.sbuf_tensor(f"{name}{i}", [P, width], F32))
                    for i in range(slots)]
        self.sem = [prog.ctx.enter_context(prog.nc.semaphore(f"{name}_filled{i}"))
                    for i in range(slots)]
        self.fills = [0] * slots
        self.free = [()] * slots
        self.at = 0

    def load(self, *moves):
        s = self.at % self.n
        self.at += 1
        assert self.free[s] is not None, "the slot is in use"
        self.prog.wait(self.queue, self.free[s])
        self.free[s] = None
        for source, place in moves:
            self.fills[s] += 16
            self.prog.dma(self.queue, place(self.buf[s]), source, self.sem[s])
        return s, self.buf[s], (self.sem[s], self.fills[s])

    def release(self, s, *tokens):
        self.free[s] = tokens


def build(nc, A, out):
    with ExitStack() as ctx:
        _build(nc, ctx, A, out)


def _build(nc, ctx, A, out):
    p = Program(nc, ctx)

    def sb(name, shape, dt=F32):
        return ctx.enter_context(nc.sbuf_tensor(name, shape, dt))

    def PE(f, *after):
        return p.op("tensor", f, *after)

    def V(f, *after):
        return p.op("vector", f, *after)

    def V_beside(f, *after):
        return p.op("vector", f, *after, beside=True)

    def S(f, *after):
        return p.op("scalar", f, *after)

    def G_beside(f, *after):
        return p.op("gpsimd", f, *after, beside=True)

    def G(f, *after):
        return p.op("gpsimd", f, *after)

    psum = [ctx.enter_context(nc.psum_tensor(f"bank{i}", [P, BANK], F32)) for i in range(8)]
    bank_free = [() for _ in range(8)]

    weights = Ring(p, "weight", "sync", 5, UNIT)
    vectors = Ring(p, "vector_param", "gpsimd", 2, D)

    def pair(name, shape):
        return sb(name + "_hi", shape, F32R)[:], sb(name + "_lo", shape, F32R)[:]

    SPLITS = 5
    splits = [pair(f"split{i}", [P, UNIT]) for i in range(SPLITS)]
    split_free = [() for _ in range(SPLITS)]
    split_at = [0]

    x_rows = sb("x_rows", [P, NT, D])
    ctx_rows = sb("ctx_rows", [P, NT, D])
    x_cols = pair("x_cols", [P, KD, SEQ])
    hidden_parts = [pair(f"hidden{i}", [P, 2, SEQ]) for i in range(2)]
    ident = sb("ident", [P, P])
    ones = sb("ones", [P, P])
    iota = sb("iota", [P, P])
    causal = sb("causal", [P, NT, SEQ])
    ARENA = 21376
    arena = sb("arena", [P, ARENA])
    top = [0]

    def fresh():
        p.stage()
        top[0] = 0

    def room(shape, parts=P, dt=F32):
        n = int(np.prod(shape))
        a = arena[0:parts, top[0]:top[0] + n]
        top[0] += n
        assert top[0] <= ARENA, top[0]
        if dt is F16:
            a = a[:, 0:n // 2]
            top[0] -= n // 2
        if dt is not F32:
            a = a.bitcast(dt)
        if len(shape) == 2:
            a = a.rearrange("p (a b) -> p a b", a=shape[0])
        elif len(shape) == 3:
            a = a.rearrange("p (a b c) -> p a b c", a=shape[0], b=shape[1])
        elif len(shape) == 4:
            a = a.rearrange("p (a b c d) -> p a b c d", a=shape[0], b=shape[1], c=shape[2])
        return a

    def constant(name, tile):
        s = ctx.enter_context(nc.semaphore(f"{name}_loaded"))
        p.dma("scalar", tile, A[name], s)
        return (s, 16)

    t_ident = constant("c_ident", ident[:])
    t_iota = constant("c_iota", iota[:])
    t_causal = constant("c_causal", causal[:])
    t_ones = V(lambda e: e.memset(ones[:], 1.0))
    t_x = constant("x", x_rows[:])

    def bcast(ap, shape):
        return ap.broadcast_to(shape)

    def product(bank_ap, pairs, *after):
        for i, (lhsT, rhs, *tok) in enumerate(pairs):
            last = i == len(pairs) - 1
            f = lambda e, l=lhsT, r=rhs, a=(i == 0), z=last: e.matmul(bank_ap, l, r, start=a, stop=z)
            if last:
                return PE(f, *after, *tok)
            p.quiet("tensor", f, *after, *tok)

    def product3(bank_ap, pairs, *after):
        return product(bank_ap, [x for (l, r, *tok) in pairs for x in
                                 ((l[0], r[0], *tok), (l[0], r[1]), (l[1], r[0]))], *after)

    def at(parts, *index):
        return parts[0][index], parts[1][index]

    def split(parts, src, *after, engine=V):
        tok = S(lambda e: e.activation(parts[0], src, ACT.Copy), *after)
        return engine(lambda e: e.tensor_tensor(parts[1], src, parts[0].bitcast(F32), ALU.subtract), tok)

    announced, landed, ready = [], [], []

    def announce(*units):
        announced.extend(units)

    def shaped(buf, shape):
        n = int(np.prod(shape))
        return buf[:, 0:n] if len(shape) == 1 else buf[:, 0:n].rearrange("p (a b) -> p a b", a=shape[0])

    def feed(engine=V):
        moved = True
        while moved:
            moved = False
            if announced and weights.free[weights.at % weights.n] is not None:
                source, shape = announced.pop(0)
                landed.append((shape, weights.load((source, lambda b: shaped(b, shape)))))
                moved = True
            i = split_at[0] % SPLITS
            if landed and split_free[i] is not None:
                shape, (s, buf, tok) = landed.pop(0)
                parts = shaped(splits[i][0], shape), shaped(splits[i][1], shape)
                tok = split(parts, shaped(buf, shape), tok, *split_free[i], engine=engine)
                weights.release(s, tok)
                split_free[i] = None
                split_at[0] += 1
                ready.append((parts, i, tok))
                moved = True

    def take(shape, fed=True):
        if fed:
            feed()
        unit = ready.pop(0)
        assert list(unit[0][0].shape[1:]) == list(shape), (unit[0][0].shape, shape)
        return unit

    evac_turn = [0]

    def copy_out(dst, src, *after):
        evac_turn[0] += 1
        if evac_turn[0] % 2:
            return S(lambda e: e.activation(dst, src, ACT.Copy), *after)
        return V(lambda e: e.tensor_copy(dst, src), *after)

    def to_cols(dst, rows, n, banks, *after, evac=None):
        tokens = []
        for j, k0 in enumerate(range(0, n, 2)):
            b = banks[j % len(banks)]
            ks = range(k0, min(k0 + 2, n))
            for k in ks:
                for t in range(NT):
                    o = psum[b][:, (k - k0) * SEQ + t * P:(k - k0) * SEQ + (t + 1) * P]
                    tok = PE(lambda e, o=o, i=rows(k, t): e.transpose(o, i, ident[:]),
                             *after, t_ident, *bank_free[b])
            src = psum[b][:, 0:len(ks) * SEQ].rearrange("p (k t) -> p k t", t=SEQ)
            if evac is not None:
                done = [evac(k0, src, tok)]
            elif isinstance(dst, tuple):
                done = [split(at(dst, slice(None), slice(k0, k0 + len(ks))), src, tok)]
            else:
                done = [copy_out(dst[:, k0:k0 + len(ks), :], src, tok)]
            bank_free[b] = tuple(done)
            tokens += done
        return tokens

    HK = KD // 2

    def announce_chunks(w, *chunks):
        for c0, cn in chunks:
            announce(*[(w[i * HK * P:(i + 1) * HK * P, c0:c0 + cn].rearrange("(k p) n -> p k n", p=P), (HK, cn))
                       for i in range(2)])

    def take_chunk(cn):
        units = [take((HK, cn)) for _ in range(2)]
        return (lambda k, cols: at(units[k // HK][0], slice(None), k % HK, cols),
                [u[1] for u in units], [u[2] for u in units])

    def release_splits(numbers, *tokens):
        for i in numbers:
            split_free[i] = tokens

    def project_rows(cols, cn, bank, *after):
        wt, numbers, tok = take_chunk(cn)
        for t in range(NT):
            o = psum[bank][:, t * CHUNK:t * CHUNK + cn]
            done = product3(o, [(at(cols, slice(None), k, slice(t * P, (t + 1) * P)), wt(k, slice(0, cn)))
                                for k in range(KD)], *after, *tok, *bank_free[bank])
        release_splits(numbers, done)
        return psum[bank][:].rearrange("p (t n) -> p t n", t=NT)[:, :, 0:cn], done

    def project_cols(cols, bank, *after):
        wt, numbers, tok = take_chunk(CHUNK)
        for j in range(2):
            o = psum[bank][:, j * SEQ:(j + 1) * SEQ]
            done = product3(o, [(wt(k, slice(j * P, (j + 1) * P)), at(cols, slice(None), k)) for k in range(KD)],
                            *after, *tok, *bank_free[bank])
        release_splits(numbers, done)
        return psum[bank][:].rearrange("p (j t) -> p j t", j=2), done

    def vector_row(*sources):
        at, moves = 0, []
        for v in sources:
            n = v.shape[0]
            moves.append((v.partition_broadcast(P), lambda b, a=at, n=n: b[:, a:a + n]))
            at += n
        return vectors.load(*moves)

    small = sb("small", [P, 128])
    small_at = [0]

    def tiny(n):
        if small_at[0] + n > 128:
            small_at[0] = 0
        a = small[:, small_at[0]:small_at[0] + n]
        small_at[0] += n
        return a

    def inv_root(dst, src, eps, *after):
        tok = V(lambda e: e.tensor_scalar(dst, src, eps, None, ALU.add), *after)
        tok = S(lambda e: e.activation(dst, dst, ACT.Sqrt), tok)
        return V(lambda e: e.reciprocal(dst, dst), tok)

    def normalise(dst, src, width, *after):
        n = -(-width // 512)
        w = width // n
        stats, mv, rstd = tiny(6 * n), tiny(2), tiny(1)
        for i in range(n):
            tok = V(lambda e, i=i: e.bn_stats(stats[:, 6 * i:6 * i + 6], src[:, w * i:w * (i + 1)]),
                    *after)
        tok = V(lambda e: e.bn_aggr(mv, stats), tok)
        tok = inv_root(rstd, mv[:, 1:2], LN_EPS, tok)
        return V(lambda e: e.tensor_scalar(dst, src, mv[:, 0:1], rstd, ALU.subtract, ALU.mult), tok)

    def rms_factor(src, width, scratch, eps, *after):
        ms, r = tiny(1), tiny(1)
        tok = V(lambda e: e.tensor_tensor_reduce(scratch, src, src, 1.0 / width, 0.0, ALU.mult,
                                                 ALU.add, ms), *after)
        return r, inv_root(r, ms, eps, tok)

    def affine_rows(rows, g, b, scratch_tok):
        sg, bg, tg = vector_row(g)
        sb_, bb, tb = vector_row(b)
        toks = []
        for t in range(NT):
            a = V(lambda e, t=t: e.tensor_tensor(rows[:, t, :], rows[:, t, :], bg[:, 0:g.shape[0]], ALU.mult),
                  scratch_tok[t], tg)
            toks.append(V(lambda e, t=t: e.tensor_tensor(rows[:, t, :], rows[:, t, :], bb[:, 0:g.shape[0]],
                                                         ALU.add), a, tb))
        vectors.release(sg, toks[-1])
        vectors.release(sb_, toks[-1])
        return toks

    def post_norm(g, b, residual_toks):
        toks = [normalise(x_rows[:, t, :], x_rows[:, t, :], D, residual_toks[t]) for t in range(NT)]
        spare(2)
        return affine_rows(x_rows, g, b, toks)

    def add_scaled_residual(c0, cn, ps, done):
        return [V(lambda e, t=t: e.scalar_tensor_tensor(
            out=x_rows[:, t, c0:c0 + cn], in0=x_rows[:, t, c0:c0 + cn], scalar=ALPHA,
            in1=ps[:, t, :], op0=ALU.mult, op1=ALU.add), done) for t in range(NT)]

    def attention(tile, heads, nk, q_of, k_of, v_of, scale, mask, finish, bufs, *after, beside=lambda: None):
        masked, prob, prob_t, neg_max, sums = bufs
        hg = BANK // nk
        kt = nk // P
        n = heads // hg
        order = [h0 + h for h0 in range(0, heads, 8) for h in (0, 2, 4, 6, 1, 3, 5, 7)]
        exp_tok, t_tok, mm_tok = {}, {}, {}
        pt_free, prob_free = {}, {}
        out_free = [(), ()]

        def scores(g):
            b = g % 2
            for i in range(hg):
                tok = PE(lambda e, i=i: e.matmul(psum[b][:, i * nk:(i + 1) * nk], q_of(order[g * hg + i]),
                                                 k_of(order[g * hg + i]), start=True, stop=True),
                         *after, *bank_free[b])
            s3 = psum[b][:].rearrange("p (h k) -> p h k", h=hg)
            h0 = order[g * hg]
            nm = neg_max[:, h0:h0 + 2 * hg - 1:2]
            if mask is not None:
                m3 = masked[b].rearrange("p (h k) -> p h k", h=hg)
                tok = V(lambda e: e.scalar_tensor_tensor(
                    out=m3, in0=s3, scalar=scale, in1=bcast(mask.unsqueeze(1), [P, hg, nk]),
                    op0=ALU.mult, op1=ALU.add), tok, t_causal, *exp_tok.get(g - 2, ()))
                bank_free[b] = (tok,)
                tok = V(lambda e: e.tensor_reduce(nm, m3, AX_X, ALU.max, negate=True), tok)
                src, sc = m3, 1.0
            else:
                tok = V(lambda e: e.tensor_reduce(nm, s3, AX_X, ALU.max, negate=True), tok)
                tok = V(lambda e: e.tensor_scalar(nm, nm, scale, None, ALU.mult), tok)
                src, sc = s3, scale
            pr = prob[g % 3].rearrange("p (h k) -> p h k", h=hg)
            for i in range(hg):
                h = h0 + 2 * i
                tok2 = S(lambda e: e.activation(pr[:, i, :], src[:, i, :], ACT.Exp, bias=neg_max[:, h:h + 1],
                                                scale=sc, accum_out=sums[:, h:h + 1]),
                         tok, *prob_free.get(g - 3, ()))
            if mask is None:
                bank_free[b] = (tok2,)
            exp_tok[g] = (tok2,)

        def flips(g):
            b = 2 + g % 2
            for i in range(4):
                tok = PE(lambda e, i=i: e.transpose(psum[b][:, i * P:(i + 1) * P],
                                                    prob[g % 3][:, i * P:(i + 1) * P], ident[:]),
                         *exp_tok[g], *bank_free[b])
            prob_free[g] = (tok,)
            tok = copy_out(prob_t[g % 3], psum[b][:], tok, *pt_free.get(g - 3, ()))
            bank_free[b] = (tok,)
            t_tok[g] = tok

        def values(g):
            for i in range(hg):
                h = order[g * hg + i]
                b = 4 + (h // 8) % 2
                o = psum[b][:, (h % 8) * DH:(h % 8 + 1) * DH]
                tok = product(o, [(prob_t[g % 3][:, (i * kt + j) * P:(i * kt + j + 1) * P], v_of(h, j))
                                  for j in range(kt)], t_tok[g], *bank_free[b])
                if (g * hg + i) % 8 == 7:
                    h -= h % 8
                    bank_free[b] = finish(h, psum[b][:].rearrange("p (h d) -> p h d", h=8),
                                          sums[:, h:h + 8], tok)
            pt_free[g] = (tok,)

        for g in range(n + 2):
            if g < n:
                scores(g)
                beside()
            if 1 <= g <= n:
                flips(g - 1)
                beside()
            if g >= 2:
                values(g - 2)

    def attention_buffers():
        return ([room([BANK]) for _ in range(2)], [room([BANK]) for _ in range(3)],
                [room([BANK]) for _ in range(3)], room([NSA_H]), room([NSA_H]))

    NMOD = 6 * KD
    mod = [sb(f"mod{l}", [P, NMOD, 2]) for l in range(DEPTH)]
    gate_row = sb("gate_row", [P, D])
    rope_cos, rope_sin = sb("rope_cos", [P, NT, DH // 2]), sb("rope_sin", [P, NT, DH // 2])
    param_sems = {}

    def modulation():
        NC2, COLS = 2 * KD, UNIT // 2
        c2 = ctx_rows[:, 0, 0:NC2].rearrange("p (k s) -> p k s", s=2)
        bm = ctx_rows[:, 0, NC2:NC2 + DEPTH * NMOD].rearrange("p (l m) -> p l m", l=DEPTH)
        rows = ctx_rows[0:2, 1, 0:COLS]
        s_c = ctx.enter_context(nc.semaphore("conditions_loaded"))
        for dst, n in ((c2, "cond"), (bm, "b_mod_t"), (rope_cos[:], "c_rope_cos"), (rope_sin[:], "c_rope_sin")):
            p.dma("scalar", dst, A[n], s_c)
        t_c = S(lambda e: e.activation(c2, c2, ACT.Silu), (s_c, 64))
        for m in (KD, 4 * KD):
            V(lambda e: e.tensor_scalar(bm[:, :, m:m + KD], bm[:, :, m:m + KD], 1.0, None, ALU.add), (s_c, 64))

        def steps():
            before = None
            for l in range(DEPTH):
                for c0 in range(0, NMOD * P, COLS):
                    if before:
                        before = before()
                    for k in range(0, KD, 2):
                        s, buf, tw = weights.load((
                            A["w_mod_2"][l, k * P:(k + 2) * P, c0:c0 + COLS].rearrange("(k p) n -> p k n", p=P),
                            lambda b: b[:, :].rearrange("p (k n) -> p k n", k=2)))
                        for i in range(2):
                            done = PE(lambda e: e.matmul(psum[7][0:2, :], c2[:, k + i, :],
                                                         buf[:, i * COLS:(i + 1) * COLS], start=(k + i == 0),
                                                         stop=(k + i == KD - 1)), t_c, tw, *bank_free[7])
                        weights.release(s, done)
                    tok = S(lambda e: e.activation(rows, psum[7][0:2, :], ACT.Copy), done)
                    bank_free[7] = (tok,)

                    def turn(tok=tok, l=l, m0=c0 // P):
                        n = COLS // P
                        for m in range(n):
                            done = PE(lambda e: e.transpose(psum[7][:, 2 * m:2 * m + 2], rows[:, m * P:(m + 1) * P],
                                                            ident[0:2, 0:2]), tok, t_ident, *bank_free[7])
                        tok = S(lambda e: e.activation(
                            mod[l][:, m0:m0 + n, :], psum[7][:, 0:2 * n].rearrange("p (m s) -> p m s", s=2),
                            ACT.Copy), done)
                        bank_free[7] = (tok,)
                    before = turn
                    yield
            before()
            for l in range(DEPTH):
                V(lambda e: e.tensor_tensor(mod[l][:], mod[l][:], bcast(bm[:, l, :].unsqueeze(2), [P, NMOD, 2]), ALU.add),
                  p.latest("scalar"))
        return steps()

    mod_steps = modulation()

    def spare(n=1):
        for _ in range(n):
            next(mod_steps, None)

    def mixer_0():
        fresh()
        w_in = A["ab_w_in"][0]
        t_cols = to_cols(x_cols, lambda k, t: x_rows[:, t, k * P:(k + 1) * P], KD, (0, 1, 2, 3), t_x)
        u, v = room([NT, GM_W]), room([NT, GM_W])
        cq, ckv = room([NT, Q_RANK]), room([NT, KV_RANK + ROPE])
        mix = room([NT, D])
        toks = {}
        parts_of_h = [(1024, 256, cq, 0), (1280, 160, ckv, 0), (512, 256, v, 0), (768, 256, v, 256),
                      (0, 256, u, 0), (256, 256, u, 256)]
        announce_chunks(w_in, *[(c0, cn) for c0, cn, _, _ in parts_of_h])
        for j, (_, cn, dst, first) in enumerate(parts_of_h):
            b = 4 + j % 2
            ps, done = project_rows(x_cols, cn, b, *t_cols)
            d = dst[:, :, first:first + cn]
            if dst is u or dst is v:
                tok = S(lambda e, d=d, ps=ps: e.activation(d, ps, ACT.Gelu_apprx_tanh), done)
            else:
                tok = V(lambda e, d=d, ps=ps: e.tensor_copy(d, ps), done)
            bank_free[b] = (tok,)
            toks[j] = tok

        half = ROPE // 2
        pos_i, pos = room([NT], dt=I32), room([NT])
        freq = room([half])
        ang, turns, cos, sin = (room([NT, half]) for _ in range(4))
        s_pos = ctx.enter_context(nc.semaphore("positions_loaded"))
        p.wait("scalar", [p.latest("vector")])
        p.dma("scalar", pos_i, A["positions"], s_pos)
        p.dma("scalar", freq, A["c_freq"], s_pos)
        tok = V(lambda e: e.tensor_copy(pos, pos_i), (s_pos, 32))
        tok = V(lambda e: e.tensor_tensor(ang, bcast(pos.unsqueeze(2), [P, NT, half]),
                                          bcast(freq.unsqueeze(1), [P, NT, half]), ALU.mult), tok)
        tok = V(lambda e: e.tensor_scalar(turns, ang, 1.0 / (2 * math.pi), None, ALU.mult), tok)
        magic = 1.5 * 2.0 ** 23
        tok = V(lambda e: e.tensor_scalar(turns, turns, magic, None, ALU.add), tok)
        tok = V(lambda e: e.tensor_scalar(turns, turns, magic, None, ALU.subtract), tok)
        rest = 2 * math.pi
        for bits in (10, 10, None):
            part = rest if bits is None else float(np.floor(rest * 2.0 ** (bits - math.floor(math.log2(rest))))
                                                   / 2.0 ** (bits - math.floor(math.log2(rest))))
            rest -= part
            tok = V(lambda e, c=part: e.scalar_tensor_tensor(out=ang, in0=turns, scalar=-c, in1=ang,
                                                             op0=ALU.mult, op1=ALU.add), tok)
        pi = float(np.nextafter(np.float32(math.pi), np.float32(0)))
        wrap = turns
        t1 = V(lambda e: e.tensor_scalar(cos, ang, math.pi / 2, None, ALU.add), tok)
        t1 = V(lambda e: e.tensor_scalar(wrap, cos, pi, -2 * math.pi, ALU.is_gt, ALU.mult), t1)
        t1 = V(lambda e: e.tensor_tensor(cos, cos, wrap, ALU.add), t1)
        t1 = V(lambda e: e.tensor_scalar(cos, cos, pi, -pi, ALU.min, ALU.max), t1)
        t2 = V(lambda e: e.tensor_scalar(sin, ang, pi, -pi, ALU.min, ALU.max), t1)
        t_cs = S(lambda e: e.activation(cos, cos, ACT.Sin), t2)
        t_cs = S(lambda e: e.activation(sin, sin, ACT.Sin), t2, t_cs)

        scratch = room([GM_W])
        sg, gains, t_gain = vector_row(A["ab_mla_q_norm"][0], A["ab_mla_kv_norm"][0])
        nt = []
        for t in range(NT):
            for src, w, g0, dep in ((cq[:, t, :], Q_RANK, 0, toks[0]), (ckv[:, t, 0:KV_RANK], KV_RANK, Q_RANK, toks[1])):
                r, tok = rms_factor(src, w, scratch[:, 0:w], LN_EPS, dep)
                nt.append(V(lambda e, src=src, r=r, g0=g0, w=w: e.scalar_tensor_tensor(
                    out=src, in0=src, scalar=r, in1=gains[:, g0:g0 + w], op0=ALU.mult, op1=ALU.mult), tok, t_gain))
        vectors.release(sg, nt[-1])
        spare(2)
        lat = room([3, SEQ])
        t_lat = to_cols(lat, lambda k, t: (cq[:, t, k * P:(k + 1) * P] if k < 2 else ckv[:, t, 0:KV_RANK]),
                        3, (0, 1), *nt)
        q_rows, k_rows = room([NT, MLA_H, MLA_D]), room([NT, MLA_H, MLA_D])
        v_rows = room([NT, MLA_H * MLA_V])
        QD = MLA_H * MLA_D
        wqs = [weights.load((A["ab_mla_w_uq"][0, k * P:(k + 1) * P, :], lambda b: b[:, 0:QD])) for k in range(2)]
        s2, wkv, t_wkv = weights.load((A["ab_mla_w_uk"][0], lambda b: b[:, 0:512]),
                                      (A["ab_mla_w_uv"][0], lambda b: b[:, 512:1024]))
        t_rows = []
        for t in range(NT):
            ts = slice(t * P, (t + 1) * P)
            qf = q_rows[:, t].rearrange("p h d -> p (h d)")
            for i in range(2):
                done = product(psum[2 + i][:, 0:QD // 2], [
                    (lat[:, k, ts], wqs[k][1][:, i * QD // 2:(i + 1) * QD // 2], wqs[k][2])
                    for k in range(2)], *t_lat, *bank_free[2 + i])
                bank_free[2 + i] = (copy_out(qf[:, i * QD // 2:(i + 1) * QD // 2], psum[2 + i][:, 0:QD // 2], done),)
                t_rows += bank_free[2 + i]
            for i in range(2):
                done = product(psum[6 + i][:, :], [(lat[:, 2, ts], wkv[:, i * 512:(i + 1) * 512])],
                               *t_lat, t_wkv, *bank_free[6 + i])
                if i == 0:
                    src = psum[6][:, :].rearrange("p (h d) -> p h d", h=MLA_H)
                    bank_free[6] = (copy_out(k_rows[:, t, :, 0:NOPE], src, done),)
                else:
                    bank_free[7] = (copy_out(v_rows[:, t, :], psum[7][:, :], done),)
                t_rows += bank_free[6 + i]
        for slot in (wqs[0][0], wqs[1][0], s2):
            weights.release(slot, done)
        spare(2)
        a1, a2 = room([MLA_H, half]), room([MLA_H, half])
        t_rope = []
        tok = None
        for t in range(NT):
            for x1, x2, h, o1, o2 in (
                    (q_rows[:, t, :, NOPE:NOPE + half], q_rows[:, t, :, NOPE + half:MLA_D], MLA_H,
                     q_rows[:, t, :, NOPE:NOPE + half], q_rows[:, t, :, NOPE + half:MLA_D]),
                    (ckv[:, t, KV_RANK:KV_RANK + half].unsqueeze(1), ckv[:, t, KV_RANK + half:].unsqueeze(1), 1,
                     k_rows[:, t, 0:1, NOPE:NOPE + half], k_rows[:, t, 0:1, NOPE + half:MLA_D])):
                c = bcast(cos[:, t, :].unsqueeze(1), [P, h, half])
                s = bcast(sin[:, t, :].unsqueeze(1), [P, h, half])
                tok = rotate(x1, x2, o1, o2, c, s, a1[:, 0:h], a2[:, 0:h], t_cs, *t_rows)
            tok = V(lambda e, t=t: e.tensor_copy(k_rows[:, t, 1:, NOPE:],
                                                 bcast(k_rows[:, t, 0:1, NOPE:], [P, MLA_H - 1, ROPE])), tok)
            t_rope.append(tok)
        qc, kc = room([MLA_H, SEQ]), room([MLA_H, SEQ])
        t_qk = []
        for j, (dst, src) in enumerate(((qc, q_rows), (kc, k_rows))):
            for h0 in range(0, MLA_H, 2):
                b = 2 + (h0 // 2) % 2
                for h in (h0, h0 + 1):
                    for t in range(NT):
                        o = psum[b][0:MLA_D, (h - h0) * SEQ + t * P:(h - h0) * SEQ + (t + 1) * P]
                        tok = PE(lambda e, o=o, i=src[:, t, h, :]: e.transpose(o, i, ident[:]),
                                 t_rope[-1], *bank_free[b])
                tok = copy_out(dst[0:MLA_D, h0:h0 + 2, :],
                               psum[b][0:MLA_D, :].rearrange("p (h t) -> p h t", h=2), tok)
                bank_free[b] = (tok,)
                t_qk.append(tok)

        sp, wsp, t_wsp = weights.load((A["gm_ws_t"].rearrange("g s t -> s g t"),
                                       lambda b: b[:, 0:512].rearrange("p (g t) -> p g t", g=GM_G)),
                                      (A["gm_bs_t"], lambda b: b[:, 512:516]),
                                      (A["c_upper"], lambda b: b[:, 520:648]))
        ws = room([GM_G, P])
        t_ws = V(lambda e: e.tensor_tensor(ws, wsp[:, 0:512].rearrange("p (g t) -> p g t", g=GM_G),
                                           bcast(wsp[:, 520:648].unsqueeze(1), [P, GM_G, P]), ALU.mult), t_wsp)
        t_v = [normalise(v[:, t, :], v[:, t, :], GM_W, toks[3]) for t in range(NT)]
        t_v = affine_rows(v, A["ab_gm_ln_g"][0], A["ab_gm_ln_b"][0], t_v)
        t_mix = []
        for t in range(NT):
            for g in range(GM_G):
                done = product(psum[6 + t][:, g * P:(g + 1) * P], [(ws[:, g, :], v[:, t, g * P:(g + 1) * P])],
                               t_v[t], t_ws, *bank_free[6 + t])
            for g in range(GM_G):
                gs = slice(g * P, (g + 1) * P)
                tok = V(lambda e, t=t, g=g, gs=gs: e.scalar_tensor_tensor(
                    out=mix[:, t, gs], in0=psum[6 + t][:, gs], scalar=wsp[:, 512 + g:513 + g],
                    in1=u[:, t, gs], op0=ALU.add, op1=ALU.mult), done, toks[5])
            bank_free[6 + t] = (tok,)
            t_mix.append(tok)
        weights.release(sp, t_mix[-1])
        spare(1)

        bufs = attention_buffers()
        inv = room([8])
        for t in range(NT):
            def finish(h0, ps, sums, tok, t=t):
                tok = V(lambda e: e.reciprocal(inv, sums), tok)
                tok = V(lambda e: e.tensor_tensor(
                    mix[:, t, GM_W:].rearrange("p (h d) -> p h d", h=8), ps,
                    bcast(inv.unsqueeze(2), [P, 8, DH]), ALU.mult), tok)
                t_mix.append(tok)
                return (tok,)
            nk = (t + 1) * P
            attention(t, MLA_H, nk, lambda h, t=t: qc[0:MLA_D, h, t * P:(t + 1) * P],
                      lambda h, nk=nk: kc[0:MLA_D, h, 0:nk],
                      lambda h, j: v_rows[:, j, h * DH:(h + 1) * DH],
                      float(MLA_D) ** -0.5, causal[:, t, 0:nk], finish, bufs, *t_qk)
        toks = output_projection(mix, A["ab_w_o"][0], add_scaled_residual, x_cols, *t_mix)
        return post_norm(A["ln1_g"][0], A["ln1_b"][0], toks)

    def rotate(x1, x2, o1, o2, c, s, a1, a2, *after):
        t1 = V(lambda e: e.tensor_tensor(a1, x1, s, ALU.mult), *after)
        t2 = V(lambda e: e.tensor_tensor(a2, x2, s, ALU.mult), *after)
        t3 = V(lambda e: e.tensor_tensor(o1, x1, c, ALU.mult), t1, t2)
        t3 = V(lambda e: e.tensor_tensor(o1, o1, a2, ALU.subtract), t3)
        t4 = V(lambda e: e.tensor_tensor(o2, x2, c, ALU.mult), t3)
        return V(lambda e: e.tensor_tensor(o2, o2, a1, ALU.add), t4)

    def output_projection(mix_rows, w, add, cols, *after, evac=None):
        t_cols = to_cols(cols, lambda k, t: mix_rows[:, t, k * P:(k + 1) * P], KD, (0, 1, 2, 3), *after,
                         evac=evac)
        toks = None
        announce_chunks(w, *[(c0, CHUNK) for c0 in range(0, D, CHUNK)])
        for j, c0 in enumerate(range(0, D, CHUNK)):
            b = 4 + j % 2
            ps, done = project_rows(cols, CHUNK, b, *t_cols)
            toks = add(c0, CHUNK, ps, done)
            bank_free[b] = tuple(toks)
        return toks

    def moe(layer, t_in):
        fresh()
        t_cols = to_cols(x_cols, lambda k, t: x_rows[:, t, k * P:(k + 1) * P], KD, (0, 1, 2, 3), *t_in)
        NL = MOE_G + N_EXP
        announce((A["router_w"][layer].rearrange("(k p) n -> p k n", p=P), (KD, NL)))
        ups = [[(A[w][layer, e_, j].rearrange("p (k f) -> p k f", k=KD), (KD, P))
                for j in range(2) for w in ("moe_gate", "moe_up")] for e_ in range(N_EXP)]
        downs = [[(A["moe_w_down"][layer, e_, j * P:(j + 1) * P, :], (D,)) for j in range(2)]
                 for e_ in range(N_EXP)]
        for now, before in zip(ups + [[]], [[]] + downs):
            announce(*now, *before)
        wr, number, t_wr = take((KD, NL))
        sv, rb, t_rb = vector_row(A["router_b"][layer])
        for t in range(NT):
            done = product3(psum[6][:, t * NL:(t + 1) * NL],
                            [(at(x_cols, slice(None), k, slice(t * P, (t + 1) * P)), at(wr, slice(None), k))
                             for k in range(KD)], *t_cols, t_wr, *bank_free[6])
        release_splits([number], done)
        lg = room([NT, NL])
        tok = V(lambda e: e.tensor_tensor(lg, psum[6][:, 0:NT * NL].rearrange("p (t n) -> p t n", t=NT),
                                          bcast(rb[:, 0:NL].unsqueeze(1), [P, NT, NL]), ALU.add), done, t_rb)
        bank_free[6] = (tok,)
        vectors.release(sv, tok)
        g8, gm8, em8 = room([NT, 8]), room([NT, 8]), room([NT, 8])
        gi, ei = room([NT, 8], dt=U32), room([NT, 8], dt=U32)
        tok = V(lambda e: e.memset(g8, LOWEST), tok)
        tok = V(lambda e: e.tensor_copy(g8[:, :, 0:MOE_G], lg[:, :, 0:MOE_G]), tok)
        for t in range(NT):
            tok = V(lambda e, t=t: e.max(gm8[:, t, :], g8[:, t, :]), tok)
            tok = V(lambda e, t=t: e.max_index(gi[:, t, :], gm8[:, t, :], g8[:, t, :]), tok)
        gsel, ohg = room([NT]), room([NT, MOE_G])
        tok = V(lambda e: e.tensor_copy(gsel, gi[:, :, 0]), tok)
        tok = V(lambda e: e.tensor_tensor(ohg, bcast(iota[:, 0:MOE_G].unsqueeze(1), [P, NT, MOE_G]),
                                          bcast(gsel.unsqueeze(2), [P, NT, MOE_G]), ALU.is_equal), tok, t_iota)
        ge, gsum = room([NT, MOE_G]), room([NT])
        tok = V(lambda e: e.tensor_tensor(ge, lg[:, :, 0:MOE_G], bcast(gm8[:, :, 0:1], [P, NT, MOE_G]),
                                          ALU.subtract), tok)
        t_ge = S(lambda e: e.activation(ge, ge, ACT.Exp), tok)
        esel, picked = room([NT, MOE_E]), room([NT, MOE_E, MOE_G])
        for t in range(NT):
            tok = V(lambda e, t=t: e.tensor_tensor(
                picked[:, t], lg[:, t, MOE_G:].rearrange("p (g e) -> p e g", g=MOE_G),
                bcast(ohg[:, t, :].unsqueeze(1), [P, MOE_E, MOE_G]), ALU.mult), tok)
        tok = V(lambda e: e.tensor_reduce(esel, picked, AX_X, ALU.add), tok)
        for t in range(NT):
            tok = V(lambda e, t=t: e.max(em8[:, t, :], esel[:, t, :]), tok)
            tok = V(lambda e, t=t: e.max_index(ei[:, t, :], em8[:, t, :], esel[:, t, :]), tok)
        p2, p1, eif = room([NT]), room([NT]), room([NT, 2])
        tok = V(lambda e: e.tensor_tensor(p2, em8[:, :, 1], em8[:, :, 0], ALU.subtract), tok)
        t_p2 = S(lambda e: e.activation(p2, p2, ACT.Exp), tok)
        tok = V(lambda e: e.tensor_copy(eif, ei[:, :, 0:2]), tok)
        tok = V(lambda e: e.tensor_reduce(gsum, ge, AX_X, ALU.add), tok, t_ge)
        tok = V(lambda e: e.scalar_tensor_tensor(out=p1, in0=p2, scalar=1.0, in1=gsum, op0=ALU.add,
                                                 op1=ALU.mult), tok, t_p2)
        tok = V(lambda e: e.reciprocal(p1, p1), tok)
        tok = V(lambda e: e.tensor_tensor(p2, p2, p1, ALU.mult), tok)
        oh1, oh2, wmoe = room([NT, MOE_E]), room([NT, MOE_E]), room([NT, MOE_G, MOE_E])
        for oh, j, pr in ((oh1, 0, p1), (oh2, 1, p2)):
            tok = V(lambda e, oh=oh, j=j: e.tensor_tensor(
                oh, bcast(iota[:, 0:MOE_E].unsqueeze(1), [P, NT, MOE_E]),
                bcast(eif[:, :, j:j + 1], [P, NT, MOE_E]), ALU.is_equal), tok)
            tok = V(lambda e, oh=oh, pr=pr: e.tensor_tensor(oh, oh, bcast(pr.unsqueeze(2), [P, NT, MOE_E]),
                                                            ALU.mult), tok)
        tok = V(lambda e: e.tensor_tensor(oh1, oh1, oh2, ALU.add), tok)
        for t in range(NT):
            tok = V(lambda e, t=t: e.tensor_tensor(
                wmoe[:, t], bcast(ohg[:, t, :].unsqueeze(2), [P, MOE_G, MOE_E]),
                bcast(oh1[:, t, :].unsqueeze(1), [P, MOE_G, MOE_E]), ALU.mult), tok)
        wflat = wmoe.rearrange("p t g e -> p t (g e)")
        for t in range(NT):
            tok = V(lambda e, t=t: e.tensor_scalar(x_rows[:, t, :], x_rows[:, t, :], ALPHA, None, ALU.mult),
                    *t_cols, tok)
        t_res = [tok] * NT

        silu = [room([2, SEQ]) for _ in range(2)]
        hid = [room([2, SEQ]) for _ in range(2)]
        hid_tok, hid_free = {}, {}

        def up(e_):
            i = e_ % 2
            for j in range(2):
                for b in (2 * i, 2 * i + 1):
                    wt, number, tk = take((KD, P))
                    done = product3(psum[b][:, j * SEQ:(j + 1) * SEQ],
                                    [(at(wt, slice(None), k), at(x_cols, slice(None), k)) for k in range(KD)],
                                    *t_cols, tk, *bank_free[b])
                    release_splits([number], done)
            gate, upper = (psum[2 * i + c][:, :].rearrange("p (j t) -> p j t", j=2) for c in range(2))
            a = S(lambda e: e.activation(silu[i], gate, ACT.Silu), done)
            bank_free[2 * i] = (a,)
            h = V(lambda e: e.tensor_tensor(hid[i], silu[i], upper, ALU.mult), a)
            bank_free[2 * i + 1] = (h,)
            hid_tok[e_] = split(hidden_parts[i], hid[i], h, *hid_free.get(e_ - 2, ()))

        def out_(e_):
            i = e_ % 2
            for j in range(2):
                wt, number, tk = take((D,))
                for t in range(NT):
                    for h in range(2):
                        b = 4 + 2 * t + h
                        l = at(hidden_parts[i], slice(None), j, slice(t * P, (t + 1) * P))
                        r = at(wt, slice(None), slice(h * 512, (h + 1) * 512))
                        for n, (x, y) in enumerate(((l[0], r[0]), (l[0], r[1]), (l[1], r[0]))):
                            done = PE(lambda e: e.matmul(psum[b][:, :], x, y, start=(j == 0 and n == 0),
                                                         stop=(j == 1 and n == 2)),
                                      hid_tok[e_], tk, *bank_free[b])
                        if j == 1:
                            xs = x_rows[:, t, h * 512:(h + 1) * 512]
                            t_res[t] = V(lambda e: e.scalar_tensor_tensor(
                                out=xs, in0=psum[b][:, :], scalar=wflat[:, t, e_:e_ + 1], in1=xs,
                                op0=ALU.mult, op1=ALU.add), done, t_res[t])
                            bank_free[b] = (t_res[t],)
                release_splits([number], done)
            hid_free[e_] = (done,)

        for e_ in range(N_EXP + 1):
            if e_ < N_EXP:
                up(e_)
            if e_ >= 1:
                out_(e_ - 1)
        return post_norm(A["ln2_g"][layer], A["ln2_b"][layer], [t_res[1], t_res[1]])

    def store(rows, *after):
        s = ctx.enter_context(nc.semaphore("stored"))
        p.wait("sync", after)
        p.dma("sync", out.rearrange("b (t p) d -> p (b t) d", p=P), rows, s)
        p.wait("sync", [(s, 16)])

    def mixer_1(t_in):
        fresh()
        w_in = A["c_w_in"][0]
        t_cols = to_cols(x_cols, lambda k, t: x_rows[:, t, k * P:(k + 1) * P], KD, (0, 1, 2, 3), *t_in)
        q = room([NSA_H // 2, SEQ])
        kv = {n: room([NSA_G, SEQ]) for n in ("kc", "vc", "ks", "kw")}
        vals = {n: room([NT, P]) for n in ("vs", "vw")}
        gates = room([NT, 3 * NSA_H])
        o_rows = room([NT, D])
        straight, swap = room([SEQ]), room([P])
        s_sw = ctx.enter_context(nc.semaphore("swap_loaded"))
        p.wait("scalar", [p.latest("vector"), p.latest("tensor")])
        p.dma("scalar", swap, A["c_swap"], s_sw)
        t_swap = (s_sw, 16)
        NG = 3 * NSA_H
        t_q = []
        announce_chunks(w_in, *[(c0, CHUNK) for c0 in range(0, 1792, CHUNK)], (1792, NG))
        for j in range(4):
            b = 4 + j % 2
            ps, done = project_cols(x_cols, b, *t_cols)
            tok = copy_out(q[:, 2 * j:2 * j + 2, :], ps, done)
            bank_free[b] = (tok,)
            t_q.append(tok)
        t_kv = {}
        for names in (("kc", "vc"), ("ks", "vs"), ("kw", "vw")):
            wt, numbers, tw = take_chunk(CHUNK)
            for i, n in enumerate(names):
                b = 4 + i
                if n in vals:
                    for t in range(NT):
                        done = product3(psum[b][:, t * P:(t + 1) * P],
                                        [(at(x_cols, slice(None), k, slice(t * P, (t + 1) * P)),
                                          wt(k, slice(i * P, (i + 1) * P)))
                                         for k in range(KD)], *t_cols, *tw, *bank_free[b])
                    tok = copy_out(vals[n], psum[b][:, 0:NT * P].rearrange("p (t n) -> p t n", t=NT), done)
                else:
                    done = product3(psum[b][:, 0:SEQ],
                                    [(wt(k, slice(i * P, (i + 1) * P)), at(x_cols, slice(None), k))
                                     for k in range(KD)], *tw, *t_cols, *bank_free[b])
                    tok = copy_out(straight, psum[b][:, 0:SEQ], done, p.latest("vector"), p.latest("scalar"),
                                   p.latest("tensor"))
                    done = product(psum[b][:, SEQ:], [(swap, straight)], tok, t_swap)
                    lower, upper = slice(0, DH), slice(DH, P)
                    tok = V(lambda e: e.tensor_copy(kv[n][lower, 0, :], straight[lower, :]), done)
                    tok = V(lambda e: e.tensor_copy(kv[n][upper, 1, :], straight[upper, :]), tok)
                    tok = V(lambda e: e.tensor_copy(kv[n][upper, 0, :], psum[b][upper, SEQ:]), tok)
                    tok = V(lambda e: e.tensor_copy(kv[n][lower, 1, :], psum[b][lower, SEQ:]), tok)
                bank_free[b] = (tok,)
                t_kv[n] = tok
            release_splits(numbers, done)
        sv, gb, t_gb = vector_row(A["c_gate_b"][0])
        ps, done = project_rows(x_cols, NG, 4, *t_cols)
        tok = V(lambda e: e.tensor_tensor(gates, ps, bcast(gb[:, 0:NG].unsqueeze(1), [P, NT, NG]), ALU.add),
                done, t_gb)
        bank_free[4] = (tok,)
        vectors.release(sv, tok)
        t_gate = S(lambda e: e.activation(gates, gates, ACT.Sigmoid), tok)

        NB = NSA_G * N_CMP
        k_cmp = room([NB])
        v_cmp = room([NSA_G, DH])
        NPAIR = CMP_LEN // 2
        blocks = room([NPAIR, NB])
        hidden = room([2, NB])
        pos_col = room([2, NPAIR])
        s_pc = ctx.enter_context(nc.semaphore("cmp_pos_loaded"))
        p.wait("scalar", [p.latest("vector")])
        p.dma("scalar", pos_col, A["cmp_pos_t"], s_pc)
        hid_rows = room([CMP_HID])
        PER = UNIT // CMP_HID
        for i, (n, w1, w2) in enumerate((("kc", "c_w_ck1", "c_w_ck2"), ("vc", "c_w_cv1", "c_w_cv2"))):
            src = kv[n].rearrange("p g (m b r) -> p g m b r", b=CMP_STRIDE // 2, r=2)
            NS2 = CMP_STRIDE // 2
            for a in range(CMP_LEN // CMP_STRIDE):
                for g in range(NSA_G):
                    for r in range(2):
                        hs = slice(r * DH, (r + 1) * DH)
                        tok = V(lambda e: e.tensor_tensor(
                            blocks[hs, a * NS2:(a + 1) * NS2, g * N_CMP:(g + 1) * N_CMP],
                            src[hs, g, a:a + N_CMP, :, r].rearrange("p m b -> p b m"),
                            bcast(pos_col[hs, i, a * NS2:(a + 1) * NS2].unsqueeze(2), [DH, NS2, N_CMP]),
                            ALU.add), t_kv[n], (s_pc, 16), p.latest("tensor"))
            spare(1)
            for l0 in range(0, NPAIR, PER):
                s, buf, tw = weights.load((A[w1][0, l0 * P:(l0 + PER) * P, :].rearrange("(l d) n -> d l n", d=P),
                                           lambda b: b[:, :].rearrange("p (l n) -> p l n", l=PER)))
                for l in range(l0, l0 + PER):
                    at_l = (l - l0) * CMP_HID
                    done = PE(lambda e: e.matmul(psum[6][0:NB, 0:CMP_HID], blocks[:, l, :],
                                                 buf[:, at_l:at_l + CMP_HID], start=(l == 0),
                                                 stop=(l == NPAIR - 1)), tok, tw, *bank_free[6])
                weights.release(s, done)
            tok = S(lambda e: e.activation(hid_rows[0:NB], psum[6][0:NB, 0:CMP_HID], ACT.Gelu_apprx_tanh), done)
            bank_free[6] = (tok,)
            spare(1)
            for j in range(2):
                done = PE(lambda e: e.transpose(psum[7][:, j * NB:(j + 1) * NB], hid_rows[0:NB, j * P:(j + 1) * P],
                                                ident[0:NB, 0:NB]), tok, *bank_free[7])
            tok = copy_out(hidden, psum[7][:, 0:2 * NB].rearrange("p (j n) -> p j n", j=2), done)
            bank_free[7] = (tok,)
            s, buf, tw = weights.load((A[w2][0].rearrange("(j p) n -> p j n", p=P),
                                       lambda b: b[:, 0:2 * DH].rearrange("p (j n) -> p j n", j=2)))
            if n == "kc":
                for half in (0, DH):
                    done = product(psum[7][half:half + DH, 0:NB],
                                   [(buf[:, j * DH:(j + 1) * DH], hidden[:, j, :]) for j in range(2)],
                                   tok, tw, *bank_free[7])
                tok = t_kc = copy_out(k_cmp, psum[7][:, 0:NB], done)
            else:
                for g in range(NSA_G):
                    done = product(psum[7][0:N_CMP, g * DH:(g + 1) * DH],
                                   [(hidden[:, j, g * N_CMP:(g + 1) * N_CMP], buf[:, j * DH:(j + 1) * DH])
                                    for j in range(2)], tok, tw, *bank_free[7])
                tok = t_vc = copy_out(v_cmp[0:N_CMP], psum[7][0:N_CMP, 0:NSA_G * DH]
                                      .rearrange("p (g d) -> p g d", g=NSA_G), done)
            bank_free[7] = (tok,)
            weights.release(s, done)

        def q_of(h, ts):
            half = (h % 2) * DH
            return q[half:half + DH, h // 2, ts]

        cmask = room([NT, 3, N_CMP])
        s_cm = ctx.enter_context(nc.semaphore("cmp_mask_loaded"))
        p.dma("scalar", cmask, A["c_cmp_mask"], s_cm)
        sc, csum, cmax = room([NSA_H, N_CMP]), room([NSA_H]), room([NSA_H])
        pt = room([4, P])
        factor = room([8])
        part = room([8, DH])
        t_o = []
        for t in range(NT):
            ts = slice(t * P, (t + 1) * P)
            shape = [P, NSA_H, N_CMP]
            for odd in range(2):
                b, half, nh = 6 + odd, odd * DH, NSA_H // 2
                for i in range(nh):
                    h = 2 * i + odd
                    g = h // 8
                    done = product(psum[b][:, i * N_CMP:(i + 1) * N_CMP],
                                   [(q_of(h, ts), k_cmp[half:half + DH, g * N_CMP:(g + 1) * N_CMP])],
                                   *t_q, t_kc, *bank_free[b])
                tok = V(lambda e: e.scalar_tensor_tensor(
                    out=sc[:, odd::2, :], in0=psum[b][:, 0:nh * N_CMP].rearrange("p (h n) -> p h n", h=nh),
                    scalar=DH ** -0.5, in1=bcast(cmask[:, t, 0:1, :], [P, nh, N_CMP]), op0=ALU.mult,
                    op1=ALU.add), done, (s_cm, 16), p.latest("tensor"))
                bank_free[b] = (tok,)
            tok = V(lambda e: e.tensor_reduce(cmax, sc, AX_X, ALU.max), tok)
            tok = V(lambda e: e.tensor_tensor(sc, sc, bcast(cmax.unsqueeze(2), shape), ALU.subtract), tok)
            tok = S(lambda e: e.activation(sc, sc, ACT.Exp), tok)
            tok = V(lambda e, t=t: e.tensor_tensor(sc, sc, bcast(cmask[:, t, 1:2, :], shape), ALU.mult), tok)
            t_sc = tok
            tok = V(lambda e: e.tensor_reduce(csum, sc, AX_X, ALU.add), tok)
            tok = V(lambda e, t=t: e.tensor_scalar(csum, csum, cmask[:, t, 2, 0:1], None, ALU.add), tok)
            tok = V(lambda e: e.reciprocal(csum, csum), tok)
            tok = t_fac = V(lambda e, t=t: e.tensor_tensor(csum, csum, gates[:, t, 0:NSA_H], ALU.mult), tok, t_gate)
            spare(1)
            for h0 in range(0, NSA_H, 4):
                b = h0 // 4 % 2
                for i in range(4):
                    tok = PE(lambda e, i=i: e.transpose(psum[b][0:N_CMP, i * P:(i + 1) * P], sc[:, h0 + i, :],
                                                        ident[:]), t_sc, *bank_free[b])
                tok = copy_out(pt[0:N_CMP], psum[b][0:N_CMP, :].rearrange("p (i t) -> p i t", i=4), tok,
                               p.latest("tensor"))
                bank_free[b] = (tok,)
                ob = 2 + h0 // 8
                for i in range(4):
                    h = h0 + i
                    done = product(psum[ob][:, (h % 8) * DH:(h % 8 + 1) * DH],
                                   [(pt[0:N_CMP, i, :], v_cmp[0:N_CMP, h // 8, :])], tok, t_vc, *bank_free[ob])
                if h0 % 8 == 4:
                    hb = h0 - 4
                    tok = V(lambda e, t=t, hb=hb, ob=ob: e.tensor_tensor(
                        o_rows[:, t, hb * DH:(hb + 8) * DH].rearrange("p (h d) -> p h d", h=8),
                        psum[ob][:, :].rearrange("p (h d) -> p h d", h=8),
                        bcast(csum[:, hb:hb + 8].unsqueeze(2), [P, 8, DH]), ALU.mult), done, t_fac)
                    bank_free[ob] = (tok,)
        bufs = attention_buffers()
        turns = [0]

        def spare_now_and_then():
            turns[0] += 1
            if turns[0] % 5 == 1:
                spare(1)

        for br, (kn, vn) in enumerate((("ks", "vs"), ("kw", "vw"))):
            for t in range(NT):
                def finish(h0, ps, sums, tok, t=t, br=br):
                    tok = V(lambda e: e.reciprocal(factor, sums), tok)
                    g0 = (br + 1) * NSA_H + h0
                    tok = V(lambda e: e.tensor_tensor(factor, factor, gates[:, t, g0:g0 + 8], ALU.mult), tok)
                    tok = V(lambda e: e.tensor_tensor(part, ps, bcast(factor.unsqueeze(2), [P, 8, DH]),
                                                      ALU.mult), tok)
                    o = o_rows[:, t, h0 * DH:(h0 + 8) * DH].rearrange("p (h d) -> p h d", h=8)
                    t_o.append(V(lambda e: e.tensor_tensor(o, o, part, ALU.add), tok))
                    return (tok,)
                ts, nk = slice(t * P, (t + 1) * P), (t + 1) * P
                attention(t, NSA_H, nk, lambda h, ts=ts: q_of(h, ts),
                          lambda h, nk=nk, kn=kn: kv[kn][(h % 2) * DH:(h % 2 + 1) * DH, h // 8, 0:nk],
                          lambda h, j, vn=vn: vals[vn][:, j, (h // 8) * DH:(h // 8 + 1) * DH],
                          DH ** -0.5, causal[:, t, 0:nk], finish, bufs, *t_q, *t_kv.values(),
                          beside=spare_now_and_then)
        toks = output_projection(o_rows, A["c_w_o"][0], add_scaled_residual, x_cols, *t_o)
        return post_norm(A["ln1_g"][1], A["ln1_b"][1], toks)

    def spread_gate(l, stream, first, *after):
        diag = room([KD, P])
        tok = V(lambda e: e.tensor_tensor(diag, bcast(ident[:].unsqueeze(1), [P, KD, P]),
                                          bcast(mod[l][:, first:first + KD, stream].unsqueeze(2), [P, KD, P]),
                                          ALU.mult), *after, t_ident)
        for h in range(2):
            done = product(psum[6 + h][:, :], [(ones[:], diag[:, 4 * h:4 * h + 4, :])], tok, t_ones,
                           *bank_free[6 + h])
            tok2 = V(lambda e: e.tensor_copy(gate_row[:, h * 512:(h + 1) * 512], psum[6 + h][:, :]), done)
            bank_free[6 + h] = (tok2,)
        return tok2

    def modulated_cols(dst, rows, l, shift, stream, after):
        normed = room([NT, D])
        toks = []
        for t in range(NT):
            r, tok = rms_factor(rows[:, t, :], D, normed[:, t, :], RMS_EPS, *after)
            toks.append(V(lambda e, t=t, r=r: e.tensor_scalar(normed[:, t, :], rows[:, t, :], r, None, ALU.mult),
                          tok))

        moved = [room([2, SEQ]) for _ in range(2)]

        def evac(k0, ps, tok):
            m = moved[k0 // 2 % 2]
            for k in (k0, k0 + 1):
                sc, sh = mod[l][:, shift + KD + k, stream:stream + 1], mod[l][:, shift + k, stream:stream + 1]
                tok = V(lambda e: e.tensor_scalar(m[:, k - k0, :], ps[:, k - k0, :], sc, sh, ALU.mult, ALU.add),
                        tok)
            return split(at(dst, slice(None), slice(k0, k0 + 2)), m, tok)
        return to_cols(dst, lambda k, t: normed[:, t, k * P:(k + 1) * P], KD, (0, 1, 2, 3), *toks, evac=evac)

    key_cols = sb("key_cols", [P, KV_HEADS, 2 * SEQ])
    val_rows = sb("val_rows", [P, 2 * NT, KVW])

    def qkv_chunks(with_q):
        return (0, 256, 512) if with_q else (512,)

    def announce_qkv(l, with_q):
        announce_chunks(A["w_in_2"][l], *[(c0, CHUNK) for c0 in qkv_chunks(with_q)])

    def qkv(cols, l, with_q, rotary, key_at, after, between=lambda t: None):
        NHEAD = Q_HEADS + KV_HEADS
        qk = room([NT, NHEAD, DH])
        flat = qk.rearrange("p t h d -> p t (h d)")
        toks = []
        chunks = qkv_chunks(with_q)
        for j, c0 in enumerate(chunks):
            b = 4 + j % 2
            ps, done = project_rows(cols, CHUNK, b, *after)
            if c0 < QW:
                tok = (copy_out(flat[:, :, c0:c0 + CHUNK], ps, done),)
            else:
                tok = (copy_out(flat[:, :, QW:QW + KVW], ps[:, :, 0:KVW], done),)
                tok += (copy_out(val_rows[:, key_at // P:key_at // P + NT, :], ps[:, :, KVW:], *tok),)
            bank_free[b] = tok
            toks += tok
        h0 = 0 if with_q else Q_HEADS
        nh = NHEAD - h0
        sg, gains, t_g = vectors.load(
            (A["q_gain_2"][l].partition_broadcast(P), lambda b: b[:, 0:DH]),
            (A["k_gain_2"][l].partition_broadcast(P), lambda b: b[:, DH:2 * DH]))
        sq, ms = room([NHEAD, DH]), room([NHEAD])
        a1, a2 = room([NHEAD, DH // 2]), room([NHEAD, DH // 2])
        kdup = room([KV_HEADS, 2, DH])
        q_cols = room([Q_HEADS // 2, SEQ])
        out_toks = []
        for t in range(NT):
            x = qk[:, t, h0:, :]
            tok = V(lambda e: e.tensor_tensor(sq[:, h0:], x, x, ALU.mult), *toks)
            tok = V(lambda e: e.tensor_reduce(ms[:, h0:], sq[:, h0:], AX_X, ALU.add), tok)
            tok = V(lambda e: e.tensor_scalar(ms[:, h0:], ms[:, h0:], 1.0 / DH, RMS_EPS, ALU.mult, ALU.add), tok)
            tok = S(lambda e: e.activation(ms[:, h0:], ms[:, h0:], ACT.Sqrt), tok)
            tok = V(lambda e: e.reciprocal(ms[:, h0:], ms[:, h0:]), tok)
            tok = V(lambda e: e.tensor_tensor(x, x, bcast(ms[:, h0:].unsqueeze(2), [P, nh, DH]), ALU.mult), tok)
            for a, b, g0 in ((h0, Q_HEADS, 0), (Q_HEADS, NHEAD, DH)):
                if b > a:
                    y = qk[:, t, a:b, :]
                    tok = V(lambda e, y=y, g0=g0, n=b - a: e.tensor_tensor(
                        y, y, bcast(gains[:, g0:g0 + DH].unsqueeze(1), [P, n, DH]), ALU.mult), tok, t_g)
            if rotary:
                hf = DH // 2
                c = bcast(rope_cos[:, t, :].unsqueeze(1), [P, nh, hf])
                s = bcast(rope_sin[:, t, :].unsqueeze(1), [P, nh, hf])
                tok = rotate(x[:, :, 0:hf], x[:, :, hf:], x[:, :, 0:hf], x[:, :, hf:], c, s,
                             a1[:, h0:], a2[:, h0:], tok)
            tok = V(lambda e, t=t: e.tensor_copy(kdup, bcast(qk[:, t, Q_HEADS:, :].unsqueeze(2),
                                                             [P, KV_HEADS, 2, DH])), tok, p.latest("tensor"))
            between(t)
            for g in range(KV_HEADS):
                done = PE(lambda e, g=g: e.transpose(psum[6][:, g * P:(g + 1) * P],
                                                     kdup[:, g].rearrange("p a d -> p (a d)"), ident[:]),
                          tok, *bank_free[6])
            k0 = key_at + t * P
            kt = copy_out(key_cols[:, :, k0:k0 + P], psum[6][:, 0:2 * P].rearrange("p (g t) -> p g t", g=2), done)
            bank_free[6] = (kt,)
            out_toks.append(kt)
            if with_q:
                for j in range(Q_HEADS // 2):
                    done = PE(lambda e, j=j, t=t: e.transpose(
                        psum[7][:, j * P:(j + 1) * P], flat[:, t, j * P:(j + 1) * P], ident[:]),
                        tok, *bank_free[7])
                kt = copy_out(q_cols[:, :, t * P:(t + 1) * P],
                              psum[7][:, :].rearrange("p (j t) -> p j t", t=P), done)
                bank_free[7] = (kt,)
                out_toks.append(kt)
        vectors.release(sg, p.latest("vector"))
        return q_cols, out_toks + toks

    def conformer(cols, l, dst, after):
        NC = CONV_W // P
        PAD = CONV_K // 2
        w_in = A["w_in_2"][l]
        g = room([NC, SEQ + 2 * PAD])
        y = room([NC, SEQ])
        a, gt = room([NC, SEQ]), room([2, SEQ])
        cw = room([NC, CONV_K + 1])
        s_cw = ctx.enter_context(nc.semaphore(f"conv_w_loaded_{len(param_sems)}"))
        param_sems[len(param_sems)] = s_cw
        p.wait("scalar", [p.latest("vector"), p.latest("tensor")])
        p.dma("scalar", cw, A["conv_wb_t"][l], s_cw)
        V(lambda e: e.memset(g, 0.0))
        U0 = QW + 2 * KVW
        announce_chunks(w_in, *[(U0 + i * CONV_W + j * CHUNK, CHUNK) for j in range(2) for i in range(2)])
        toks = [()] * NC

        def project(j):
            ps, done = project_cols(cols, 4, *after)
            t_a = copy_out(a[:, 2 * j:2 * j + 2, :], ps, done)
            bank_free[4] = (t_a,)
            ps, done = project_cols(cols, 5, *after)
            tok = S(lambda e: e.activation(gt, ps, ACT.Sigmoid), done, p.latest("vector"))
            bank_free[5] = (tok,)
            tok = V(lambda e: e.tensor_tensor(g[:, 2 * j:2 * j + 2, PAD:PAD + SEQ], a[:, 2 * j:2 * j + 2, :],
                                              gt, ALU.mult), tok, t_a)
            toks[2 * j] = toks[2 * j + 1] = (tok,)

        first = 1

        def taps():
            for i in range(CONV_K):
                for c in range(first, NC):
                    w, src = cw[:, c, i:i + 1], g[:, c, i:i + SEQ]
                    if i == 0:
                        f = lambda e: e.tensor_scalar(y[:, c, :], src, w, cw[:, c, CONV_K:], ALU.mult, ALU.add)
                    else:
                        f = lambda e: e.scalar_tensor_tensor(out=y[:, c, :], in0=src, scalar=w, in1=y[:, c, :],
                                                             op0=ALU.mult, op1=ALU.add)
                    toks[c] = (V_beside(f, *toks[c], (s_cw, 16)),)
                yield

        def gpsimd_taps():
            products = [room([SEQ]) for _ in range(2)]
            for i in range(CONV_K):
                for c in range(first):
                    w, src, prod = cw[:, c, i:i + 1], g[:, c, i:i + SEQ], products[i % 2]
                    if i == 0:
                        toks[c] = (G(lambda e: e.tensor_scalar(y[:, c, :], src, w, cw[:, c, CONV_K:], ALU.mult,
                                                               ALU.add), *toks[c], (s_cw, 16)),)
                    else:
                        tok = G_beside(lambda e: e.tensor_scalar(prod, src, w, None, ALU.mult), *toks[c])
                        toks[c] = (G(lambda e: e.tensor_tensor(y[:, c, :], y[:, c, :], prod, ALU.add), tok),)

        def finish():
            t_rows = []
            for t in range(NT):
                for c in range(NC):
                    done = PE(lambda e, c=c, t=t: e.transpose(psum[6 + t][:, c * P:(c + 1) * P],
                                                              y[:, c, t * P:(t + 1) * P], ident[:]),
                              *toks[c], *bank_free[6 + t])
                t_rows.append(copy_out(dst[:, t, :], psum[6 + t][:, :], done))
                bank_free[6 + t] = (t_rows[-1],)
            t_rows = [normalise(dst[:, t, :], dst[:, t, :], CONV_W, t_rows[t]) for t in range(NT)]
            t_rows = affine_rows(dst, A["ln_g_2"][l], A["ln_b_2"][l], t_rows)
            return S(lambda e: e.activation(dst, dst, ACT.Silu), *t_rows)
        return project, taps(), gpsimd_taps, finish

    def merge(l, o_attn, o_conv, rows, after):
        beta = room([KD])
        s_b = ctx.enter_context(nc.semaphore(f"beta_loaded_{len(param_sems)}"))
        param_sems[len(param_sems)] = s_b
        p.wait("scalar", [p.latest("vector"), p.latest("tensor")])
        p.dma("scalar", beta, A["beta_t"][l], s_b)
        scratch = room([QW])
        toks = []
        for src in (o_attn, o_conv):
            for t in range(NT):
                r, tok = rms_factor(src[:, t, :], QW, scratch, RMS_EPS, *after)
                toks.append(V(lambda e, src=src, t=t, r=r: e.tensor_scalar(src[:, t, :], src[:, t, :], r, None,
                                                                           ALU.mult), tok))

        moved = [room([2, SEQ]) for _ in range(2)]

        def evac(k0, ps, tok):
            m = moved[k0 // 2 % 2]
            tok = V(lambda e: e.tensor_tensor(m, ps, bcast(beta[:, k0:k0 + 2].unsqueeze(2), [P, 2, SEQ]),
                                              ALU.mult), tok, (s_b, 16))
            return split(at(x_cols, slice(None), slice(k0, k0 + 2)), m, tok)

        t_cols = to_cols(x_cols, lambda k, t: (o_attn[:, t, k * P:(k + 1) * P] if k < QW // P else
                                               o_conv[:, t, (k * P - QW):(k * P - QW) + P]),
                         KD, (0, 1, 2, 3), *toks, evac=evac)
        part = room([NT, CHUNK])
        announce_chunks(A["w_o_2"][l], *[(c0, CHUNK) for c0 in range(0, D, CHUNK)])
        for j, c0 in enumerate(range(0, D, CHUNK)):
            b = 4 + j % 2
            ps, done = project_rows(x_cols, CHUNK, b, *t_cols)
            tok = V(lambda e, ps=ps, c0=c0: e.tensor_tensor(
                part, ps, bcast(gate_row[:, c0:c0 + CHUNK].unsqueeze(1), [P, NT, CHUNK]), ALU.mult), done)
            bank_free[b] = (tok,)
            r = rows[:, :, c0:c0 + CHUNK]
            tok = V(lambda e, r=r: e.tensor_tensor(r, r, part, ALU.add), tok)
        return tok

    def attend(l, rows, stream, nk, after):
        fresh()
        t_gate = spread_gate(l, stream, 2 * KD, *after)
        t_cols = modulated_cols(x_cols, rows, l, 0, stream, after)
        top[0] = 0
        p.stage()
        key_at = 0 if stream else SEQ
        o_attn, o_conv = room([NT, QW]), room([NT, CONV_W])
        announce_qkv(l, True)
        project, taps, gpsimd_taps, finish_conv = conformer(x_cols, l, o_conv, t_cols)
        q_cols, t_qkv = qkv(x_cols, l, True, not stream, key_at, t_cols, project)
        inv = room([8])
        bufs = attention_buffers()
        gpsimd_taps()
        t_o = []
        for t in range(NT):
            def finish(h0, ps, sums, tok, t=t):
                tok = V(lambda e: e.reciprocal(inv, sums), tok)
                t_o.append(V(lambda e: e.tensor_tensor(o_attn[:, t, :].rearrange("p (h d) -> p h d", h=8), ps,
                                                       bcast(inv.unsqueeze(2), [P, 8, DH]), ALU.mult), tok))
                return (t_o[-1],)
            G4 = Q_HEADS // KV_HEADS
            attention(t, Q_HEADS, nk, lambda h, t=t: q_cols[(h % 2) * DH:(h % 2 + 1) * DH, h // 2, t * P:(t + 1) * P],
                      lambda h: key_cols[(h % 2) * DH:(h % 2 + 1) * DH, h // G4, 0:nk],
                      lambda h, j: val_rows[:, j, (h // G4) * DH:(h // G4 + 1) * DH],
                      DH ** -0.5, None, finish, bufs, *t_qkv, beside=lambda: next(taps, None))
        for _ in taps:
            pass
        t_conv = finish_conv()
        return merge(l, o_attn, o_conv, rows, [*t_o, t_conv, t_gate])

    def peer(l, rows, stream, t_in):
        fresh()
        spread_gate(l, stream, 5 * KD, t_in)
        t_cols = modulated_cols(x_cols, rows, l, 3 * KD, stream, [t_in])
        top[0] = 0
        p.stage()
        HT = PEER_H * PEER_TOP
        slots = room([3, SEQ])
        w_parts = room([2, SEQ], dt=F16)
        NQ = 4
        KQ = PEER_K // NQ
        TB = SEQ // KQ
        dense = [room([SEQ, KQ])]
        hot2 = [room([TB, PEER_K], dt=F16) for _ in range(2)]
        apart = [room([TB, PEER_K], dt=F16) for _ in range(2)]
        hot1 = [room([TB, KQ], dt=F16) for _ in range(2)]
        hot1w = [room([TB, 2, KQ], dt=F16) for _ in range(2)]
        act = [room([SEQ]) for _ in range(2)]
        scaled = room([SEQ])
        kept = top[0]
        q = room([PEER_H, SEQ])
        keys = room([PEER_H, PEER_K])
        s_k = ctx.enter_context(nc.semaphore(f"peer_keys_loaded_{l}{stream}"))
        p.wait("scalar", [p.latest("vector"), p.latest("tensor")])
        p.dma("scalar", keys, A["peer_keys_t"][l], s_k)
        t_q = []
        announce_chunks(A["peer_wq_2"][l], *[(j * CHUNK, CHUNK) for j in range(4)])
        for j in range(4):
            b = 4 + j % 2
            ps, done = project_cols(x_cols, b, *t_cols)
            t_q.append(copy_out(q[:, 2 * j:2 * j + 2, :], ps, done))
            bank_free[b] = (t_q[-1],)
        NS = 2 * PEER_H
        score = room([NS, PEER_K])
        best2 = room([NS, PEER_TOP])
        key_u = room([NS, PEER_TOP], dt=U32)
        key_f = room([NS, PEER_TOP])
        flat_score = score.rearrange("p i k -> p (i k)")
        cand = flat_score.rearrange("p (h a b) -> p h a b", h=PEER_H, a=PEER_TOP)
        pick = flat_score.rearrange("p (s k) -> p s k", k=PEER_TOP)
        best, place_u = room([PEER_H, PEER_TOP]), room([PEER_H, PEER_TOP], dt=U32)
        row_u, col_u = room([HT], dt=U32), room([HT], dt=U32)
        row_f, col_f = room([HT]), room([HT])
        chosen = room([2, HT])
        wsum = room([PEER_H])
        early_act = [room([SEQ]) for _ in range(6)]
        AHEAD = len(early_act) + len(act)

        SCALE = 2.0 ** 15
        t_slots, t_parts = [], []
        dense_tok, read_dense = {}, {}
        hot_free, hot2_tok, hot1_tok, built = {}, {}, {}, {}
        distance1 = {}
        distance, apart_free, apart_at = {}, [(), ()], [0]

        S2 = [P, TB, PEER_K]

        def key_slots(n, c):
            t0 = n % KQ * TB
            return slots[:, c, t0:t0 + TB].unsqueeze(2)

        def second_distance(n, squared=True):
            i = apart_at[0] % 2
            apart_at[0] += 1
            d = apart[i]
            tok = G(lambda e: e.tensor_tensor(d, bcast(iota[:].unsqueeze(1), S2), bcast(key_slots(n, 1), S2),
                                              ALU.subtract), t_slots[n % KQ * TB // P], *apart_free[i])
            if squared:
                tok = G(lambda e: e.tensor_tensor(d, d, d, ALU.mult), tok)
            distance[n] = (i, squared, tok)

        def second_hots(n):
            i, squared, tok = distance[n]
            if not squared:
                tok = S(lambda e: e.activation(apart[i], apart[i], ACT.Square), tok)
            hot2_tok[n] = S(lambda e: e.activation(hot2[n % 2], apart[i], ACT.Relu, bias=1.0, scale=-1.0),
                            tok, *hot_free.get(n - 2, ()))
            apart_free[i] = (hot2_tok[n],)

        def second_hots_at_once(n):
            hot2_tok[n] = V_beside(lambda e: e.tensor_tensor(hot2[n % 2], bcast(iota[:].unsqueeze(1), S2),
                                                      bcast(key_slots(n, 1), S2), ALU.is_equal),
                            t_slots[n % KQ * TB // P], *hot_free.get(n - 2, ()))

        def last(tokens, n):
            return (tokens[n],) if n in tokens else ()

        def first_hots(n):
            qt, t0 = n // KQ, n % KQ * TB
            s1, s3 = [P, TB, KQ], [P, TB, 2, KQ]
            tok = V_beside(lambda e: e.tensor_tensor(hot1[n % 2], bcast(iota[:, qt * KQ:(qt + 1) * KQ].unsqueeze(1), s1),
                                              bcast(key_slots(n, 0), s1), ALU.is_equal), t_slots[n % KQ * TB // P],
                    *last(hot1_tok, n - 2))
            parts = w_parts[:, :, t0:t0 + TB].rearrange("p c t -> p t c")
            hot1_tok[n] = V(lambda e: e.tensor_tensor(hot1w[n % 2], bcast(hot1[n % 2].unsqueeze(2), s3),
                                                      bcast(parts.unsqueeze(3), s3), ALU.mult),
                            tok, t_parts[n % KQ * TB // P], *hot_free.get(n - 2, ()))

        def first_distance(n):
            h, s1 = hot1[n % 2], [P, TB, KQ]
            tok = G(lambda e: e.tensor_tensor(h, bcast(iota[:, n // KQ * KQ:(n // KQ + 1) * KQ].unsqueeze(1), s1),
                                              bcast(key_slots(n, 0), s1), ALU.subtract),
                    t_slots[n % KQ * TB // P], *last(hot1_tok, n - 2))
            tok = S(lambda e: e.activation(h, h, ACT.Square), tok)
            distance1[n] = S(lambda e: e.activation(h, h, ACT.Relu, bias=1.0, scale=-1.0), tok)

        def product_hots(n):
            t0, s3 = n % KQ * TB, [P, TB, 2, KQ]
            parts = w_parts[:, :, t0:t0 + TB].rearrange("p c t -> p t c")
            hot1_tok[n] = G(lambda e: e.tensor_tensor(hot1w[n % 2], bcast(hot1[n % 2].unsqueeze(2), s3),
                                                      bcast(parts.unsqueeze(3), s3), ALU.mult),
                            distance1[n], t_parts[n % KQ * TB // P], *hot_free.get(n - 2, ()))

        def build_batch(n):
            qt, j = divmod(n, KQ)
            i, t0, b = n % 2, j * TB, 2 + n % 2
            for m in range(TB):
                for c in range(2):
                    f = lambda e: e.matmul(psum[b][:, m * KQ:(m + 1) * KQ], hot2[i][:, m, :], hot1w[i][:, m, c, :],
                                           start=(c == 0), stop=(c == 1))
                    if m == TB - 1 and c == 1:
                        done = PE(f)
                    else:
                        p.quiet("tensor", f, hot2_tok[n], hot1_tok[n], *bank_free[b])
            hot_free[n] = (done,)
            built[n] = done

        def keep_batch(n):
            qt, j = divmod(n, KQ)
            t0, b = j * TB, 2 + n % 2
            tok = S(lambda e: e.activation(dense[qt % 2][:, t0:t0 + TB, :],
                                           psum[b][:, 0:TB * KQ].rearrange("p (t k) -> p t k", t=TB), ACT.Copy,
                                           scale=1.0 / SCALE),
                    built[n], *read_dense.get(qt - 2, ()))
            bank_free[b] = (tok,)
            dense_tok[qt] = tok

        def weight_parts(ts, after):
            rest = scaled[:, ts]
            tok = V(lambda e: e.tensor_scalar(rest, slots[:, 2, ts], SCALE, None, ALU.mult), after)
            tok = V(lambda e: e.tensor_copy(w_parts[:, 0, ts], rest), tok)
            return V(lambda e: e.tensor_tensor(w_parts[:, 1, ts], rest, w_parts[:, 0, ts], ALU.subtract), tok)

        EARLY, EVERY = P // TB, 8
        ticks, early = [0], [0]

        def early_batch():
            n = early[0]
            early[0] += 1
            for m in range(n + (n > 0), min(n + 2, EARLY)):
                if m % 2 == 0:
                    first_distance(m)
                if m % 4 != 3:
                    second_distance(m, False)
            if n % 4 != 3:
                second_hots(n)
            else:
                second_hots_at_once(n)
            if n % 2 == 0:
                product_hots(n)
            else:
                first_hots(n)
            if n >= 1:
                keep_batch(n - 1)
            build_batch(n)
            if n == EARLY - 1:
                keep_batch(n)

        def tick():
            ticks[0] += 1
            if t_slots and ticks[0] % EVERY == 0 and early[0] < EARLY:
                early_batch()

        def top16(values, best, index, after):
            steps = (lambda e, i: e.max(best(i)[:, 0:8], values[i]),
                     lambda e, i: e.max_index(index(i)[:, 0:8], best(i)[:, 0:8], values[i]),
                     lambda e, i: e.match_replace(values[i], best(i)[:, 0:8], values[i], LOWEST),
                     lambda e, i: e.max(best(i)[:, 8:16], values[i]),
                     lambda e, i: e.max_index(index(i)[:, 8:16], best(i)[:, 8:16], values[i]))
            toks = [(after, p.latest("vector"))] * len(values)
            for f in steps:
                for i in range(len(values)):
                    toks[i] = (V_beside(lambda e: f(e, i), *toks[i]),)
                    tick()
            return toks[-1][0]

        hidden_tok, act_tok, scaled_tok, round_tok, parts_tok, parts_free = {}, {}, {}, {}, {}, {}
        us = [(A["peer_u_t"][l, i].rearrange("p (k e) -> p k e", k=KD), (KD, P)) for i in range(PEER_K)]
        vs = [(A["peer_v_2"][l, i * P:(i + 1) * P, :], (D,)) for i in range(PEER_K)]
        LAG = 3
        announce(*us[:AHEAD])
        for i in range(PEER_K + LAG):
            announce(*(us[i:i + 1] if i >= AHEAD else ()), *(vs[i - LAG:i - LAG + 1] if i >= LAG else ()))

        def act_of(i1):
            return early_act[i1] if i1 < len(early_act) else act[i1 % 2]

        def scaled_parts(i1):
            return at(hidden_parts[i1 % 2], slice(None), i1 // 2 % 2)

        def hidden(i1):
            ut, number, tw = take((KD, P), False)
            b = i1 % 2
            done = product3(psum[b][:, 0:SEQ], [(at(ut, slice(None), k), at(x_cols, slice(None), k))
                                                for k in range(KD)], tw, *t_cols, *bank_free[b])
            release_splits([number], done)
            hidden_tok[i1] = done

        def activate(i1):
            b = i1 % 2
            tok = S(lambda e: e.activation(act_of(i1), psum[b][:, 0:SEQ], ACT.Gelu), hidden_tok[i1],
                    *(scaled_tok.get(i1 - 2, ()) if i1 >= AHEAD else ()))
            bank_free[b] = (tok,)
            act_tok[i1] = tok

        def weigh(i1):
            qt, kk = divmod(i1, KQ)
            tok = V(lambda e: e.tensor_tensor(scaled, act_of(i1), dense[qt % 2][:, :, kk], ALU.mult),
                    act_tok[i1], dense_tok[qt], *parts_tok.get(i1 - 1, ()))
            read_dense[qt] = (tok,)
            scaled_tok[i1] = (tok,)

        def round_part(i1):
            round_tok[i1] = S(lambda e: e.activation(scaled_parts(i1)[0], scaled, ACT.Copy), *scaled_tok[i1],
                              *parts_free.get(i1 - 4, ()))

        def rest_part(i1):
            hi, lo = scaled_parts(i1)
            tok = V(lambda e: e.tensor_tensor(lo, scaled, hi.bitcast(F32), ALU.subtract), round_tok[i1])
            parts_tok[i1] = (tok,)

        def outputs(i1):
            vt, number, tw = take((D,), False)
            for t in range(NT):
                for h in range(2):
                    b = 4 + 2 * t + h
                    w0 = (*parts_tok[i1], tw) + (tuple(bank_free[b]) if i1 == 0 else ())
                    x = at(scaled_parts(i1), slice(None), slice(t * P, (t + 1) * P))
                    y = at(vt, slice(None), slice(h * 512, (h + 1) * 512))
                    for n, (xx, yy) in enumerate(((x[0], y[0]), (x[0], y[1]), (x[1], y[0]))):
                        done = PE(lambda e: e.matmul(psum[b][:, :], xx, yy, start=(i1 == 0 and n == 0),
                                                     stop=(i1 == PEER_K - 1 and n == 2)), *w0)
            release_splits([number], done)
            parts_free[i1] = (done,)
            return done

        for t in range(NT):
            ts = slice(t * P, (t + 1) * P)
            for b in range(4):
                c, h0 = b % 2, b // 2 * 4
                half = c * DH
                for h in range(h0, h0 + 4):
                    done = PE(lambda e: e.matmul(
                        psum[b][:, (h - h0) * P:(h - h0 + 1) * P], q[half:half + DH, h, ts],
                        keys[half:half + DH, h, :], start=True, stop=True), *t_q, (s_k, 16), *bank_free[b])
                tok = copy_out(score[:, 2 * h0 + c:2 * h0 + c + 7:2, :],
                               psum[b][:, :].rearrange("p (i k) -> p i k", k=PEER_K), done, p.latest("vector"))
                bank_free[b] = (tok,)
            t_score = p.latest("scalar")
            if t == 0:
                for i in range(AHEAD):
                    feed(G)
                    hidden(i)
                    activate(i)
                feed(G)
            tok = top16([score[:, i, :] for i in range(NS)], lambda i: best2[:, i, :], lambda i: key_u[:, i, :],
                        t_score)
            tok = V(lambda e: e.tensor_copy(key_f, key_u), tok)
            halves = best2.rearrange("p (h c) k -> p h c k", c=2)
            s4 = [P, PEER_H, PEER_TOP, PEER_TOP]
            tok = V(lambda e: e.tensor_tensor(cand, bcast(halves[:, :, 0, :].unsqueeze(3), s4),
                                              bcast(halves[:, :, 1, :].unsqueeze(2), s4), ALU.add), tok)
            tok = top16([cand[:, h].rearrange("p a b -> p (a b)") for h in range(PEER_H)],
                        lambda h: best[:, h, :], lambda h: place_u[:, h, :], tok)
            w3 = best
            tok = V(lambda e: e.tensor_copy(wsum, best[:, :, 0]), tok)
            tok = V(lambda e: e.tensor_tensor(w3, w3, bcast(wsum.unsqueeze(2), [P, PEER_H, PEER_TOP]),
                                              ALU.subtract), tok)
            tok = S(lambda e: e.activation(w3, w3, ACT.Exp), tok)
            tok = V(lambda e: e.tensor_reduce(wsum, w3, AX_X, ALU.add), tok)
            tok = V(lambda e: e.reciprocal(wsum, wsum), tok)
            tok = V(lambda e: e.tensor_tensor(w3, w3, bcast(wsum.unsqueeze(2), [P, PEER_H, PEER_TOP]),
                                              ALU.mult), tok)
            flat_u = place_u.rearrange("p h k -> p (h k)")
            tok = V(lambda e: e.tensor_scalar(row_u, flat_u, 4, None, ALU.logical_shift_right), tok)
            tok = V(lambda e: e.tensor_scalar(col_u, flat_u, 15, None, ALU.bitwise_and), tok)
            tok = V(lambda e: e.tensor_copy(row_f, row_u), tok)
            tok = V(lambda e: e.tensor_copy(col_f, col_u), tok)
            for c, place in enumerate((row_f, col_f)):
                tok = V(lambda e: e.tensor_tensor(
                    pick, bcast(iota[:, 0:PEER_TOP].unsqueeze(1), [P, HT, PEER_TOP]),
                    bcast(place.unsqueeze(2), [P, HT, PEER_TOP]), ALU.is_equal), tok)
                pick4 = pick.rearrange("p (h s) k -> p h s k", h=PEER_H)
                keys4 = key_f.rearrange("p (h c) k -> p h c k", c=2)[:, :, c, :].unsqueeze(2)
                tok = V(lambda e: e.tensor_tensor(pick4, pick4, bcast(keys4, s4), ALU.mult), tok)
                tok = V(lambda e, c=c: e.tensor_reduce(chosen[:, c, :], pick, AX_X, ALU.add), tok)
            for i, src in enumerate((chosen[:, 0, :], chosen[:, 1, :], w3.rearrange("p h k -> p (h k)"))):
                done = PE(lambda e, i=i, src=src: e.transpose(psum[6][:, i * P:(i + 1) * P], src, ident[:]),
                          tok, *bank_free[6])
            tok = copy_out(slots[:, :, ts], psum[6][:, 0:3 * P].rearrange("p (i t) -> p i t", i=3), done)
            bank_free[6] = (tok,)
            t_slots.append(tok)
            t_parts.append(weight_parts(ts, tok))
            tick()

        while early[0] < EARLY:
            early_batch()
        top[0] = kept
        dense.append(room([SEQ, KQ]))
        ahead = [n for n in range(EARLY, KQ) if n % 2 == 0]
        second_distance(ahead.pop(0), False)
        second_distance(ahead.pop(0), False)
        for n in range(EARLY, KQ):
            first_hots(n)
            if n in distance:
                second_hots(n)
                if ahead:
                    second_distance(ahead.pop(0), False)
            else:
                second_hots_at_once(n)
            if n > EARLY:
                keep_batch(n - 1)
            build_batch(n)
        keep_batch(KQ - 1)

        second_distance(KQ, False)
        second_hots(KQ)
        first_hots(KQ)
        second_distance(KQ + 1, False)
        feed()
        for i in range(PEER_K + LAG):
            n = i + KQ
            if AHEAD <= i - 1 < PEER_K:
                activate(i - 1)
            if i >= LAG:
                rest_part(i - 3)
            if 0 <= i - 2 < PEER_K:
                weigh(i - 2)
            feed()
            if i and n - 1 < PEER_K:
                keep_batch(n - 1)
            if n + 1 < PEER_K:
                second_hots(n + 1)
            if n + 2 < PEER_K:
                second_distance(n + 2, i >= AHEAD // 2)
            if 0 <= i - 2 < PEER_K:
                round_part(i - 2)
            if n + 1 < PEER_K:
                first_hots(n + 1)
            if AHEAD <= i < PEER_K:
                hidden(i)
            if i >= LAG:
                done = outputs(i - LAG)
            if n < PEER_K:
                build_batch(n)
        top[0] -= 2 * SEQ + SEQ
        gated = room([BANK])
        for t in range(NT):
            for h in range(2):
                b = 4 + 2 * t + h
                hs = slice(h * 512, (h + 1) * 512)
                tok = V(lambda e, b=b, hs=hs: e.tensor_tensor(gated, psum[b][:, :], gate_row[:, hs], ALU.mult),
                        done)
                bank_free[b] = (tok,)
                tok = V(lambda e, t=t, hs=hs: e.tensor_tensor(rows[:, t, hs], rows[:, t, hs], gated, ALU.add), tok)
        return tok

    def second(t_in):
        fresh()
        t_c = attend(0, ctx_rows, 1, SEQ, [t_ctx])
        t_c = peer(0, ctx_rows, 1, t_c)
        t_x = p.latest("vector")
        for l in range(DEPTH):
            if l == 1:
                fresh()
                t_cc = modulated_cols(x_cols, ctx_rows, l, 0, 1, [t_c])
                fresh()
                announce_qkv(l, False)
                qkv(x_cols, l, False, False, 0, t_cc)
            t_x = attend(l, x_rows, 0, 2 * SEQ, [t_x])
            t_x = peer(l, x_rows, 0, t_x)
        fresh()
        scratch = room([D])
        sv, fg, t_fg = vector_row(A["final_g_2"])
        toks = []
        for t in range(NT):
            r, tok = rms_factor(x_rows[:, t, :], D, scratch, RMS_EPS, t_x)
            toks.append(V(lambda e, t=t, r=r: e.scalar_tensor_tensor(
                out=x_rows[:, t, :], in0=x_rows[:, t, :], scalar=r, in1=fg[:, :], op0=ALU.mult, op1=ALU.mult),
                tok, t_fg))
        store(x_rows[:], *toks)

    t_in = mixer_0()
    t_in = moe(0, t_in)
    t_in = mixer_1(t_in)
    for _ in mod_steps:
        pass
    p.wait("scalar", [p.latest("vector"), p.latest("tensor"), p.latest("scalar")])
    t_ctx = constant("ctx_2", ctx_rows[:])
    t_in = moe(1, t_in)
    second(t_in)


def host_layout(inputs):
    a = {n: np.asarray(v) for n, v in inputs.items()}

    def tiles(v):
        return v.reshape(NT, P, -1).transpose(1, 0, 2)

    d = {n: a[n] for n in (
        "ab_w_in", "ab_gm_ln_g", "ab_gm_ln_b", "ab_mla_q_norm", "ab_mla_kv_norm", "ab_mla_w_uq",
        "ab_mla_w_uk", "ab_mla_w_uv", "ab_w_o", "moe_w_down", "ln1_g", "ln1_b", "ln2_g", "ln2_b")}
    d["x"], d["ctx_2"] = tiles(a["x"]), tiles(a["ctx_2"])
    d["positions"] = a["positions"].reshape(NT, P).T
    d["gm_ws_t"] = a["ab_gm_ws"][0].transpose(0, 2, 1)
    d["gm_bs_t"] = a["ab_gm_bs"][0].T
    d["router_w"] = np.concatenate([a["moe_w_rg"], a["moe_w_re"]], axis=-1)
    d["router_b"] = np.concatenate([a["moe_b_rg"], a["moe_b_re"]], axis=-1)
    for new, old in (("moe_gate", "moe_w_gate"), ("moe_up", "moe_w_up")):
        w = a[old].reshape(DEPTH, N_EXP, KD, P, MOE_HID // P, P)
        d[new] = w.transpose(0, 1, 4, 3, 2, 5).reshape(DEPTH, N_EXP, MOE_HID // P, P, KD * P)

    d["c_swap"] = np.roll(np.eye(P, dtype=np.float32), P // 2, 0)
    d["c_ident"] = np.eye(P, dtype=np.float32)
    d["c_iota"] = np.tile(np.arange(P, dtype=np.float32), (P, 1))
    d["c_upper"] = np.triu(np.ones((P, P), np.float32))
    q = np.arange(SEQ)
    d["c_causal"] = tiles(np.where(q[:, None] >= q[None, :], 0.0, NEG).astype(np.float32))
    half = ROPE // 2
    f = np.exp(np.float32(-math.log(10000.0)) * np.arange(half, dtype=np.float32) / np.float32(half))
    d["c_freq"] = np.tile(f.astype(np.float32), (P, 1))
    for n in ("c_w_in", "c_w_ck1", "c_w_ck2", "c_w_cv1", "c_w_cv2", "c_gate_b", "c_w_o", "w_mod_2", "w_in_2",
              "q_gain_2", "k_gain_2", "ln_g_2", "ln_b_2", "w_o_2", "peer_wq_2", "peer_v_2", "final_g_2"):
        d[n] = a[n]
    d["cmp_pos_t"] = a["c_cmp_pos"][0].reshape(2, CMP_LEN // 2, 2, DH).transpose(2, 3, 0, 1).reshape(P, 2, -1)
    end = np.arange(N_CMP) * CMP_STRIDE + CMP_LEN - 1
    ended = q[:, None] >= end[None, :]
    none = np.broadcast_to(~ended.any(1, keepdims=True), ended.shape)
    d["c_cmp_mask"] = np.stack([tiles(m.astype(np.float32)) for m in (np.where(ended, 0.0, NEG), ended, none)], 2)
    cond = np.stack([a["c_2"][0], a["c_ctx_2"]], -1)
    d["cond"] = cond.reshape(KD, P, 2).transpose(1, 0, 2)
    d["b_mod_t"] = a["b_mod_2"].reshape(DEPTH, 6 * KD, P).transpose(2, 0, 1)
    n4 = DH // 4
    inv = (np.float32(10000.0) ** (-np.arange(n4, dtype=np.float32) / np.float32(n4))).astype(np.float32)
    row, col = (np.repeat(np.arange(SEQ // 64), 64), np.tile(np.arange(64), SEQ // 64))
    ang = np.concatenate([row[:, None].astype(np.float32) * inv, col[:, None].astype(np.float32) * inv], -1)
    d["c_rope_cos"] = tiles(np.cos(ang).astype(np.float32))
    d["c_rope_sin"] = tiles(np.sin(ang).astype(np.float32))
    wb = np.concatenate([a["conv_w_2"], a["conv_b_2"][:, None, :]], 1)
    d["conv_wb_t"] = wb.reshape(DEPTH, CONV_K + 1, CONV_W // P, P).transpose(0, 3, 2, 1)
    beta = np.concatenate([a["beta_attn_2"], a["beta_conv_2"]], -1)
    d["beta_t"] = beta.reshape(DEPTH, KD, P).transpose(0, 2, 1)
    pk = a["peer_keys_2"]
    d["peer_keys_t"] = pk.transpose(0, 2, 4, 1, 3).reshape(DEPTH, P, PEER_H, PEER_K)
    u = a["peer_u_2"].reshape(DEPTH, PEER_K, P, KD, P)
    d["peer_u_t"] = u.transpose(0, 1, 4, 3, 2).reshape(DEPTH, PEER_K, P, D)
    return {n: np.ascontiguousarray(v) for n, v in d.items()}


def kernel(**inputs):
    import concourse.bacc as bacc
    from concourse.bass_utils import run_bass_kernel_spmd

    nc = bacc.Bacc("TRN2", target_bir_lowering=False, num_devices=1)
    arrays, aps = {}, {}
    for name, a in host_layout(inputs).items():
        arrays[f"in_{name}"] = a
        aps[name] = nc.dram_tensor(f"in_{name}", a.shape, mybir.dt.from_np(a.dtype), kind="ExternalInput").ap()
    out = nc.dram_tensor("out_0_dram", (1, SEQ, D), F32, kind="ExternalOutput").ap()
    build(nc, aps, out)
    r = run_bass_kernel_spmd(nc, [arrays], core_ids=[0])
    return r.results[0]["out_0_dram"]
```
